# Optimizing a Trainium2 kernel written in Bass

```python
import math
import jax, jax.numpy as jnp
from jax import lax
import numpy as np

D_MODEL = 1024
BATCH = 1
SEQ = 256
DEPTH = 2

MEM_LEN = 256
RMS_EPS = 1e-6
ROPE_THETA = 500000.0
ROPE_FRACTION = 4
Q_BLOCK = 128
MOBA_HEADS = 6
MOBA_DIM = 64
MOBA_BLOCK = 256
MOBA_TOPK = 3
MOBA_Q_BLOCK = 64
DIFF_HEADS = 4
DIFF_QK_DIM = 32
DIFF_V_DIM = 64
SB_HEADS = 6
SB_DIM = 64
XATTN_HEADS = 4
XATTN_DIM = 128

MOBA_W = MOBA_HEADS * MOBA_DIM
DIFF_QK_W = DIFF_HEADS * 2 * DIFF_QK_DIM
DIFF_W = DIFF_HEADS * DIFF_V_DIM
SB_W = SB_HEADS * SB_DIM
D_MIX = MOBA_W + DIFF_W + SB_W
IN_SPLIT_SIZES = (MOBA_W, MOBA_W, MOBA_W, MOBA_W,
                  DIFF_QK_W, DIFF_QK_W, DIFF_W, DIFF_W,
                  SB_W, SB_W, SB_W, SB_W)
D_IN = 4 * MOBA_W + 2 * DIFF_QK_W + 2 * DIFF_W + 4 * SB_W
XATTN_W = XATTN_HEADS * XATTN_DIM


def rms_norm(x, g):
    xf = x.astype(jnp.float32)
    y = xf * lax.rsqrt(jnp.mean(xf * xf, axis=-1, keepdims=True) + RMS_EPS)
    return (y * g.astype(jnp.float32)).astype(x.dtype)

def to_heads(t, n_heads, d):
    b, s, _ = t.shape
    return t.reshape(b, s, n_heads, d).transpose(0, 2, 1, 3)

def from_heads(t):
    b, h, s, d = t.shape
    return t.transpose(0, 2, 1, 3).reshape(b, s, h * d)

def rope_tables(positions, head_dim):
    rot = head_dim // ROPE_FRACTION
    inv = 1.0 / (ROPE_THETA ** (jnp.arange(0, rot, 2, dtype=jnp.float32) / rot))
    ang = positions.astype(jnp.float32)[..., None] * inv
    return jnp.cos(ang)[:, None], jnp.sin(ang)[:, None]

def apply_partial_rope(x, cos, sin):
    r2 = cos.shape[-1]
    c = cos.astype(x.dtype)
    s = sin.astype(x.dtype)
    x1 = x[..., :r2]
    x2 = x[..., r2:2 * r2]
    return jnp.concatenate([x1 * c - x2 * s, x2 * c + x1 * s, x[..., 2 * r2:]], axis=-1)

def sweep_blocks(fn, seq, qb):
    out = lax.map(fn, jnp.arange(seq // qb))
    n, b, h, _, d = out.shape
    return out.transpose(1, 2, 0, 3, 4).reshape(b, h, n * qb, d)

def moba_attention(q, k, v):
    b, h, s, d = q.shape
    nb = -(-s // MOBA_BLOCK)
    pad = nb * MOBA_BLOCK - s
    kp = jnp.pad(k, ((0, 0), (0, 0), (0, pad), (0, 0)))
    vp = jnp.pad(v, ((0, 0), (0, 0), (0, pad), (0, 0)))
    kb = kp.reshape(b, h, nb, MOBA_BLOCK, d)
    vb = vp.reshape(b, h, nb, MOBA_BLOCK, d)
    k_mean = jnp.mean(kb.astype(jnp.float32), axis=3)
    n_sel = min(MOBA_TOPK, nb)
    scale = d ** -0.5
    bi = jnp.arange(b)[:, None, None, None]
    hi = jnp.arange(h)[None, :, None, None]

    def block(i):
        q0 = i * MOBA_Q_BLOCK
        qi = lax.dynamic_slice_in_dim(q, q0, MOBA_Q_BLOCK, axis=2)
        own = q0 // MOBA_BLOCK
        tq = q0 + jnp.arange(MOBA_Q_BLOCK)
        gate = jnp.einsum('bhqd,bhnd->bhqn', qi.astype(jnp.float32), k_mean)
        gate = jnp.where(jnp.arange(nb) < own, gate, -jnp.inf)
        _, idx = lax.top_k(gate, n_sel)
        valid = idx < own
        ks = kb[bi, hi, idx]
        vs = vb[bi, hi, idx]
        s_sel = jnp.einsum('bhqd,bhqnld->bhqnl', qi, ks).astype(jnp.float32) * scale
        s_sel = jnp.where(valid[..., None], s_sel, -jnp.inf)
        s_sel = s_sel.reshape(b, h, MOBA_Q_BLOCK, n_sel * MOBA_BLOCK)
        ko = lax.dynamic_slice_in_dim(kp, own * MOBA_BLOCK, MOBA_BLOCK, axis=2)
        vo = lax.dynamic_slice_in_dim(vp, own * MOBA_BLOCK, MOBA_BLOCK, axis=2)
        s_own = jnp.einsum('bhqd,bhld->bhql', qi, ko).astype(jnp.float32) * scale
        to = own * MOBA_BLOCK + jnp.arange(MOBA_BLOCK)
        s_own = jnp.where(to[None, :] <= tq[:, None], s_own, -jnp.inf)
        p = jax.nn.softmax(jnp.concatenate([s_sel, s_own], axis=-1), axis=-1)
        p_sel = p[..., :n_sel * MOBA_BLOCK].reshape(b, h, MOBA_Q_BLOCK, n_sel, MOBA_BLOCK).astype(v.dtype)
        p_own = p[..., n_sel * MOBA_BLOCK:].astype(v.dtype)
        return (jnp.einsum('bhqnl,bhqnld->bhqd', p_sel, vs)
                + jnp.einsum('bhql,bhld->bhqd', p_own, vo))

    return sweep_blocks(block, s, MOBA_Q_BLOCK)

def diff_attention(q, k, v, lam, head_norm_g, lam_init):
    b, h2, s, dq = q.shape
    h = h2 // 2
    scale = dq ** -0.5
    kpos = jnp.arange(s)

    def block(i):
        q0 = i * Q_BLOCK
        qi = lax.dynamic_slice_in_dim(q, q0, Q_BLOCK, axis=2)
        sc = jnp.einsum('bhqd,bhkd->bhqk', qi, k).astype(jnp.float32) * scale
        mask = kpos[None, :] <= (q0 + jnp.arange(Q_BLOCK))[:, None]
        p = jax.nn.softmax(jnp.where(mask, sc, -jnp.inf), axis=-1).reshape(b, h, 2, Q_BLOCK, s)
        a = p[:, :, 0] - lam * p[:, :, 1]
        return jnp.einsum('bhqk,bhkd->bhqd', a.astype(v.dtype), v)

    o = sweep_blocks(block, s, Q_BLOCK)
    o = rms_norm(o, head_norm_g)
    return o * (1.0 - lam_init)

def stick_breaking_attention(q, k, v):
    b, h, s, d = q.shape
    scale = d ** -0.5
    kpos = jnp.arange(s)

    def block(i):
        q0 = i * Q_BLOCK
        qi = lax.dynamic_slice_in_dim(q, q0, Q_BLOCK, axis=2)
        z = jnp.einsum('bhqd,bhkd->bhqk', qi, k).astype(jnp.float32) * scale
        mask = kpos[None, :] < (q0 + jnp.arange(Q_BLOCK))[:, None]
        log_beta = jax.nn.log_sigmoid(z)
        log_1m_beta = jnp.where(mask, log_beta - z, 0.0)
        between = lax.cumsum(log_1m_beta, axis=3, reverse=True) - log_1m_beta
        w = jnp.where(mask, jnp.exp(log_beta + between), 0.0)
        return jnp.einsum('bhqk,bhkd->bhqd', w.astype(v.dtype), v)

    return sweep_blocks(block, s, Q_BLOCK)

def hybrid_mixer(hn, rope64, rope32, w_in, w_out, lq1, lk1, lq2, lk2, head_norm_g, lam_init):
    proj = hn @ w_in
    cuts = list(np.cumsum(IN_SPLIT_SIZES)[:-1])
    (mq, mk, mv, mg, dq_, dk_, dv_, dg, sq, sk, sv, sg) = jnp.split(proj, cuts, axis=-1)
    cos64, sin64 = rope64
    a_q = apply_partial_rope(to_heads(mq, MOBA_HEADS, MOBA_DIM), cos64, sin64)
    a_k = apply_partial_rope(to_heads(mk, MOBA_HEADS, MOBA_DIM), cos64, sin64)
    a_o = moba_attention(a_q, a_k, to_heads(mv, MOBA_HEADS, MOBA_DIM))
    cos32, sin32 = rope32
    b_q = apply_partial_rope(to_heads(dq_, 2 * DIFF_HEADS, DIFF_QK_DIM), cos32, sin32)
    b_k = apply_partial_rope(to_heads(dk_, 2 * DIFF_HEADS, DIFF_QK_DIM), cos32, sin32)
    f32 = jnp.float32
    lam = (jnp.exp(jnp.sum(lq1.astype(f32) * lk1.astype(f32)))
           - jnp.exp(jnp.sum(lq2.astype(f32) * lk2.astype(f32))) + lam_init)
    b_o = diff_attention(b_q, b_k, to_heads(dv_, DIFF_HEADS, DIFF_V_DIM), lam, head_norm_g, lam_init)
    c_o = stick_breaking_attention(to_heads(sq, SB_HEADS, SB_DIM), to_heads(sk, SB_HEADS, SB_DIM),
                                   to_heads(sv, SB_HEADS, SB_DIM))
    merged = jnp.concatenate([from_heads(a_o) * jax.nn.silu(mg),
                              from_heads(b_o).astype(hn.dtype) * jax.nn.silu(dg),
                              from_heads(c_o) * jax.nn.silu(sg)], axis=-1)
    return merged @ w_out

def memory_cross_attention(hn, mem_n, w_xq, w_xkv, w_xo):
    q = to_heads(hn @ w_xq, XATTN_HEADS, XATTN_DIM)
    k, v = jnp.split(mem_n @ w_xkv, 2, axis=-1)
    k = to_heads(k, XATTN_HEADS, XATTN_DIM)
    v = to_heads(v, XATTN_HEADS, XATTN_DIM)
    sc = jnp.einsum('bhsd,bhmd->bhsm', q, k).astype(jnp.float32) * (XATTN_DIM ** -0.5)
    p = jax.nn.softmax(sc, axis=-1).astype(v.dtype)
    o = jnp.einsum('bhsm,bhmd->bhsd', p, v)
    return from_heads(o) @ w_xo

def first_inputs(seed: int = 0) -> dict:
    key = jax.random.key(seed)
    ks = jax.random.split(key, 20)
    f32 = jnp.float32

    def w(k, shape, fan_in):
        return jax.random.normal(k, shape, f32) * (fan_in ** -0.5)

    def gain(k, shape):
        return 1.0 + 0.02 * jax.random.normal(k, shape, f32)

    offsets = jax.random.randint(ks[2], (BATCH, 1), 0, 4096, dtype=jnp.int32)
    positions = offsets + jnp.arange(SEQ, dtype=jnp.int32)[None, :]
    return {
        "x": jax.random.normal(ks[0], (BATCH, SEQ, D_MODEL), f32),
        "mem": jax.random.normal(ks[1], (BATCH, MEM_LEN, D_MODEL), f32),
        "positions": positions,
        "attn_norm_g": gain(ks[3], (DEPTH, D_MODEL)),
        "w_in": w(ks[4], (DEPTH, D_MODEL, D_IN), D_MODEL),
        "w_out": w(ks[5], (DEPTH, D_MIX, D_MODEL), D_MIX),
        "diff_lambda_q1": 0.1 * jax.random.normal(ks[6], (DEPTH, DIFF_QK_DIM), f32),
        "diff_lambda_k1": 0.1 * jax.random.normal(ks[7], (DEPTH, DIFF_QK_DIM), f32),
        "diff_lambda_q2": 0.1 * jax.random.normal(ks[8], (DEPTH, DIFF_QK_DIM), f32),
        "diff_lambda_k2": 0.1 * jax.random.normal(ks[9], (DEPTH, DIFF_QK_DIM), f32),
        "diff_head_norm_g": gain(ks[10], (DEPTH, DIFF_V_DIM)),
        "xattn_norm_g": gain(ks[11], (DEPTH, D_MODEL)),
        "mem_norm_g": gain(ks[12], (DEPTH, D_MODEL)),
        "w_xq": w(ks[13], (DEPTH, D_MODEL, XATTN_W), D_MODEL),
        "w_xkv": w(ks[14], (DEPTH, D_MODEL, 2 * XATTN_W), D_MODEL),
        "w_xo": w(ks[15], (DEPTH, XATTN_W, D_MODEL), XATTN_W),
        "final_norm_g": gain(ks[16], (D_MODEL,)),
    }

def first_block(x, mem, positions, attn_norm_g, w_in, w_out, diff_lambda_q1, diff_lambda_k1,
              diff_lambda_q2, diff_lambda_k2, diff_head_norm_g, xattn_norm_g, mem_norm_g,
              w_xq, w_xkv, w_xo, final_norm_g):
    rope64 = rope_tables(positions, MOBA_DIM)
    rope32 = rope_tables(positions, DIFF_QK_DIM)
    h = x
    for l in range(DEPTH):
        lam_init = 0.8 - 0.6 * math.exp(-0.3 * l)
        hn = rms_norm(h, attn_norm_g[l])
        h = h + hybrid_mixer(hn, rope64, rope32, w_in[l], w_out[l],
                             diff_lambda_q1[l], diff_lambda_k1[l], diff_lambda_q2[l], diff_lambda_k2[l],
                             diff_head_norm_g[l], lam_init)
        h = h + memory_cross_attention(rms_norm(h, xattn_norm_g[l]), rms_norm(mem, mem_norm_g[l]),
                                       w_xq[l], w_xkv[l], w_xo[l])
    return rms_norm(h, final_norm_g)


CONV_DIM = 512
CONV_WIDTH = 3
NSA_HEADS = 8
NSA_GROUPS = 2
HEADS_PER_GROUP = NSA_HEADS // NSA_GROUPS
HEAD_DIM = 64
ROT_DIM = HEAD_DIM // 4
CMP_BLOCK = 32
CMP_STRIDE = 16
CMP_HIDDEN = 256
SLC_BLOCK = 64
N_SELECT = 16
WINDOW = 512
MEM_HEADS = 4
MEM_HEAD_DIM = 128
D_FF = 2816
EPS = 1e-6
NEG = -1e30
BIG = 1e30
SPLIT_SIZES = (CONV_DIM, CONV_DIM, CONV_DIM, NSA_HEADS * HEAD_DIM, 6 * NSA_GROUPS * HEAD_DIM, 3 * NSA_HEADS, MEM_HEADS * MEM_HEAD_DIM, 3 * D_MODEL)
MIX_IN = 3 * CONV_DIM + NSA_HEADS * HEAD_DIM + 6 * NSA_GROUPS * HEAD_DIM + 3 * NSA_HEADS + MEM_HEADS * MEM_HEAD_DIM + 3 * D_MODEL


def rms_norm_2(x, g):
    xf = x.astype(jnp.float32)
    y = xf * lax.rsqrt(jnp.mean(xf * xf, axis=-1, keepdims=True) + EPS)
    return (y * g.astype(jnp.float32)).astype(x.dtype)

def swiglu(h, w_in, w_out):
    a, b = jnp.split(h @ w_in, 2, axis=-1)
    return (jax.nn.silu(a) * b) @ w_out

def rope_tables_2(positions):
    inv_freq = ROPE_THETA ** (-jnp.arange(0, ROT_DIM, 2, dtype=jnp.float32) / ROT_DIM)
    ang = positions.astype(jnp.float32)[..., None] * inv_freq
    return jnp.cos(ang)[:, :, None, :], jnp.sin(ang)[:, :, None, :]

def partial_rope(t, cos, sin):
    half = ROT_DIM // 2
    t1, t2, rest = t[..., :half], t[..., half:ROT_DIM], t[..., ROT_DIM:]
    return jnp.concatenate([t1 * cos - t2 * sin, t2 * cos + t1 * sin, rest], axis=-1)

def masked_softmax(s, mask):
    s = jnp.where(mask, s.astype(jnp.float32), NEG)
    m = jnp.max(s, axis=-1, keepdims=True)
    p = jnp.where(mask, jnp.exp(s - m), 0.0)
    return p / jnp.maximum(jnp.sum(p, axis=-1, keepdims=True), 1e-30)

def short_conv(v, w):
    return lax.conv_general_dilated(v, w[:, None, :].astype(v.dtype), window_strides=(1,),
                                    padding=[(CONV_WIDTH - 1, 0)],
                                    dimension_numbers=('NWC', 'WIO', 'NWC'),
                                    feature_group_count=v.shape[-1])

def compress(t, pos_emb, w1, b1, w2):
    b, s, g, d = t.shape
    chunks = t.reshape(b, s // CMP_STRIDE, CMP_STRIDE, g, d)
    blocks = jnp.concatenate([chunks[:, :-1], chunks[:, 1:]], axis=2)
    blocks = blocks + pos_emb[None, None, :, None, :]
    flat = jnp.moveaxis(blocks, 3, 2).reshape(b, -1, g, CMP_BLOCK * d)
    return jax.nn.gelu(flat @ w1 + b1) @ w2

def cmp_to_slc_matrix(n_cmp, n_slc):
    i = jnp.arange(n_cmp)[:, None] * CMP_STRIDE
    j = jnp.arange(n_slc)[None, :] * SLC_BLOCK
    ov = jnp.minimum(i + CMP_BLOCK, j + SLC_BLOCK) - jnp.maximum(i, j)
    return jnp.maximum(ov, 0).astype(jnp.float32) / CMP_BLOCK

def nsa_attention(q, q_rot, k_cmp, v_cmp, k_slc, v_slc, k_win, v_win, gates):
    b, s, h, d = q.shape
    n_cmp = k_cmp.shape[1]
    n_slc = s // SLC_BLOCK
    top = min(N_SELECT, n_slc)
    scale = HEAD_DIM ** -0.5
    q_plain_g = q.reshape(b, s, NSA_GROUPS, HEADS_PER_GROUP, d)
    q_rot_g = q_rot.reshape(b, s, NSA_GROUPS, HEADS_PER_GROUP, d)
    kc = jnp.transpose(k_cmp, (0, 2, 1, 3))
    vc = jnp.transpose(v_cmp, (0, 2, 1, 3))
    cmp_end = jnp.arange(n_cmp) * CMP_STRIDE + CMP_BLOCK - 1
    overlap = cmp_to_slc_matrix(n_cmp, n_slc)
    ks_blocks = k_slc.reshape(b, n_slc, SLC_BLOCK, NSA_GROUPS, d).transpose(0, 3, 1, 2, 4)
    vs_blocks = v_slc.reshape(b, n_slc, SLC_BLOCK, NSA_GROUPS, d).transpose(0, 3, 1, 2, 4)
    pad = ((0, 0), (WINDOW, 0), (0, 0), (0, 0))
    kw_pad = jnp.pad(k_win, pad)
    vw_pad = jnp.pad(v_win, pad)
    bi = jnp.arange(b)[:, None, None, None]
    gi = jnp.arange(NSA_GROUPS)[None, :, None, None]
    blk = jnp.arange(n_slc)

    def block(start):
        t = start + jnp.arange(Q_BLOCK)
        qp = lax.dynamic_slice_in_dim(q_plain_g, start, Q_BLOCK, axis=1)
        qr = lax.dynamic_slice_in_dim(q_rot_g, start, Q_BLOCK, axis=1)
        s_c = jnp.einsum('bqghd,bgnd->bghqn', qp, kc) * scale
        p_c = masked_softmax(s_c, cmp_end[None, :] <= t[:, None])
        o_c = jnp.einsum('bghqn,bgnd->bqghd', p_c.astype(vc.dtype), vc)
        imp = jnp.einsum('bghqn,nj->bgqj', p_c, overlap)
        cur = (t // SLC_BLOCK)[:, None]
        forced = (blk == 0) | (blk == cur) | (blk == cur - 1)
        imp = jnp.where(blk > cur, NEG, jnp.where(forced, BIG, imp))
        _, idx = lax.top_k(imp, top)
        ks = ks_blocks[bi, gi, idx].reshape(b, NSA_GROUPS, Q_BLOCK, top * SLC_BLOCK, d)
        vs = vs_blocks[bi, gi, idx].reshape(b, NSA_GROUPS, Q_BLOCK, top * SLC_BLOCK, d)
        kpos = (idx[..., None] * SLC_BLOCK + jnp.arange(SLC_BLOCK)).reshape(b, NSA_GROUPS, Q_BLOCK, top * SLC_BLOCK)
        m_s = kpos <= t[None, None, :, None]
        s_s = jnp.einsum('bqghd,bgqld->bghql', qr, ks) * scale
        p_s = masked_softmax(s_s, m_s[:, :, None])
        o_s = jnp.einsum('bghql,bgqld->bqghd', p_s.astype(vs.dtype), vs)
        kw = lax.dynamic_slice_in_dim(kw_pad, start, WINDOW + Q_BLOCK, axis=1)
        vw = lax.dynamic_slice_in_dim(vw_pad, start, WINDOW + Q_BLOCK, axis=1)
        wpos = start - WINDOW + jnp.arange(WINDOW + Q_BLOCK)
        m_w = (wpos[None, :] >= 0) & (wpos[None, :] <= t[:, None]) & (wpos[None, :] > t[:, None] - WINDOW)
        s_w = jnp.einsum('bqghd,bkgd->bghqk', qr, kw) * scale
        p_w = masked_softmax(s_w, m_w)
        o_w = jnp.einsum('bghqk,bkgd->bqghd', p_w.astype(vw.dtype), vw)
        g = lax.dynamic_slice_in_dim(gates, start, Q_BLOCK, axis=1)
        return g[..., 0:1] * o_c + g[..., 1:2] * o_s + g[..., 2:3] * o_w

    out = lax.map(block, jnp.arange(s // Q_BLOCK) * Q_BLOCK)
    return jnp.moveaxis(out, 0, 1).reshape(b, s, h * d)

def token_mixer(h, mem, cos, sin, mem_g, w_in, conv_w, cmp_pos_k, cmp_pos_v,
                ck_w1, ck_b1, ck_w2, cv_w1, cv_b1, cv_w2,
                w_mem_kv, w_br_conv, w_br_nsa, w_br_mem, w_out):
    b, s, _ = h.shape
    points, acc = [], 0
    for n in SPLIT_SIZES[:-1]:
        acc += n
        points.append(acc)
    u, bg, cg, q, kv, nsa_g, q_mem, merge_g = jnp.split(h @ w_in, points, axis=-1)
    cos = cos.astype(h.dtype)
    sin = sin.astype(h.dtype)
    y_conv = bg * short_conv(cg * u, conv_w)
    q = q.reshape(b, s, NSA_HEADS, HEAD_DIM)
    kv = kv.reshape(b, s, 6, NSA_GROUPS, HEAD_DIM)
    k_cmp = compress(kv[:, :, 0], cmp_pos_k, ck_w1, ck_b1, ck_w2)
    v_cmp = compress(kv[:, :, 1], cmp_pos_v, cv_w1, cv_b1, cv_w2)
    k_slc = partial_rope(kv[:, :, 2], cos, sin)
    k_win = partial_rope(kv[:, :, 4], cos, sin)
    q_rot = partial_rope(q, cos, sin)
    gates = jax.nn.sigmoid(nsa_g).reshape(b, s, NSA_GROUPS, HEADS_PER_GROUP, 3)
    y_nsa = nsa_attention(q, q_rot, k_cmp, v_cmp, k_slc, kv[:, :, 3], k_win, kv[:, :, 5], gates)
    m_len = mem.shape[1]
    mkv = (rms_norm_2(mem, mem_g) @ w_mem_kv).reshape(b, m_len, 2, MEM_HEADS, MEM_HEAD_DIM)
    q_m = q_mem.reshape(b, s, MEM_HEADS, MEM_HEAD_DIM)
    s_m = jnp.einsum('bshd,bmhd->bhsm', q_m, mkv[:, :, 0]).astype(jnp.float32) * (MEM_HEAD_DIM ** -0.5)
    p_m = jax.nn.softmax(s_m, axis=-1)
    y_mem = jnp.einsum('bhsm,bmhd->bshd', p_m.astype(mkv.dtype), mkv[:, :, 1]).reshape(b, s, MEM_HEADS * MEM_HEAD_DIM)
    g_conv, g_nsa, g_mem = jnp.split(jax.nn.sigmoid(merge_g), 3, axis=-1)
    merged = g_conv * (y_conv @ w_br_conv) + g_nsa * (y_nsa @ w_br_nsa) + g_mem * (y_mem @ w_br_mem)
    return merged @ w_out

def second_inputs(seed: int = 0) -> dict:
    key = jax.random.key(seed)
    keys = iter(jax.random.split(key, 40))
    L = DEPTH

    def dense(shape, fan_in):
        return jax.random.normal(next(keys), shape, jnp.float32) * fan_in ** -0.5

    def gain(shape):
        return 1.0 + 0.05 * jax.random.normal(next(keys), shape, jnp.float32)

    def small(shape, scale):
        return scale * jax.random.normal(next(keys), shape, jnp.float32)

    x = jax.random.normal(next(keys), (BATCH, SEQ, D_MODEL), jnp.float32)
    mem = jax.random.normal(next(keys), (BATCH, MEM_LEN, D_MODEL), jnp.float32)
    offset = jax.random.randint(next(keys), (BATCH, 1), 0, 4096, dtype=jnp.int32)
    positions = (jnp.arange(SEQ, dtype=jnp.int32)[None, :] + offset).astype(jnp.int32)
    return {
        'x': x,
        'mem': mem,
        'positions': positions,
        'ffn1_norm_pre': gain((L, D_MODEL)),
        'ffn1_norm_post': gain((L, D_MODEL)),
        'ffn1_w_in': dense((L, D_MODEL, 2 * D_FF), D_MODEL),
        'ffn1_w_out': dense((L, D_FF, D_MODEL), D_FF),
        'mix_norm_pre': gain((L, D_MODEL)),
        'mix_norm_post': gain((L, D_MODEL)),
        'mem_norm': gain((L, D_MODEL)),
        'w_mix_in': dense((L, D_MODEL, MIX_IN), D_MODEL),
        'conv_w': dense((L, CONV_WIDTH, CONV_DIM), CONV_WIDTH),
        'cmp_pos_k': small((L, CMP_BLOCK, HEAD_DIM), 0.1),
        'cmp_pos_v': small((L, CMP_BLOCK, HEAD_DIM), 0.1),
        'cmp_k_w1': dense((L, CMP_BLOCK * HEAD_DIM, CMP_HIDDEN), CMP_BLOCK * HEAD_DIM),
        'cmp_k_b1': small((L, CMP_HIDDEN), 0.01),
        'cmp_k_w2': dense((L, CMP_HIDDEN, HEAD_DIM), CMP_HIDDEN),
        'cmp_v_w1': dense((L, CMP_BLOCK * HEAD_DIM, CMP_HIDDEN), CMP_BLOCK * HEAD_DIM),
        'cmp_v_b1': small((L, CMP_HIDDEN), 0.01),
        'cmp_v_w2': dense((L, CMP_HIDDEN, HEAD_DIM), CMP_HIDDEN),
        'w_mem_kv': dense((L, D_MODEL, 2 * MEM_HEADS * MEM_HEAD_DIM), D_MODEL),
        'w_branch_conv': dense((L, CONV_DIM, D_MODEL), CONV_DIM),
        'w_branch_nsa': dense((L, NSA_HEADS * HEAD_DIM, D_MODEL), NSA_HEADS * HEAD_DIM),
        'w_branch_mem': dense((L, MEM_HEADS * MEM_HEAD_DIM, D_MODEL), MEM_HEADS * MEM_HEAD_DIM),
        'w_mix_out': dense((L, D_MODEL, D_MODEL), D_MODEL),
        'ffn2_norm_pre': gain((L, D_MODEL)),
        'ffn2_norm_post': gain((L, D_MODEL)),
        'ffn2_w_in': dense((L, D_MODEL, 2 * D_FF), D_MODEL),
        'ffn2_w_out': dense((L, D_FF, D_MODEL), D_FF),
    }

def second_block(x, mem, positions, ffn1_norm_pre, ffn1_norm_post, ffn1_w_in, ffn1_w_out,
              mix_norm_pre, mix_norm_post, mem_norm, w_mix_in, conv_w,
              cmp_pos_k, cmp_pos_v, cmp_k_w1, cmp_k_b1, cmp_k_w2, cmp_v_w1, cmp_v_b1, cmp_v_w2,
              w_mem_kv, w_branch_conv, w_branch_nsa, w_branch_mem, w_mix_out,
              ffn2_norm_pre, ffn2_norm_post, ffn2_w_in, ffn2_w_out):
    cos, sin = rope_tables_2(positions)
    for l in range(DEPTH):
        h = rms_norm_2(x, ffn1_norm_pre[l])
        x = x + 0.5 * rms_norm_2(swiglu(h, ffn1_w_in[l], ffn1_w_out[l]), ffn1_norm_post[l])
        h = rms_norm_2(x, mix_norm_pre[l])
        y = token_mixer(h, mem, cos, sin, mem_norm[l], w_mix_in[l], conv_w[l],
                        cmp_pos_k[l], cmp_pos_v[l], cmp_k_w1[l], cmp_k_b1[l], cmp_k_w2[l],
                        cmp_v_w1[l], cmp_v_b1[l], cmp_v_w2[l], w_mem_kv[l],
                        w_branch_conv[l], w_branch_nsa[l], w_branch_mem[l], w_mix_out[l])
        x = x + rms_norm_2(y, mix_norm_post[l])
        h = rms_norm_2(x, ffn2_norm_pre[l])
        x = x + 0.5 * rms_norm_2(swiglu(h, ffn2_w_in[l], ffn2_w_out[l]), ffn2_norm_post[l])
    return x


def setup_inputs(seed=0):
    out = dict(first_inputs(seed))
    for name, value in second_inputs(seed + 1).items():
        if name != "x":
            out[name + "_2"] = value
    return out


def reference(
    x, mem, positions, attn_norm_g, w_in, w_out, diff_lambda_q1, diff_lambda_k1, diff_lambda_q2,
    diff_lambda_k2, diff_head_norm_g, xattn_norm_g, mem_norm_g, w_xq, w_xkv, w_xo, final_norm_g,
    mem_2, positions_2, ffn1_norm_pre_2, ffn1_norm_post_2, ffn1_w_in_2, ffn1_w_out_2,
    mix_norm_pre_2, mix_norm_post_2, mem_norm_2, w_mix_in_2, conv_w_2, cmp_pos_k_2, cmp_pos_v_2,
    cmp_k_w1_2, cmp_k_b1_2, cmp_k_w2_2, cmp_v_w1_2, cmp_v_b1_2, cmp_v_w2_2, w_mem_kv_2,
    w_branch_conv_2, w_branch_nsa_2, w_branch_mem_2, w_mix_out_2, ffn2_norm_pre_2,
    ffn2_norm_post_2, ffn2_w_in_2, ffn2_w_out_2,
):
    x = first_block(
        x, mem, positions, attn_norm_g, w_in, w_out, diff_lambda_q1, diff_lambda_k1,
        diff_lambda_q2, diff_lambda_k2, diff_head_norm_g, xattn_norm_g, mem_norm_g, w_xq, w_xkv,
        w_xo, final_norm_g,
    )
    return second_block(
        x, mem_2, positions_2, ffn1_norm_pre_2, ffn1_norm_post_2, ffn1_w_in_2, ffn1_w_out_2,
        mix_norm_pre_2, mix_norm_post_2, mem_norm_2, w_mix_in_2, conv_w_2, cmp_pos_k_2,
        cmp_pos_v_2, cmp_k_w1_2, cmp_k_b1_2, cmp_k_w2_2, cmp_v_w1_2, cmp_v_b1_2, cmp_v_w2_2,
        w_mem_kv_2, w_branch_conv_2, w_branch_nsa_2, w_branch_mem_2, w_mix_out_2,
        ffn2_norm_pre_2, ffn2_norm_post_2, ffn2_w_in_2, ffn2_w_out_2,
    )


_drawn_inputs = setup_inputs


def setup_inputs(seed=0):
    import zlib

    import numpy as np

    out = dict(_drawn_inputs(seed))
    spreads = {}
    factors = {'diff_lambda_q1': 5.779,
     'diff_head_norm_g': 3.618,
     'xattn_norm_g': 8.0,
     'mem_norm_g': 6.189,
     'mem_norm_2': 7.115,
     'cmp_pos_k_2': 58.595,
     'cmp_k_b1_2': 64.0,
     'cmp_v_b1_2': 64.0,
     'cmp_pos_v_2': 8.0,
     'cmp_k_w1_2': 3.673,
     'cmp_k_w2_2': 3.346}
    for name, (base, spread) in spreads.items():
        noise = np.random.default_rng([zlib.crc32(name.encode()), seed]).standard_normal(out[name].shape)
        drawn = base * np.exp(spread * noise) if base else spread * noise
        out[name] = __import__('jax').numpy.asarray(drawn.astype(out[name].dtype))
    for name, factor in factors.items():
        out[name] = (out[name] * factor).astype(out[name].dtype)
    return out
```

```python
import math
from contextlib import ExitStack

import numpy as np

import concourse.bass as bass
from concourse import mybir

F32 = mybir.dt.float32
BF16 = mybir.dt.bfloat16
F32R = mybir.dt.float32r
I32 = mybir.dt.int32
ALU = mybir.AluOpType
ACT = mybir.ActivationFunctionType
AX = mybir.AxisListType

P = 128
SEQ = 256
T = SEQ // P
D = 1024
KC = D // P
DEPTH = 2
EPS = 1e-6
THETA = 500000.0
NEG = -1e30

MOBA_W, DIFF_W, SB_W = 384, 256, 384
MOBA_H, DIFF_H, SB_H = 6, 4, 6
HD = 64
DIFF_QK = 32
X_H, XD = 4, 128
XW = X_H * XD

D_FF = 2816
FC = D_FF // P
CONV = 512
NSA_H, NSA_G, HPG = 8, 2, 4
NSA_W = NSA_H * HD
CMP_L, CMP_STRIDE, CMP_HID = 32, 16, 256
NCMP = SEQ // CMP_STRIDE - 1
NPAD = NCMP + 1
KVW = 6 * NSA_G * HD + 3 * NSA_H
MIX = (CONV, CONV, CONV, NSA_W, 6 * NSA_G * HD, 3 * NSA_H, XW, 3 * D)

UNIT = 1024
RAW = 5
SPLIT = 3
NB = 512


def cols_units(name, chunks, first=0):
    return [(name, 0, KC, P * c, P) for c in range(first, first + chunks)]


def rows_units(name, c0, width=NB, nk=KC):
    per = UNIT // width if width != KVW - NB else 2
    return [(name, k, per, c0, width) for k in range(0, nk, per)]


def layer1_units():
    return (cols_units("w_xkv_k", 4) + cols_units("w_s", 6)
            + rows_units("w_qk", 0) + rows_units("w_qk", NB) + rows_units("w_qk", 2 * NB, 256)
            + rows_units("w_v", 0) + rows_units("w_v", NB)
            + rows_units("w_gate", 0) + rows_units("w_gate", NB)
            + rows_units("w_out", 0) + rows_units("w_out", NB)
            + rows_units("w_xkv_v", 0) + cols_units("w_xq", 4)
            + rows_units("w_xo", 0, nk=4) + rows_units("w_xo", NB, nk=4))


def ffn_units(name):
    units = []
    for pair in range(FC // 2 + 1):
        for j in (2 * pair, 2 * pair + 1):
            if pair < FC // 2:
                units += cols_units(name + "_in", 2, 2 * j)
        for j in (2 * pair - 2, 2 * pair - 1):
            if pair:
                units += [(name + "_out", j, 1, 0, D)]
    return units


def layer2_units():
    units = cols_units("w_mkv_k", 4) + ffn_units("ffn1") + rows_units("w_mkv_v", 0)
    units += rows_units("w_q", 0) + rows_units("w_kv", 0) + rows_units("w_kv", NB, KVW - NB)
    units += [(name, k, 4, 0, CMP_HID) for name in ("cmp_k_w1", "cmp_v_w1") for k in (0, 4, 8, 12)]
    units += cols_units("w_qmem", 4) + cols_units("w_conv", 12)
    for c in (0, NB):
        for b in range(3):
            units += rows_units("w_merge", b * D + c) + rows_units(f"w_br{b}", c, nk=4)
    units += rows_units("w_mix_out", 0) + rows_units("w_mix_out", NB)
    return units + ffn_units("ffn2")


def all_units():
    return ([(l, u) for l in range(DEPTH) for u in layer1_units()]
            + [(l, u) for l in range(DEPTH) for u in layer2_units()])


class Job:

    def __init__(self, bank, full, drained):
        self.bank = bank
        self.full = full
        self.drained = drained
        self.last = None
        self.hi = None


class Banks:

    def __init__(self, full, drained):
        self.full_sem, self.drained_sem = full, drained
        self.fulls, self.uses, self.at = [0] * 8, [0] * 8, 0

    def take(self, among=8, base=0, full=None):
        self.at += 1
        return self.take_bank(base + self.at % among, full)

    def take_bank(self, b, full=None):
        self.uses[b] += 1
        if full is None:
            self.fulls[b] += 1
            full = (self.full_sem[b], self.fulls[b])
        return Job(b, full, self.uses[b])


def build(nc, args):
    with ExitStack() as ctx:
        program(nc, ctx, args)


def program(nc, ctx, A):
    def sb(name, shape, dt=F32):
        return ctx.enter_context(nc.sbuf_tensor(name, shape, dt))

    def sem(name):
        return ctx.enter_context(nc.semaphore(name))

    bank = [ctx.enter_context(nc.psum_tensor(f"bank{i}", [P, NB], F32)) for i in range(8)]

    raw = sb("raw", [P, RAW, UNIT])
    w_hi = sb("w_hi", [P, SPLIT, UNIT], F32R)
    w_lo = sb("w_lo", [P, SPLIT, UNIT], F32R)
    x = sb("x", [P, T, D])
    rows = sb("rows", [P, T, D])
    attn = sb("attn", [P, T, D])
    h_hi, h_lo = sb("h_hi", [P, KC, SEQ], F32R), sb("h_lo", [P, KC, SEQ], F32R)
    m_hi, m_lo = sb("m_hi", [P, KC, SEQ], F32R), sb("m_lo", [P, KC, SEQ], F32R)
    f_hi, f_lo = sb("f_hi", [P, 4, SEQ], F32R), sb("f_lo", [P, 4, SEQ], F32R)
    hT, memS, fS = (h_hi, h_lo), (m_hi, m_lo), (f_hi, f_lo)
    memnT = sb("memnT", [P, KC, SEQ])
    qkT = sb("qkT", [P, 10, SEQ])
    xkT = sb("xkT", [P, X_H, SEQ])
    xv = sb("xv", [P, T, XW])
    probs = sb("probs", [P, 3, NB])
    probsT = sb("probsT", [P, 3, NB])
    negmax = sb("negmax", [P, 16, T])
    rowsum = sb("rowsum", [P, 16, T])
    rinv = sb("rinv", [P, 16, T])
    sumsq = sb("sumsq", [P, T])
    sumsq4 = sb("sumsq4", [P, T, T])
    ms = sb("ms", [P, T])
    rstd = sb("rstd", [P, T])
    half_pow = sb("half_pow", [P, 32])
    gain_cols = sb("gain_cols", [P, 7, DEPTH, KC])
    WORK = 11520
    work = sb("work", [P, WORK])

    at = [0]

    def part(n):
        at[0] += n
        return work[:, at[0] - n:at[0]]

    qk_rows = part(T * 1280).rearrange("p (t n) -> p t n", t=T)
    gates = work[:, 0:T * D].rearrange("p (t n) -> p t n", t=T)
    v_rows = part(T * D).rearrange("p (t n) -> p t n", t=T)
    xqT1 = work[:, at[0] - 4 * SEQ:at[0]].rearrange("p (c n) -> p c n", c=X_H)
    l1m = part(SB_H * 384).rearrange("p (h n) -> p h n", h=SB_H)
    sT = work[:, at[0] - SB_H * 384:at[0] - SB_H * 384 + 6 * SEQ].rearrange("p (c n) -> p c n", c=6)
    zall = part(SB_H * 384).rearrange("p (h n) -> p h n", h=SB_H)
    ln1p = part(SB_H * 384).rearrange("p (h n) -> p h n", h=SB_H)
    assert at[0] <= WORK, at
    at[0] = 0
    q_rows = part(T * NSA_W).rearrange("p (t n) -> p t n", t=T)
    qrot = part(T * NSA_W).rearrange("p (t n) -> p t n", t=T)
    merge = work[:, 0:2 * T * NB].rearrange("p (s t n) -> p s t n", s=2, t=T)
    kv = part(T * KVW).rearrange("p (t n) -> p t n", t=T)
    convT = part(4 * (SEQ + 2)).rearrange("p (c n) -> p c n", c=4)
    yconvT = part(4 * SEQ).rearrange("p (c n) -> p c n", c=4)
    cmp_raw = part(4 * P).rearrange("p (a n) -> p a n", a=4)
    cmp_x = part(2 * 16 * 2 * NCMP).rearrange("p (v m g i) -> p v m g i", v=2, m=16, g=2)
    utmp = part(2 * SEQ).rearrange("p (c n) -> p c n", c=2)
    cmp_rep = part(2 * P).rearrange("p (a n) -> p a n", a=2)
    vbd = part(NSA_H * HD).rearrange("p (h d) -> p h d", h=NSA_H)
    cs = part(T * NSA_H * NPAD).rearrange("p (h n) -> p h n", n=NPAD)
    cmp_pT = part(T * P).rearrange("p (t n) -> p t n", t=T)
    xqT2 = part(X_H * SEQ).rearrange("p (c n) -> p c n", c=X_H)
    gain_row = part(D)
    assert at[0] <= WORK, at
    ffn_th = probs
    hid = probsT
    cmp_h = sb("cmp_h", [P, 4, 30])
    cmp_t = sb("cmp_t", [P, 4, 30])
    cmp_g = sb("cmp_g", [P, 4, 32])
    kcT = sb("kcT", [P, NPAD])
    cstat = sb("cstat", [P, 3, 16])
    nsa_g = sb("nsa_g", [P, T, 3 * NSA_H])
    gsc = sb("gsc", [P, 16, T])

    dsq = probs[:, :, :].rearrange("p s n -> p (s n)")[:, 0:T * DIFF_H * HD].rearrange(
        "p (t h d) -> p t h d", t=T, h=DIFF_H)
    rt = [probsT[:, :, :].rearrange("p s n -> p (s n)")[:, 192 * i:192 * (i + 1)] for i in range(4)]

    ident = sb("ident", [P, P])
    ident_bf = sb("ident_bf", [P, P], BF16)
    causal_bf = sb("causal_bf", [P, T, SEQ], BF16)
    later = sb("later", [P, P])
    ones = sb("ones", [P, P])
    sb_keep = sb("sb_keep", [P, 384])
    sb_neg = sb("sb_neg", [P, 384])
    cmp_keep = sb("cmp_keep", [P, T * NSA_H, NPAD])
    cmp_neg = sb("cmp_neg", [P, T * NSA_H, NPAD])
    blockdiag = sb("blockdiag", [P, NSA_H])
    pos_i = sb("pos_i", [P, 2, T], I32)
    pos_f = sb("pos_f", [P, 2, T])
    inv_freq = sb("inv_freq", [P, 20])
    ang = sb("ang", [P, T, 20])
    turns = sb("turns", [P, T, 20])
    turns_i = sb("turns_i", [P, T, 20], I32)
    wrap = sb("wrap", [P, T, 20])
    ang2 = sb("ang2", [P, T, 20])
    sint = sb("sint", [P, T, 20])
    cost = sb("cost", [P, T, 20])
    lam_in = sb("lam_in", [P, DEPTH, 4, DIFF_QK])
    lam_prod = sb("lam_prod", [P, DEPTH, 2, DIFF_QK])
    lam_dot = sb("lam_dot", [P, DEPTH, 2])
    lam_exp = sb("lam_exp", [P, DEPTH, 2])
    neg_lam = sb("neg_lam", [P, DEPTH])
    head_g = sb("head_g", [P, DEPTH, HD])
    lam_const = sb("lam_const", [P, DEPTH, 2])
    conv_w = sb("conv_w", [P, DEPTH, 3, 4])
    cmp_b1 = sb("cmp_b1", [P, DEPTH, 2, 2])
    cmp_pos = sb("cmp_pos", [P, DEPTH, 2, 16])
    cmp_w2 = sb("cmp_w2", [P, DEPTH, 2, 2, HD])
    dstat = sb("dstat", [P, T, DIFF_H])
    dstat2 = sb("dstat2", [P, T, DIFF_H])

    full = [sem(f"bank{i}_full") for i in range(8)]
    drained = [sem(f"bank{i}_drained") for i in range(8)]
    loaded = [sem(f"unit_loaded{i}") for i in range(RAW)]
    weights_hi = sem("weights_hi_ready")
    weights_split = sem("weights_split")
    weights_used = sem("weights_used")
    turn_hi = sem("turned_hi_ready")
    mem_hi = sem("memory_hi_ready")
    x_loaded, mem_loaded, params_loaded, row_loaded, stored = map(
        sem, ("x_loaded", "mem_loaded", "params_loaded", "gain_row_loaded", "stored"))
    mem2_loaded = sem("mem2_loaded")
    consts_ready = sem("consts_ready")
    x_ready = sem("x_ready")
    sumsq_ready = sem("sumsq_ready")
    ms_ready = sem("ms_ready")
    rstd_ready = sem("rstd_ready")
    rows_ready = sem("rows_ready")
    memT_ready = sem("memT_ready")
    rope_ready = sem("rope_ready")
    tables_ready = sem("tables_ready")
    tables_in = sem("angles_ready")
    lam_ready = sem("lam_ready")
    max_ready = sem("max_ready")
    pv_done = sem("pv_done")
    ffn_th_ready = sem("ffn_th_ready")
    ffn_out_used = sem("ffn_out_used")
    z_ready, absz_ready, lnz_ready, l1m_ready, arg_ready, w_ready, lb_ready = map(sem, (
        "z_ready", "absz_ready", "lnz_ready", "l1m_ready", "arg_ready", "w_ready", "lb_ready"))
    th_ready = sem("gate_tanh_ready")
    vec_step, act_step, pool_step = sem("vector_step"), sem("scalar_step"), sem("pool_step")
    row_used = sem("gain_row_used")
    attn_free = sem("attn_free")
    cmpx_ready, cmph_ready, cmpg_ready, cexp_in, cexp_out, cmpp_ready = map(sem, (
        "cmp_x_ready", "cmp_hidden_ready", "cmp_gelu_ready", "cmp_shifted", "cmp_exp_done", "cmp_probs_ready"))
    cmpu_ready, cmpth_ready = sem("cmp_cubic_ready"), sem("cmp_tanh_ready")
    ysum_part, ysum_done = sem("nsa_part_ready"), sem("nsa_part_added")
    bsum_part, bsum_done = sem("branch_part_ready"), sem("branch_part_added")
    u_ready = sem("conv_u_ready")
    conv_split = sem("conv_branch_split")
    nsag_ready = sem("nsa_gate_tanh_ready")
    dsum_ready, dpow_ready = sem("diff_ms_ready"), sem("diff_rstd_ready")

    B = Banks(full, drained)
    plan_of = all_units()
    is_raw = [u[0].startswith("cmp_") for _, u in plan_of]
    width_of = [u[2] * u[4] for _, u in plan_of]
    nth_split = np.cumsum([0 if x else 1 for x in is_raw]).tolist()
    units = []
    pvs, outs, used, turns_hi = [0], [0], [0], [0]

    def take(n):
        return [B.take() for _ in range(n)]

    def release(n, event=None):
        for k in range(n):
            if event is not None and k == n - 1:
                units.append(event)
            else:
                used[0] += 1
                units.append((weights_used, used[0]))

    def plan_turn(n):
        jobs = take(n)
        for j in jobs:
            turns_hi[0] += 1
            j.hi = turns_hi[0]
        return jobs

    def plan_norm():
        return plan_turn(4)

    def plan_cols(n):
        jobs = take(n)
        for j in jobs:
            release(2, j.full)
            j.last = len(units) - 1
        return jobs

    def plan_block(n_units):
        jobs = take(T)
        release(n_units, jobs[-1].full)
        for j in jobs:
            j.last = len(units) - 1
        return jobs

    def plan_attention(groups):
        n = sum(groups)
        S, PT, O, first = [], [], [], {}
        starts = [sum(groups[:g]) for g in range(len(groups))]
        for i in range(n + 3):
            if i < n:
                S.append(B.take())
            if 2 <= i < n + 2:
                PT.append(B.take())
            if i >= 3 and i - 3 in starts:
                g = starts.index(i - 3)
                O.append(B.take(full=(pv_done, pvs[0] + starts[g] + groups[g])))
        base = pvs[0]
        pvs[0] += n
        return dict(n=n, groups=groups, starts=starts, S=S, PT=PT, O=O, pv=base)

    def plan_sb_out():
        jobs = dict(btw=[], O=[], pv=pvs[0])
        for h in range(SB_H):
            jobs["btw"].append(B.take())
        for g, n in ((0, 4), (1, 2)):
            jobs["O"].append(B.take(full=(pv_done, pvs[0] + 4 * g + n)))
        pvs[0] += SB_H
        return jobs

    def plan_ffn():
        last = (ffn_out_used, outs[0] + FC)
        acc = [B.take_bank(b, last if b == 3 else None) for b in range(4)]
        inner, out_unit = [], []
        base = outs[0]
        for pair in range(FC // 2 + 1):
            if pair < FC // 2:
                for j in (2 * pair, 2 * pair + 1):
                    inner.append(B.take_bank(4 + j % 4))
                    release(2, inner[-1].full)
                    inner[-1].last = len(units) - 1
            if pair:
                for j in (2 * pair - 2, 2 * pair - 1):
                    release(1, (ffn_out_used, base + j + 1))
                    out_unit.append(len(units) - 1)
        outs[0] += FC
        B.at = 7
        return dict(acc=acc, inner=inner, base=base, out_unit=out_unit)

    def plan_layer1():
        J = {}
        J["xk"] = plan_cols(2)
        J["hT"] = plan_norm()
        J["s"] = plan_cols(3)
        J["qk"] = plan_block(4) + plan_block(4) + plan_block(2)
        J["z"] = take(SB_H)
        J["v"] = plan_block(4) + plan_block(4)
        J["qkT"] = take(5)
        J["gate"] = plan_block(4) + plan_block(4)
        J["att"] = plan_attention([4, 2, 4, 4])
        J["sb"] = plan_sb_out()
        J["mT"] = plan_turn(4)
        J["out"] = plan_block(4) + plan_block(4)
        J["xv"] = plan_block(4)
        J["hT2"] = plan_norm()
        J["xq"] = plan_cols(2)
        J["xatt"] = plan_attention([2, 2])
        J["xoT"] = plan_turn(2)
        J["xo"] = plan_block(2) + plan_block(2)
        return J

    def plan_layer2():
        J = {}
        J["mk"] = plan_cols(2)
        J["hT1"] = plan_norm()
        J["ffn1"] = plan_ffn()
        J["mv"] = plan_block(4)
        J["hT"] = plan_norm()
        J["q"] = plan_block(4)
        J["kv"] = plan_block(4) + plan_block(4)
        J["crT"] = take(2)
        J["cmp"] = take(2)
        release(8, J["cmp"][1].full)
        J["qmem"] = plan_cols(2)
        J["conv"] = plan_cols(6)
        J["qkT"] = take(5)
        J["kvc"] = take(2)
        J["cs"] = take(NSA_G)
        J["cpT"] = take(1)
        J["co"] = take(2)
        J["att"] = plan_attention([4, 4, 4, 4])
        J["matt"] = plan_attention([2, 2])
        J["yT"] = plan_turn(4)
        J["merge"], J["br"] = [], []
        for _ in range(6):
            J["merge"] += plan_block(4)
            J["br"] += plan_block(2)
        J["mT"] = plan_turn(4)
        J["out"] = plan_block(4) + plan_block(4)
        J["hT2"] = plan_norm()
        J["ffn2"] = plan_ffn()
        return J

    mem1 = take(4)
    L1 = [plan_layer1() for _ in range(DEPTH)]
    mem2 = take(4)
    L2 = [plan_layer2() for _ in range(DEPTH)]
    n_units = len(units)
    assert n_units == len(plan_of) == A["stream"].shape[0], (n_units, len(plan_of))

    def wait_empty(pe, job):
        if job.drained > 1:
            pe.wait_ge(drained[job.bank], job.drained - 1)

    def wait_full(eng, job):
        eng.wait_ge(*job.full)

    def wait_drained(eng, *jobs):
        for job in jobs:
            eng.wait_ge(drained[job.bank], job.drained)

    def norm1(l, i):
        return 1 + 2 * l + i

    final = 1 + 2 * DEPTH
    mem2_norm = final + 1

    def norm2(l, i):
        return mem2_norm + 1 + 6 * l + i

    sq = []
    for n in range(norm2(DEPTH, 0)):
        post = n > mem2_norm and (n - mem2_norm - 1) % 2 == 1
        sq.append((sq[-1] if sq else 0) + (2 * T if post else T))

    order = ["mem1"]
    for l in range(DEPTH):
        order += [("n", l, 0), ("merged", l), ("n", l, 1)]
    order += ["mem2"]
    for l in range(DEPTH):
        order += [("m", l, 0), ("m", l, 2), ("mixed", l), ("m", l, 4)]
    rows_at = {key: T * (i + 1) for i, key in enumerate(order)}

    def x_at(l, i):
        return T * (1 + 3 * l + i)

    def wait_x1(eng, l, i):
        if i == 1:
            wait_drained(eng, *L1[l]["out"])
        elif l == 0:
            eng.wait_ge(x_loaded, 16)
        else:
            wait_drained(eng, *L1[l - 1]["xo"])

    small = [
        (gain_cols[:, :, :, :], A["gain_cols"]), (head_g[:, :, :], A["head_g"]),
        (lam_in[:, :, :, :], A["lam"]), (lam_const[:, :, :], A["lam_const"]),
        (conv_w[:, :, :, :], A["conv_w"]), (cmp_b1[:, :, :, :], A["cmp_b1"]),
        (cmp_pos[:, :, :, :], A["cmp_pos"]), (cmp_w2[:, :, :, :, :], A["cmp_w2"]),
        (inv_freq[:, :], A["inv_freq"]), (pos_i[:, :, :], A["positions"]),
    ]
    N_SMALL = 16 * len(small)
    SCALE = HD ** -0.5
    qk_scale = [SCALE] * 3 + [1.0] * 3 + [DIFF_QK ** -0.5] * 2 + [1.0] * 2
    qk2_scale = [SCALE] * 8 + [1.0] * 2

    def raw_free(u):
        return units[u] if is_raw[u] else (weights_split, nth_split[u])

    def split_free(u):
        n = nth_split[u] - SPLIT
        return units[nth_split.index(n)] if n > 0 else None

    def moba_heads():
        return [dict(q=qkT[64 * (h % 2):64 * (h % 2) + 64, h // 2, :],
                     k=qkT[64 * (h % 2):64 * (h % 2) + 64, 3 + h // 2, :],
                     v=v_rows[:, :, HD * h:HD * h + HD]) for h in range(MOBA_H)]

    def diff_heads():
        out = []
        for s in range(2 * DIFF_H):
            b, c = 32 * (s % 4), s // 4
            v0 = MOBA_W + HD * (s // 2)
            out.append(dict(q=qkT[b:b + 32, 6 + c, :], k=qkT[b:b + 32, 8 + c, :], v=v_rows[:, :, v0:v0 + HD]))
        return out

    def nsa_heads():
        out = []
        for chunk, slot in ((8, 3), (9, 5)):
            for h in range(NSA_H):
                g, j = h // HPG, h % HPG
                v0 = (2 * slot + g) * HD
                out.append(dict(q=qkT[64 * g:64 * g + 64, 4 + j, :], k=qkT[64 * g:64 * g + 64, chunk, :],
                                v=kv[:, :, v0:v0 + HD]))
        return out

    def memory_heads(xqT):
        return [dict(q=xqT[:, h, :], k=xkT[:, h, :], v=xv[:, :, XD * h:XD * h + XD]) for h in range(X_H)]

    CONSTS = 21
    TWO_PI = (6.28125, float(np.float32(2 * math.pi - 6.28125)),
              2 * math.pi - 6.28125 - float(np.float32(2 * math.pi - 6.28125)))
    PI_F = float(np.nextafter(np.float32(math.pi), np.float32(0)))

    def raw_drain(eng, job, v):
        wait_full(eng, job)
        tokens = bank[job.bank][0:HD, :].rearrange("p (g n two) -> p g n two", g=NSA_G, two=2)
        for odd in range(2):
            dst = cmp_raw[HD * odd:HD * odd + HD, 2 * v:2 * v + 2, :]
            if v == 0:
                ins = eng.activation(dst, tokens[:, :, :, odd], ACT.Copy)
            else:
                ins = eng.tensor_copy(dst, tokens[:, :, :, odd])
        ins.then_inc(drained[job.bank], 1)

    block = ctx.enter_context(nc.Block())


    @block.sync
    def _(sp):
        sp.dma_start(attn[:, :, :], A["mem"].rearrange("(t p) n -> p t n", p=P)).then_inc(mem_loaded, 16)
        sp.dma_start(x[:, :, :], A["x"].rearrange("(t p) n -> p t n", p=P)).then_inc(x_loaded, 16)
        for dst, src in small:
            sp.dma_start(dst, src).then_inc(params_loaded, 16)
        for u in range(n_units):
            if u >= RAW:
                sp.wait_ge(*raw_free(u - RAW))
            sp.dma_start(raw[:, u % RAW, :], A["stream"][u]).then_inc(loaded[u % RAW], 16)
        for t in range(T):
            sp.wait_ge(x_ready, x_at(DEPTH - 1, 2) + t + 1)
            sp.dma_start(A["out"][t * P:(t + 1) * P, :], x[:, t, :]).then_inc(stored, 16)
        sp.wait_ge(stored, 16 * T)

    @block.tensor
    def _(pe):
        unit = [0]

        def next_unit():
            u = unit[0]
            unit[0] += 1
            if is_raw[u]:
                pe.wait_ge(loaded[u % RAW], 16 * (u // RAW + 1))
                return u, raw[:, u % RAW, :]
            pe.wait_ge(weights_split, nth_split[u])
            slot = (nth_split[u] - 1) % SPLIT
            return u, (w_hi[:, slot, :], w_lo[:, slot, :])

        def mark(mm, u):
            if units[u][0] is weights_used:
                mm.then_inc(weights_used, 1)

        def product(out, stat, mov, first, last):
            pe.matmul(out, stat[0], mov[0], start=first, stop=False)
            pe.matmul(out, stat[0], mov[1], start=False, stop=False)
            return pe.matmul(out, stat[1], mov[0], start=False, stop=last)

        def project_cols(jobs, src):
            for job in jobs:
                for c in range(2):
                    u, w = next_unit()
                    if c == 0:
                        wait_empty(pe, job)
                    for k in range(KC):
                        mm = product(bank[job.bank][:, c * SEQ:(c + 1) * SEQ],
                                     [part[:, k * P:(k + 1) * P] for part in w],
                                     [part[:, k, :] for part in src], k == 0, k == KC - 1)
                    mark(mm, u)
                mm.then_inc(job.full[0], 1)

        def project_rows(jobs, src, nk, per_unit, width):
            for step in range(nk // per_unit):
                u, w = next_unit()
                for t, job in enumerate(jobs):
                    if step == 0:
                        wait_empty(pe, job)
                    for kk in range(per_unit):
                        k = step * per_unit + kk
                        mm = product(bank[job.bank][:, 0:width], [part[:, k, t * P:(t + 1) * P] for part in src],
                                     [part[:, kk * width:(kk + 1) * width] for part in w], k == 0, k == nk - 1)
                    if k == nk - 1:
                        mm.then_inc(job.full[0], 1)
                mark(mm, u)

        def turn(jobs, src):
            for i, job in enumerate(jobs):
                wait_empty(pe, job)
                for c in range(2):
                    for t in range(T):
                        mm = pe.transpose(bank[job.bank][:, c * SEQ + t * P:c * SEQ + (t + 1) * P],
                                          src(2 * i + c, t), ident[:, :])
                mm.then_inc(job.full[0], 1)

        def turn_rows(jobs, key, src=rows):
            pe.wait_ge(rows_ready, rows_at[key])
            turn(jobs, lambda c, t: src[:, t, c * P:(c + 1) * P])

        def weighted_sum(out, pT, v, first, causal_heads):
            dv = v.shape[2]
            mm = pe.matmul(out[:, 0:dv], pT[:, 0:P], v[:, 0, :], start=first,
                           stop=causal_heads, skip_group_check=True)
            if not causal_heads:
                mm = pe.matmul(out[:, 0:dv], pT[:, SEQ:SEQ + P], v[:, 1, :], start=False, stop=True,
                               skip_group_check=True)
            pe.matmul(out[:, dv:2 * dv], pT[:, P:SEQ], v[:, 0, :], start=False, stop=False,
                      skip_group_check=True)
            late = pT[:, SEQ:SEQ + P] if causal_heads else pT[:, SEQ + P:2 * SEQ]
            return pe.matmul(out[:, dv:2 * dv], late, v[:, 1, :], start=False, stop=True,
                             skip_group_check=True)

        def attention(J, heads, causal_heads):
            n = J["n"]
            for i in range(n + 3):
                if i < n:
                    h, job = heads[i], J["S"][i]
                    out = bank[job.bank]
                    wait_empty(pe, job)
                    if causal_heads:
                        pe.matmul(out[:, :], ident_bf[:, :], causal_bf[:, :, :].rearrange("p t n -> p (t n)"),
                                  start=True, stop=False, skip_group_check=True)
                        pe.matmul(out[:, 0:P], h["q"][:, 0:P], h["k"][:, 0:P], start=False, stop=True,
                                  skip_group_check=True)
                        mm = pe.matmul(out[:, SEQ:2 * SEQ], h["q"][:, P:SEQ], h["k"], start=False,
                                       stop=True, skip_group_check=True)
                    else:
                        for t in range(T):
                            mm = pe.matmul(out[:, t * SEQ:(t + 1) * SEQ], h["q"][:, t * P:(t + 1) * P],
                                           h["k"], start=True, stop=True)
                    mm.then_inc(job.full[0], 1)
                if 2 <= i < n + 2:
                    i2 = i - 2
                    job, p = J["PT"][i2], probs[:, i2 % 3, :]
                    wait_drained(pe, J["S"][i2])
                    wait_empty(pe, job)
                    out = bank[job.bank]
                    pe.transpose(out[:, 0:P], p[:, 0:P], ident[:, :])
                    pe.transpose(out[:, P:SEQ], p[:, SEQ:SEQ + P], ident[:, :])
                    if causal_heads:
                        mm = pe.transpose(out[:, SEQ:SEQ + P], p[:, SEQ + P:2 * SEQ], ident[:, :])
                    else:
                        pe.transpose(out[:, SEQ:SEQ + P], p[:, P:SEQ], ident[:, :])
                        mm = pe.transpose(out[:, SEQ + P:2 * SEQ], p[:, SEQ + P:2 * SEQ], ident[:, :])
                    mm.then_inc(job.full[0], 1)
                if i >= 3:
                    i3 = i - 3
                    g = max(k for k, s in enumerate(J["starts"]) if s <= i3)
                    first = i3 == J["starts"][g]
                    job, v = J["O"][g], heads[i3]["v"]
                    wait_drained(pe, J["PT"][i3])
                    if first:
                        wait_empty(pe, job)
                    c0 = (i3 - J["starts"][g]) * 2 * v.shape[2]
                    weighted_sum(bank[job.bank][:, c0:c0 + 2 * v.shape[2]], probsT[:, i3 % 3, :], v,
                                 first, causal_heads).then_inc(pv_done, 1)

        def swiglu(J):
            for pair in range(FC // 2 + 1):
                if pair < FC // 2:
                    project_cols(J["inner"][2 * pair:2 * pair + 2], hT)
                if not pair:
                    continue
                for j in (2 * pair - 2, 2 * pair - 1):
                    u, w = next_unit()
                    wait_drained(pe, J["inner"][j])
                    for c in range(2):
                        for t in range(T):
                            job = J["acc"][2 * c + t]
                            if j == 0:
                                wait_empty(pe, job)
                            mm = product(bank[job.bank][:, :], [part[:, j % 4, t * P:(t + 1) * P] for part in fS],
                                         [part[:, c * NB:(c + 1) * NB] for part in w], j == 0, j == FC - 1)
                            if j == FC - 1 and (c, t) != (1, 1):
                                mm.then_inc(job.full[0], 1)
                    mm.then_inc(ffn_out_used, 1)

        def layer1(l):
            J = L1[l]
            pe.wait_ge(memT_ready, l + 1)
            project_cols(J["xk"], memS)
            turn_rows(J["hT"], ("n", l, 0))
            wait_drained(pe, *J["hT"])
            project_cols(J["s"], hT)
            project_rows(J["qk"][0:2], hT, KC, 2, NB)
            project_rows(J["qk"][2:4], hT, KC, 2, NB)
            project_rows(J["qk"][4:6], hT, KC, 4, 256)
            wait_drained(pe, *J["s"])
            for h in range(SB_H):
                job, b, c = J["z"][h], 64 * (h % 2), h // 2
                q, k = sT[b:b + 64, c, :], sT[b:b + 64, 3 + c, :]
                wait_empty(pe, job)
                pe.matmul(bank[job.bank][:, 0:SEQ], k[:, 0:P], q, start=True, stop=True)
                pe.matmul(bank[job.bank][:, SEQ:384], k[:, P:SEQ], q[:, P:SEQ], start=True,
                          stop=True).then_inc(job.full[0], 1)
            project_rows(J["v"][0:2], hT, KC, 2, NB)
            project_rows(J["v"][2:4], hT, KC, 2, NB)
            pe.wait_ge(rope_ready, T * l + 1)
            turn(J["qkT"], lambda c, t: qk_rows[:, t, c * P:(c + 1) * P])
            project_rows(J["gate"][0:2], hT, KC, 2, NB)
            project_rows(J["gate"][2:4], hT, KC, 2, NB)
            wait_drained(pe, *J["qkT"])
            wait_drained(pe, *J["v"])
            attention(J["att"], moba_heads() + diff_heads(), True)
            pe.wait_ge(l1m_ready, l + 1)
            for h in range(SB_H):
                job = J["sb"]["btw"][h]
                out = bank[job.bank]
                wait_empty(pe, job)
                pe.matmul(out[:, 0:SEQ], later[:, :], l1m[:, h, 0:SEQ], start=True, stop=False,
                          skip_group_check=True)
                pe.matmul(out[:, P:SEQ], ones[:, :], l1m[:, h, SEQ:384], start=False, stop=True,
                          skip_group_check=True)
                pe.matmul(out[:, SEQ:384], later[:, :], l1m[:, h, SEQ:384], start=False, stop=True,
                          skip_group_check=True).then_inc(job.full[0], 1)
            for h in range(SB_H):
                job = J["sb"]["O"][h // 4]
                if h % 4 == 0:
                    wait_empty(pe, job)
                pe.wait_ge(w_ready, SB_H * l + h + 1)
                v0 = MOBA_W + DIFF_W + HD * h
                c0 = (h % 4) * 2 * HD
                weighted_sum(bank[job.bank][:, c0:c0 + 2 * HD], zall[:, h, :], v_rows[:, :, v0:v0 + HD],
                             h % 4 == 0, True).then_inc(pv_done, 1)
            turn_rows(J["mT"], ("merged", l))
            wait_drained(pe, *J["mT"])
            project_rows(J["out"][0:2], hT, KC, 2, NB)
            project_rows(J["out"][2:4], hT, KC, 2, NB)
            project_rows(J["xv"], memS, KC, 2, NB)
            turn_rows(J["hT2"], ("n", l, 1))
            wait_drained(pe, *J["hT2"])
            project_cols(J["xq"], hT)
            wait_drained(pe, *J["xk"])
            wait_drained(pe, *J["xv"])
            wait_drained(pe, *J["xq"])
            attention(J["xatt"], memory_heads(xqT1), False)
            wait_drained(pe, *J["xatt"]["O"])
            turn(J["xoT"], lambda c, t: attn[:, t, c * P:(c + 1) * P])
            wait_drained(pe, *J["xoT"])
            project_rows(J["xo"][0:2], hT, 4, 2, NB)
            project_rows(J["xo"][2:4], hT, 4, 2, NB)

        def layer2(l):
            J = L2[l]
            pe.wait_ge(memT_ready, DEPTH + l + 1)
            project_cols(J["mk"], memS)
            turn_rows(J["hT1"], ("m", l, 0))
            wait_drained(pe, *J["hT1"])
            swiglu(J["ffn1"])
            project_rows(J["mv"], memS, KC, 2, NB)
            turn_rows(J["hT"], ("m", l, 2))
            wait_drained(pe, *J["hT"])
            project_rows(J["q"], hT, KC, 2, NB)
            project_rows(J["kv"][0:2], hT, KC, 2, NB)
            project_rows(J["kv"][2:4], hT, KC, 2, KVW - NB)
            wait_drained(pe, *J["kv"])
            for v, job in enumerate(J["crT"]):
                wait_empty(pe, job)
                for g in range(NSA_G):
                    for t in range(T):
                        mm = pe.transpose(bank[job.bank][0:HD, g * SEQ + t * P:g * SEQ + (t + 1) * P],
                                          kv[:, t, v * P + g * HD:v * P + (g + 1) * HD], ident[:, :])
                mm.then_inc(job.full[0], 1)
            wait_empty(pe, J["cmp"][0])
            wait_empty(pe, J["cmp"][1])
            pe.wait_ge(cmpx_ready, l + 1)
            for v in range(2):
                for step in range(4):
                    u, w = next_unit()
                    for half, job in enumerate(J["cmp"]):
                        for mm_ in range(4):
                            m = 4 * step + mm_
                            mm = pe.matmul(bank[job.bank][:, 30 * v:30 * v + 30],
                                           w[:, mm_ * CMP_HID + half * P:mm_ * CMP_HID + (half + 1) * P],
                                           cmp_x[:, v, m, :, :].rearrange("p g i -> p (g i)"),
                                           start=(m == 0), stop=(m == 15))
                        if v == 1 and m == 15:
                            mm.then_inc(job.full[0], 1)
                    mark(mm, u)
            project_cols(J["qmem"], hT)
            project_cols(J["conv"], hT)
            pe.wait_ge(rope_ready, T * DEPTH + l + 1)
            def qk_chunk(c, t):
                if c < 8:
                    return (q_rows if c < 4 else qrot)[:, t, (c % 4) * P:(c % 4 + 1) * P]
                slot = 2 if c == 8 else 4
                return kv[:, t, slot * P:(slot + 1) * P]
            turn(J["qkT"], qk_chunk)
            pe.wait_ge(cmpg_ready, l + 1)
            wait_empty(pe, J["kvc"][0])
            for half in range(2):
                mm = pe.matmul(bank[J["kvc"][0].bank][0:HD, 0:32], cmp_w2[:, l, 0, half, :],
                               cmp_g[:, half, :], start=(half == 0), stop=(half == 1))
            mm.then_inc(J["kvc"][0].full[0], 1)
            wait_empty(pe, J["kvc"][1])
            for half in range(2):
                mm = pe.matmul(bank[J["kvc"][1].bank][:, 0:HD], cmp_rep[:, half, :],
                               cmp_w2[:, l, 1, half, :], start=(half == 0), stop=(half == 1))
            mm.then_inc(J["kvc"][1].full[0], 1)
            wait_drained(pe, *J["kvc"])
            wait_drained(pe, *J["qkT"])
            for g, job in enumerate(J["cs"]):
                wait_empty(pe, job)
                for t in range(T):
                    for j in range(HPG):
                        c0 = (t * HPG + j) * NPAD
                        mm = pe.matmul(bank[job.bank][:, c0:c0 + NPAD],
                                       qkT[64 * g:64 * g + 64, j, t * P:(t + 1) * P],
                                       kcT[64 * g:64 * g + 64, :], start=True, stop=True)
                mm.then_inc(job.full[0], 1)
            pe.wait_ge(cmpp_ready, l + 1)
            job = J["cpT"][0]
            wait_empty(pe, job)
            for t in range(T):
                mm = pe.transpose(bank[job.bank][:, t * P:(t + 1) * P],
                                  cs[:, t * NSA_H:(t + 1) * NSA_H, :].rearrange("p h n -> p (h n)"), ident[:, :])
            mm.then_inc(job.full[0], 1)
            wait_drained(pe, job)
            for t, job in enumerate(J["co"]):
                wait_empty(pe, job)
                pe.matmul(bank[job.bank][:, :], cmp_pT[:, t, :], vbd[:, :, :].rearrange("p h d -> p (h d)"),
                          start=True, stop=True).then_inc(job.full[0], 1)
            attention(J["att"], nsa_heads(), True)
            wait_drained(pe, *J["mk"])
            wait_drained(pe, *J["mv"])
            wait_drained(pe, *J["qmem"])
            attention(J["matt"], memory_heads(xqT2), False)
            pe.wait_ge(ysum_done, 4 * (l + 1))
            wait_drained(pe, *J["matt"]["O"])
            turn(J["yT"], lambda c, t: attn[:, t, c * P:(c + 1) * P])
            wait_drained(pe, *J["yT"])
            wait_drained(pe, *J["conv"])
            pe.wait_ge(conv_split, l + 1)
            for c in range(2):
                for b in range(3):
                    n = 2 * (3 * c + b)
                    project_rows(J["merge"][n:n + 2], hT, KC, 2, NB)
                    src = fS if b == 0 else [part[:, 4 * b - 4:4 * b, :] for part in memS]
                    project_rows(J["br"][n:n + 2], src, 4, 2, NB)
            turn_rows(J["mT"], ("mixed", l))
            wait_drained(pe, *J["mT"])
            project_rows(J["out"][0:2], hT, KC, 2, NB)
            project_rows(J["out"][2:4], hT, KC, 2, NB)
            turn_rows(J["hT2"], ("m", l, 4))
            wait_drained(pe, *J["hT2"])
            swiglu(J["ffn2"])

        pe.wait_ge(consts_ready, CONSTS)
        turn_rows(mem1, "mem1")
        for l in range(DEPTH):
            layer1(l)
        turn_rows(mem2, "mem2")
        for l in range(DEPTH):
            layer2(l)
        assert unit[0] == n_units

    @block.gpsimd
    def _(pool):
        n_const = [0]

        def const(ins):
            n_const[0] += 1
            ins.then_inc(consts_ready, 1)
            pool.wait_ge(consts_ready, n_const[0])

        def select(t, pattern, base, mult, fill, op=ALU.is_ge):
            const(pool.affine_select(out=t, in_=t, pattern=pattern, compare_op=op, fill=fill, base=base,
                                     channel_multiplier=mult))

        const(pool.memset(half_pow[:, :], -0.5))
        const(pool.memset(ident[:, :], 0.0))
        select(ident[:, :], [[-1, P]], 0, 1, 1.0, ALU.not_equal)
        const(pool.tensor_copy(ident_bf[:, :], ident[:, :]))
        const(pool.memset(causal_bf[:, :, :], 0.0))
        select(causal_bf[:, :, :], [[P, T], [-1, SEQ]], 0, 1, NEG)
        const(pool.memset(ones[:, :], 1.0))
        const(pool.memset(later[:, :], 1.0))
        select(later[:, :], [[-1, P]], -1, 1, 0.0)
        const(pool.memset(sb_keep[:, :], 1.0))
        select(sb_keep[:, 0:SEQ], [[1, SEQ]], -1, -1, 0.0)
        select(sb_keep[:, SEQ:384], [[1, P]], -1, -1, 0.0)
        const(pool.memset(sb_neg[:, :], 0.0))
        select(sb_neg[:, 0:SEQ], [[1, SEQ]], -1, -1, NEG)
        select(sb_neg[:, SEQ:384], [[1, P]], -1, -1, NEG)
        ends = [[P, T], [0, NSA_H], [-CMP_STRIDE, NPAD]]
        const(pool.memset(cmp_keep[:, :, :], 1.0))
        select(cmp_keep[:, :, :], ends, 1 - CMP_L, 1, 0.0)
        const(pool.tensor_scalar(cmp_neg[:, :, :], cmp_keep[:, :, :], -1.0, -NEG, ALU.add, ALU.mult))
        const(pool.memset(blockdiag[:, :], 0.5))
        select(blockdiag[:, :], [[-NPAD, NSA_H]], 0, 1, 0.0)
        select(blockdiag[:, :], [[NPAD, NSA_H]], NPAD - 1, -1, 0.0)
        assert n_const[0] == CONSTS, n_const[0]

        def power(n):
            pool.wait_ge(ms_ready, n + 1)
            pool.tensor_tensor(rstd[:, :], ms[:, :], half_pow[:, 0:T], ALU.pow).then_inc(rstd_ready, 1)

        def rotate(dst, src, heads, width, half, c0):
            def dims(v, a):
                return v.rearrange("p t (h d) -> p t h d", d=width)[:, :, :, a:a + half]
            cos = cost[:, :, c0:c0 + half].unsqueeze(2).broadcast_to([P, T, heads, half])
            sin = sint[:, :, c0:c0 + half].unsqueeze(2).broadcast_to([P, T, heads, half])
            prods = []
            for r, (a, tab) in enumerate(((0, cos), (half, sin), (half, cos), (0, sin))):
                o = rt[r][:, 0:T * heads * half].rearrange("p (t h d) -> p t h d", t=T, h=heads)
                for t in range(T):
                    ins = pool.tensor_tensor(o[:, t], dims(src, a)[:, t], tab[:, t], ALU.mult)
                prods.append(o)
            link(ins)
            for t in range(T):
                pool.tensor_tensor(dims(dst, 0)[:, t], prods[0][:, t], prods[1][:, t], ALU.subtract)
                ins = pool.tensor_tensor(dims(dst, half)[:, t], prods[2][:, t], prods[3][:, t], ALU.add)
            return ins

        steps = [0]

        def link(ins):
            steps[0] += 1
            ins.then_inc(pool_step, 1)
            pool.wait_ge(pool_step, steps[0])

        power(0)
        for l in range(DEPTH):
            J = L1[l]
            power(norm1(l, 0))
            wait_drained(pool, *J["qk"])
            if l == 0:
                pool.wait_ge(tables_ready, 2)
            link(rotate(qk_rows[:, :, 0:768], qk_rows[:, :, 0:768], 12, HD, 8, 0))
            rotate(qk_rows[:, :, 768:1280], qk_rows[:, :, 768:1280], 16, DIFF_QK, 4, 8).then_inc(rope_ready, T)
            pool.wait_ge(dsum_ready, l + 1)
            pool.tensor_tensor(dstat2[:, :, :], dstat[:, :, :],
                               half_pow[:, 0:T * DIFF_H].rearrange("p (t h) -> p t h", t=T),
                               ALU.pow).then_inc(dpow_ready, 1)
            power(norm1(l, 1))
        wait_drained(pool, *L1[DEPTH - 1]["mT"])
        pool.dma_start(gain_row, A["post_g"][0]).then_inc(row_loaded, 16)
        power(final)
        wait_drained(pool, *L1[DEPTH - 1]["xoT"])
        pool.dma_start(attn[:, :, :], A["mem2"].rearrange("(t p) n -> p t n", p=P)).then_inc(mem2_loaded, 16)
        power(mem2_norm)

        def post_gain(l, i):
            if (l, i) == (0, 0):
                pool.wait_ge(x_ready, T)
            else:
                pool.wait_ge(x_ready, x_at(l, i))
            pool.dma_start(gain_row, A["post_g"][1 + 3 * l + i]).then_inc(row_loaded, 16)

        for l in range(DEPTH):
            J = L2[l]
            post_gain(l, 0)
            power(norm2(l, 0))
            power(norm2(l, 1))
            post_gain(l, 1)
            power(norm2(l, 2))
            pool.wait_ge(params_loaded, N_SMALL)
            wait_drained(pool, *J["crT"])
            for v in range(2):
                for g in range(NSA_G):
                    for half in range(2):
                        raw = cmp_raw[:, 2 * v + g, :].rearrange("p (i m) -> p m i", m=8)
                        src = raw[:, :, half:half + NCMP]
                        where = cmp_pos[:, l, v, 8 * half:8 * half + 8].unsqueeze(2).broadcast_to([P, 8, NCMP])
                        ins = pool.tensor_tensor(cmp_x[:, v, 8 * half:8 * half + 8, g, :], src, where, ALU.add)
            ins.then_inc(cmpx_ready, 1)
            wait_drained(pool, *J["q"])
            link(pool.tensor_copy(qrot, q_rows))
            link(rotate(qrot, q_rows, NSA_H, HD, 8, 12))
            for slot in (2, 4):
                ins = rotate(kv[:, :, slot * P:(slot + 1) * P], kv[:, :, slot * P:(slot + 1) * P], NSA_G, HD, 8, 12)
                if slot == 2:
                    link(ins)
            ins.then_inc(rope_ready, 1)
            for g in range(4):
                pool.wait_ge(ysum_part, 4 * l + g + 1)
                c0 = (g % 2) * 4 * HD
                y = attn[:, :, c0:c0 + 4 * HD]
                pool.tensor_tensor(y, y, rows[:, :, g * 4 * HD:(g + 1) * 4 * HD], ALU.add).then_inc(ysum_done, 1)
                if g == 1:
                    pool.wait_ge(ysum_done, 4 * l + g + 1)
            power(norm2(l, 3))
            post_gain(l, 2)
            power(norm2(l, 4))
            power(norm2(l, 5))
            if l + 1 < DEPTH:
                pass

    @block.scalar
    def _(act):
        steps = [0]

        def link(ins):
            steps[0] += 1
            ins.then_inc(act_step, 1)
            act.wait_ge(act_step, steps[0])

        def drain(job, pieces):
            wait_full(act, job)
            for dst, src, factor in pieces:
                ins = act.activation(dst, src, ACT.Copy, scale=factor)
            ins.then_inc(drained[job.bank], 1)

        next_split = [0]

        def keep_up(last, ahead=2):
            while next_split[0] <= min(last + ahead, n_units - 1):
                u = next_split[0]
                next_split[0] += 1
                if is_raw[u]:
                    continue
                act.wait_ge(loaded[u % RAW], 16 * (u // RAW + 1))
                if split_free(u):
                    act.wait_ge(*split_free(u))
                slot, n = (nth_split[u] - 1) % SPLIT, width_of[u]
                act.activation(w_hi[:, slot, 0:n], raw[:, u % RAW, 0:n], ACT.Copy).then_inc(weights_hi, 1)

        def square_sums(src):
            for t in range(T):
                act.activation(rows[:, t, :], src[:, t, :], ACT.Square,
                               accum_out=sumsq[:, t:t + 1]).then_inc(sumsq_ready, 1)

        def copied(jobs, dst, factors):
            for i, job in enumerate(jobs):
                if i % 2 == 0:
                    b = bank[job.bank]
                    drain(job, [(dst[:, 2 * i + c, :], b[:, c * SEQ:(c + 1) * SEQ], factors(2 * i + c))
                                for c in range(2)])

        def turned(jobs, dst, factor):
            for i, job in enumerate(jobs):
                wait_full(act, job)
                if isinstance(factor, float):
                    ins = act.activation(dst[0][:, 2 * i:2 * i + 2, :], bank[job.bank][:, :], ACT.Copy, scale=factor)
                else:
                    for c in range(2):
                        ins = act.activation(dst[0][:, 2 * i + c, :], bank[job.bank][:, c * SEQ:(c + 1) * SEQ],
                                             ACT.Copy, scale=factor(2 * i + c))
                ins.then_inc(turn_hi, 1)

        def memory_hi(mem_jobs, which, l, last_read):
            wait_drained(act, *mem_jobs)
            if last_read is not None:
                wait_full(act, last_read)
            for c in range(KC):
                ins = act.activation(m_hi[:, c, :], memnT[:, c, :], ACT.Copy, scale=gain_cols[:, which, l, c:c + 1])
            ins.then_inc(mem_hi, 1)

        def gained(which, l):
            return lambda c: gain_cols[:, which, l, c:c + 1]

        def softmax_numerators(J, causal_heads, base):
            for i, job in enumerate(J["S"]):
                act.wait_ge(max_ready, base + i + 1)
                if i >= 3:
                    wait_full(act, J["PT"][i - 3])
                b = bank[job.bank]
                for t in range(T):
                    n = P if causal_heads and t == 0 else SEQ
                    ins = act.activation(probs[:, i % 3, t * SEQ:t * SEQ + n], b[:, t * SEQ:t * SEQ + n],
                                         ACT.Exp, bias=negmax[:, i, t:t + 1],
                                         accum_out=rowsum[:, i, t:t + 1])
                ins.then_inc(drained[job.bank], 1)

        def post_squares(jobs):
            for j, job in enumerate(jobs):
                wait_full(act, job)
                act.activation(rows[:, j % 2, (j // 2) * NB:(j // 2 + 1) * NB], bank[job.bank][:, :], ACT.Square,
                               accum_out=sumsq4[:, j % 2, j // 2:j // 2 + 1]).then_inc(sumsq_ready, 1)

        def tanh_gates(J, base, aside=None):
            for j in range(FC):
                job = J["inner"][j]
                if j >= 2 and j % 2 == 0:
                    keep_up(J["out_unit"][j - 3] if j > 2 else job.last - 2)
                keep_up(job.last)
                wait_full(act, job)
                if j >= 2:
                    wait_drained(act, J["inner"][j - 2])
                act.activation(ffn_th[:, j % 2, 0:SEQ], bank[job.bank][:, 0:SEQ], ACT.Tanh,
                               scale=0.5).then_inc(ffn_th_ready, 1)
                if j == 5 and aside is not None:
                    aside()
            keep_up(J["out_unit"][-1], 3)

        def layer1(l):
            J = L1[l]
            wait_x1(act, l, 0)
            square_sums(x)
            for c, job in enumerate(J["xk"]):
                keep_up(job.last)
                drain(job, [(xkT[:, 2 * c:2 * c + 2, :], bank[job.bank][:, :], 1.0)])
            keep_up(J["xk"][1].last, 3)
            turned(J["hT"], hT, gained(0, l))
            for u, job in enumerate(J["s"]):
                b = bank[job.bank]
                keep_up(job.last)
                drain(job, [(sT[:, 2 * u + c, :], b[:, c * SEQ:(c + 1) * SEQ],
                             SCALE if 2 * u + c < 3 else 1.0) for c in range(2)])
            for j in (0, 2, 4):
                n = 256 if j == 4 else NB
                job = J["qk"][j]
                keep_up(job.last)
                drain(job, [(qk_rows[:, 0, (j // 2) * NB:(j // 2) * NB + n], bank[job.bank][:, 0:n], 1.0)])
            keep_up(J["qk"][5].last, 3)
            for h, job in enumerate(J["z"]):
                drain(job, [(zall[:, h, :], bank[job.bank][:, 0:384], 1.0)])
            for j in (0, 2):
                job = J["v"][j]
                keep_up(job.last)
                drain(job, [(v_rows[:, 0, (j // 2) * NB:(j // 2 + 1) * NB], bank[job.bank][:, :], 1.0)])
            keep_up(J["v"][3].last, 3)
            copied(J["qkT"], qkT, lambda c: qk_scale[c])
            wait_full(act, J["qkT"][-1])
            for j, job in enumerate(J["gate"]):
                keep_up(job.last)
                wait_full(act, job)
                act.activation(gates[:, j % 2, (j // 2) * NB:(j // 2 + 1) * NB], bank[job.bank][:, :], ACT.Tanh,
                               scale=0.5).then_inc(th_ready, 1)
                if j == 1:
                    wait_drained(act, *J["z"])
                    link(act.activation(ln1p[:, :, :], zall[:, :, :], ACT.Abs))
                    link(act.activation(ln1p[:, :, :], ln1p[:, :, :], ACT.Exp, scale=-1.0))
            act.activation(ln1p[:, :, :], ln1p[:, :, :], ACT.Ln, bias=1.0).then_inc(lnz_ready, 1)
            keep_up(J["gate"][3].last, 3)
            if l == 0:
                act.wait_ge(lam_ready, 1)
                act.activation(lam_exp[:, :, :], lam_dot[:, :, :], ACT.Exp).then_inc(lam_ready, 1)
            softmax_numerators(J["att"], True, 18 * l)
            for h in range(SB_H):
                act.wait_ge(arg_ready, SB_H * l + h + 1)
                act.activation(zall[:, h, :], zall[:, h, :], ACT.Exp).then_inc(w_ready, 1)
            turned(J["mT"], hT, 1.0)
            keep_up(J["out"][0].last)
            wait_full(act, J["out"][1])
            keep_up(J["out"][2].last)
            wait_full(act, J["out"][3])
            keep_up(J["out"][3].last, 3)
            wait_x1(act, l, 1)
            square_sums(x)
            keep_up(J["xv"][0].last)
            drain(J["xv"][0], [(xv[:, 0, :], bank[J["xv"][0].bank][:, :], 1.0)])
            keep_up(J["xv"][0].last, 3)
            turned(J["hT2"], hT, gained(1, l))
            if l + 1 < DEPTH:
                memory_hi(mem1, 2, l + 1, J["xv"][-1])
            for u, job in enumerate(J["xq"]):
                keep_up(job.last)
                drain(job, [(xqT1[:, 2 * u:2 * u + 2, :], bank[job.bank][:, :], XD ** -0.5)])
            keep_up(J["xq"][1].last, 3)
            softmax_numerators(J["xatt"], False, 18 * l + 14)
            turned(J["xoT"], hT, 1.0)
            keep_up(J["xo"][0].last)
            wait_full(act, J["xo"][1])
            keep_up(J["xo"][2].last)
            wait_full(act, J["xo"][3])
            keep_up(J["xo"][3].last, 3)

        def layer2(l):
            J = L2[l]
            act.wait_ge(x_ready, x_at(l, 0))
            if l == 0:
                wait_full(act, mem2[-1])
            square_sums(x)
            for c, job in enumerate(J["mk"]):
                keep_up(job.last)
                drain(job, [(xkT[:, 2 * c:2 * c + 2, :], bank[job.bank][:, :], 1.0)])
            keep_up(J["mk"][1].last, 3)
            turned(J["hT1"], hT, gained(3, l))
            tanh_gates(J["ffn1"], 2 * FC * l)
            post_squares(J["ffn1"]["acc"])
            keep_up(J["mv"][0].last)
            drain(J["mv"][0], [(xv[:, 0, :], bank[J["mv"][0].bank][:, :], 1.0)])
            keep_up(J["mv"][0].last, 3)
            act.wait_ge(x_ready, x_at(l, 1))
            square_sums(x)
            turned(J["hT"], hT, gained(4, l))
            keep_up(J["q"][0].last)
            drain(J["q"][0], [(q_rows[:, 0, :], bank[J["q"][0].bank][:, :], 1.0)])
            keep_up(J["kv"][0].last)
            drain(J["kv"][0], [(kv[:, 0, 0:NB], bank[J["kv"][0].bank][:, :], 1.0)])
            keep_up(J["kv"][2].last)
            drain(J["kv"][2], [(kv[:, 0, NB:KVW], bank[J["kv"][2].bank][:, 0:KVW - NB], 1.0)])
            raw_drain(act, J["crT"][0], 0)
            for half, job in enumerate(J["cmp"]):
                wait_full(act, job)
                for v in range(2):
                    ins = act.activation(cmp_h[:, 2 * v + half, :], bank[job.bank][:, 30 * v:30 * v + 30],
                                         ACT.Identity, bias=cmp_b1[:, l, v, half:half + 1])
                ins.then_inc(drained[job.bank], 1)
            for u, job in enumerate(J["qmem"]):
                keep_up(job.last)
                drain(job, [(xqT2[:, 2 * u:2 * u + 2, :], bank[job.bank][:, :], XD ** -0.5)])
            for c in range(4):
                job = J["conv"][c]
                keep_up(job.last)
                wait_full(act, job)
                if c >= 2:
                    wait_drained(act, J["conv"][c - 2])
                act.activation(utmp[:, c % 2, :], bank[job.bank][:, 0:SEQ], ACT.Copy).then_inc(u_ready, 1)
            keep_up(J["conv"][4].last)
            act.wait_ge(cmpu_ready, l + 1)
            act.activation(cmp_t[:, :, :], cmp_t[:, :, :], ACT.Tanh,
                           scale=math.sqrt(2.0 / math.pi)).then_inc(cmpth_ready, 1)
            wait_drained(act, *J["kv"])
            act.activation(nsa_g[:, :, :], kv[:, :, 6 * P:KVW], ACT.Tanh, scale=0.5).then_inc(nsag_ready, 1)
            keep_up(J["conv"][5].last, 3)
            copied(J["qkT"], qkT, lambda c: qk2_scale[c])
            job = J["kvc"][0]
            drain(job, [(kcT[64 * g:64 * g + 64, :], bank[job.bank][0:64, NPAD * g:NPAD * g + NPAD], 0.5)
                        for g in range(NSA_G)])
            act.wait_ge(cexp_in, l + 1)
            act.activation(cs[:, :, :], cs[:, :, :], ACT.Exp).then_inc(cexp_out, 1)
            drain(J["cpT"][0], [(cmp_pT[:, :, :], bank[J["cpT"][0].bank][:, 0:SEQ], 1.0)])
            softmax_numerators(J["att"], True, 18 * DEPTH + 20 * l)
            softmax_numerators(J["matt"], False, 18 * DEPTH + 20 * l + 16)
            turned(J["yT"], memS, 1.0)
            for n in range(6):
                for t in range(T):
                    job = J["merge"][2 * n + t]
                    keep_up(job.last)
                    wait_full(act, job)
                    if n >= 2:
                        wait_drained(act, J["br"][2 * n - 4 + t])
                    act.activation(merge[:, n % 2, t, :], bank[job.bank][:, :], ACT.Tanh,
                                   scale=0.5).then_inc(drained[job.bank], 1)
                keep_up(J["br"][2 * n].last)
            wait_full(act, J["br"][-1])
            keep_up(J["br"][-1].last, 3)
            turned(J["mT"], hT, 0.5)
            keep_up(J["out"][0].last)
            wait_full(act, J["out"][1])
            keep_up(J["out"][2].last)
            post_squares(J["out"])
            keep_up(J["out"][2].last, 3)
            act.wait_ge(x_ready, x_at(l, 2))
            square_sums(x)
            turned(J["hT2"], hT, gained(6, l))
            more = l + 1 < DEPTH
            tanh_gates(J["ffn2"], 2 * FC * l + FC,
                       (lambda: memory_hi(mem2, 5, l + 1, J["br"][-1])) if more else None)
            post_squares(J["ffn2"]["acc"])

        act.wait_ge(mem_loaded, 16)
        square_sums(attn)
        keep_up(-1, 3)
        copied(mem1, memnT, lambda c: 1.0)
        act.wait_ge(params_loaded, N_SMALL)
        memory_hi(mem1, 2, 0, None)
        act.wait_ge(tables_in, 1)
        act.activation(sint[:, :, :], ang[:, :, :], ACT.Sin).then_inc(tables_ready, 1)
        act.activation(cost[:, :, :], ang2[:, :, :], ACT.Sin).then_inc(tables_ready, 1)
        for l in range(DEPTH):
            layer1(l)
        wait_drained(act, *L1[DEPTH - 1]["xo"])
        square_sums(x)
        act.wait_ge(mem2_loaded, 16)
        square_sums(attn)
        copied(mem2, memnT, lambda c: 1.0)
        memory_hi(mem2, 5, 0, L1[DEPTH - 1]["xv"][-1])
        for l in range(DEPTH):
            layer2(l)

    @block.vector
    def _(ve):
        steps = [0]

        def link(ins):
            steps[0] += 1
            ins.then_inc(vec_step, 1)
            ve.wait_ge(vec_step, steps[0])

        def scaled(dst, src, factor):
            if isinstance(factor, float) and factor == 1.0:
                return ve.tensor_copy(dst, src)
            return ve.tensor_scalar(dst, src, factor, None, ALU.mult)

        def drain(job, pieces):
            wait_full(ve, job)
            for dst, src, factor in pieces:
                ins = scaled(dst, src, factor)
            ins.then_inc(drained[job.bank], 1)

        next_split = [0]

        def keep_up(last, ahead=2):
            while next_split[0] <= min(last + ahead, n_units - 1):
                u = next_split[0]
                next_split[0] += 1
                if is_raw[u]:
                    continue
                slot, n = (nth_split[u] - 1) % SPLIT, width_of[u]
                ve.wait_ge(weights_hi, nth_split[u])
                ve.tensor_tensor(w_lo[:, slot, 0:n], raw[:, u % RAW, 0:n], w_hi[:, slot, 0:n].bitcast(F32),
                                 ALU.subtract).then_inc(weights_split, 1)

        def copied(jobs, dst, factors):
            for i, job in enumerate(jobs):
                if i % 2 == 1:
                    b = bank[job.bank]
                    drain(job, [(dst[:, 2 * i + c, :], b[:, c * SEQ:(c + 1) * SEQ], factors(2 * i + c))
                                for c in range(2)])

        def turned(jobs, dst, factor):
            for i, job in enumerate(jobs):
                ve.wait_ge(turn_hi, job.hi)
                if isinstance(factor, float):
                    hi, lo = (part[:, 2 * i:2 * i + 2, :].rearrange("p c n -> p (c n)") for part in dst)
                    ins = ve.scalar_tensor_tensor(out=lo, in0=bank[job.bank][:, :], scalar=factor,
                                                  in1=hi.bitcast(F32), op0=ALU.mult, op1=ALU.subtract)
                else:
                    for c in range(2):
                        ins = ve.scalar_tensor_tensor(
                            out=dst[1][:, 2 * i + c, :], in0=bank[job.bank][:, c * SEQ:(c + 1) * SEQ],
                            scalar=factor(2 * i + c), in1=dst[0][:, 2 * i + c, :].bitcast(F32), op0=ALU.mult,
                            op1=ALU.subtract)
                ins.then_inc(drained[job.bank], 1)

        def memory_lo(n, which, l):
            ve.wait_ge(mem_hi, n)
            for c in range(KC):
                ins = ve.scalar_tensor_tensor(out=m_lo[:, c, :], in0=memnT[:, c, :],
                                              scalar=gain_cols[:, which, l, c:c + 1],
                                              in1=m_hi[:, c, :].bitcast(F32), op0=ALU.mult, op1=ALU.subtract)
            ins.then_inc(memT_ready, 1)

        def gained(which, l):
            return lambda c: gain_cols[:, which, l, c:c + 1]

        def mean(n):
            ve.wait_ge(sumsq_ready, sq[n])
            ve.tensor_scalar(ms[:, :], sumsq[:, :], 1.0 / D, EPS, ALU.mult, ALU.add).then_inc(ms_ready, 1)
            ve.wait_ge(rstd_ready, n + 1)

        def normalise(n, src):
            mean(n)
            for t in range(T):
                ve.tensor_scalar(rows[:, t, :], src[:, t, :], rstd[:, t:t + 1], None,
                                 ALU.mult).then_inc(rows_ready, 1)

        def post_norm(n, jobs, factor, row):
            ve.wait_ge(sumsq_ready, sq[n])
            link(ve.tensor_tensor(ms[:, :], sumsq4[:, :, 0], sumsq4[:, :, 1], ALU.add))
            ve.tensor_scalar(ms[:, :], ms[:, :], 1.0 / (D * factor * factor), EPS / (factor * factor), ALU.mult,
                             ALU.add).then_inc(ms_ready, 1)
            ve.wait_ge(rstd_ready, n + 1)
            ve.wait_ge(row_loaded, 16 * row)
            for t in range(T):
                for c in range(2):
                    job = jobs[2 * c + t]
                    ve.scalar_tensor_tensor(out=rows[:, t, c * NB:(c + 1) * NB], in0=bank[job.bank][:, :],
                                            scalar=rstd[:, t:t + 1], in1=gain_row[:, c * NB:(c + 1) * NB],
                                            op0=ALU.mult, op1=ALU.mult).then_inc(drained[job.bank], 1)
                wait_drained(ve, jobs[t], jobs[2 + t])
                ve.tensor_tensor(x[:, t, :], x[:, t, :], rows[:, t, :], ALU.add).then_inc(x_ready, 1)

        def add_to_x(jobs):
            for j, job in enumerate(jobs):
                xs = x[:, j % 2, (j // 2) * NB:(j // 2 + 1) * NB]
                keep_up(job.last)
                wait_full(ve, job)
                ve.tensor_tensor(xs, bank[job.bank][:, :], xs, ALU.add).then_inc(drained[job.bank], 1)

        def attention(J, causal_heads, put):
            n = J["n"]
            for i in range(n + 3):
                if i < n:
                    wait_full(ve, J["S"][i])
                    ve.tensor_reduce(negmax[:, i, :], bank[J["S"][i].bank][:, :].rearrange("p (t n) -> p t n", t=T),
                                     AX.X, ALU.max, negate=True).then_inc(max_ready, 1)
                if 2 <= i < n + 2:
                    i2 = i - 2
                    if i2 >= 3:
                        ve.wait_ge(pv_done, J["pv"] + i2 - 2)
                    w = 384 if causal_heads else NB
                    drain(J["PT"][i2], [(probsT[:, i2 % 3, 0:w], bank[J["PT"][i2].bank][:, 0:w], 1.0)])
                for g, s0 in enumerate(J["starts"]):
                    s1 = s0 + J["groups"][g]
                    if i - 3 == s1 - 1:
                        wait_full(ve, J["O"][g])
                        link(ve.reciprocal(rinv[:, s0:s1, :], rowsum[:, s0:s1, :]))
                        put(g, s0, s1, J["O"][g])

        def by_head(v, heads, width):
            return v.rearrange("p t (h d) -> p h t d", h=heads)

        def over_dims(v, heads, width):
            return v.unsqueeze(3).broadcast_to([P, heads, T, width])

        def put_plain(c_of):
            def put(g, s0, s1, job):
                n = s1 - s0
                c0, dst, width = c_of(g)
                ve.tensor_tensor(by_head(dst[:, :, c0:c0 + n * width], n, width),
                                 bank[job.bank][:, 0:n * 2 * width].rearrange("p (h t d) -> p h t d", h=n, t=T),
                                 over_dims(rinv[:, s0:s1, :], n, width), ALU.mult).then_inc(drained[job.bank], 1)
            return put

        def differential(l, J):
            wait_drained(ve, *J["att"]["O"][2:4])
            if l == 0:
                lambdas()
            y = attn[:, :, MOBA_W:MOBA_W + DIFF_W]
            for t in range(T):
                pair = rows[:, t, 0:NB].rearrange("p (h c d) -> p h c d", h=DIFF_H, c=2)
                ins = ve.scalar_tensor_tensor(out=y[:, t, :].rearrange("p (h d) -> p h d", h=DIFF_H),
                                              in0=pair[:, :, 1, :], scalar=neg_lam[:, l:l + 1],
                                              in1=pair[:, :, 0, :], op0=ALU.mult, op1=ALU.add)
            link(ins)
            yh = y.rearrange("p t (h d) -> p t h d", h=DIFF_H)
            link(ve.tensor_tensor(dsq[:, :, :, :], yh, yh, ALU.mult))
            link(ve.tensor_reduce(dstat[:, :, :], dsq[:, :, :, :], AX.X, ALU.add))
            ve.tensor_scalar(dstat[:, :, :], dstat[:, :, :], 1.0 / HD, EPS, ALU.mult, ALU.add).then_inc(dsum_ready, 1)
            ve.wait_ge(dpow_ready, l + 1)
            link(ve.tensor_tensor(dsq[:, :, :, :], yh, dstat2[:, :, :].unsqueeze(3).broadcast_to([P, T, DIFF_H, HD]),
                                  ALU.mult))
            for t in range(T):
                ins = ve.tensor_tensor(yh[:, t], dsq[:, t], head_g[:, l, :].unsqueeze(1).broadcast_to([P, DIFF_H, HD]),
                                       ALU.mult)
            link(ins)

        def lambdas():
            ve.wait_ge(lam_ready, 2)
            link(ve.tensor_tensor(neg_lam[:, :], lam_exp[:, :, 1], lam_exp[:, :, 0], ALU.subtract))
            link(ve.tensor_tensor(neg_lam[:, :], neg_lam[:, :], lam_const[:, :, 0], ALU.subtract))
            for k in range(DEPTH):
                ins = ve.tensor_scalar(head_g[:, k, :], head_g[:, k, :], lam_const[:, k, 1:2], None, ALU.mult)
            link(ins)

        def tables():
            ve.wait_ge(params_loaded, N_SMALL)
            link(ve.tensor_copy(pos_f[:, :, :], pos_i[:, :, :]))
            for w, (a, b) in ((0, (0, 12)), (1, (12, 20))):
                for t in range(T):
                    ins = ve.tensor_scalar(ang[:, t, a:b], inv_freq[:, a:b], pos_f[:, w, t:t + 1], None, ALU.mult)
            link(ins)
            link(ve.tensor_scalar(turns[:, :, :], ang[:, :, :], 1.0 / (2 * math.pi), None, ALU.mult))
            link(ve.tensor_copy(turns_i[:, :, :], turns[:, :, :]))
            link(ve.tensor_copy(turns[:, :, :], turns_i[:, :, :]))
            for part_of_2pi in TWO_PI:
                link(ve.scalar_tensor_tensor(out=ang[:, :, :], in0=turns[:, :, :], scalar=-part_of_2pi,
                                             in1=ang[:, :, :], op0=ALU.mult, op1=ALU.add))
            link(ve.tensor_scalar(ang2[:, :, :], ang[:, :, :], math.pi / 2, None, ALU.add))
            link(ve.tensor_scalar(wrap[:, :, :], ang2[:, :, :], math.pi, -2 * math.pi, ALU.is_gt, ALU.mult))
            link(ve.tensor_tensor(ang2[:, :, :], ang2[:, :, :], wrap[:, :, :], ALU.add))
            link(ve.tensor_scalar(ang[:, :, :], ang[:, :, :], PI_F, -PI_F, ALU.min, ALU.max))
            ve.tensor_scalar(ang2[:, :, :], ang2[:, :, :], PI_F, -PI_F, ALU.min, ALU.max).then_inc(tables_in, 1)
            link(ve.tensor_tensor(lam_prod[:, :, :, :], lam_in[:, :, 0:4:2, :], lam_in[:, :, 1:4:2, :], ALU.mult))
            ve.tensor_reduce(lam_dot[:, :, :], lam_prod[:, :, :, :], AX.X, ALU.add).then_inc(lam_ready, 1)

        def hidden(J, base, aside=None):
            for j in range(FC):
                job = J["inner"][j]
                if j >= 2 and j % 2 == 0:
                    keep_up(J["out_unit"][j - 3] if j > 2 else job.last - 2)
                keep_up(job.last)
                ve.wait_ge(ffn_th_ready, base + j + 1)
                if j >= 4:
                    ve.wait_ge(ffn_out_used, J["base"] + j - 3)
                b = bank[job.bank]
                th, h = ffn_th[:, j % 2, 0:SEQ], hid[:, j % 2, 0:SEQ]
                link(ve.scalar_tensor_tensor(out=h, in0=th, scalar=1.0, in1=b[:, 0:SEQ], op0=ALU.add,
                                             op1=ALU.mult))
                link(ve.scalar_tensor_tensor(out=h, in0=h, scalar=0.5, in1=b[:, SEQ:2 * SEQ],
                                             op0=ALU.mult, op1=ALU.mult))
                link(ve.tensor_copy(f_hi[:, j % 4, :], h))
                ve.tensor_tensor(f_lo[:, j % 4, :], h, f_hi[:, j % 4, :].bitcast(F32),
                                 ALU.subtract).then_inc(drained[job.bank], 1)
                if j == 5 and aside is not None:
                    aside()
            keep_up(J["out_unit"][-1], 3)

        def layer1(l):
            J = L1[l]
            normalise(norm1(l, 0), x)
            keep_up(J["xk"][0].last)
            keep_up(J["xk"][1].last, 3)
            turned(J["hT"], hT, gained(0, l))
            for job in J["s"]:
                keep_up(job.last)
            for j in (1, 3, 5):
                n = 256 if j == 5 else NB
                job = J["qk"][j]
                keep_up(job.last)
                drain(job, [(qk_rows[:, 1, (j // 2) * NB:(j // 2) * NB + n], bank[job.bank][:, 0:n], 1.0)])
            keep_up(J["qk"][5].last, 3)
            for j in (1, 3):
                job = J["v"][j]
                keep_up(job.last)
                drain(job, [(v_rows[:, 1, (j // 2) * NB:(j // 2 + 1) * NB], bank[job.bank][:, :], 1.0)])
            keep_up(J["v"][3].last, 3)
            copied(J["qkT"], qkT, lambda c: qk_scale[c])
            for j, job in enumerate(J["gate"]):
                g = gates[:, j % 2, (j // 2) * NB:(j // 2 + 1) * NB]
                keep_up(job.last)
                ve.wait_ge(th_ready, 4 * l + j + 1)
                ve.scalar_tensor_tensor(out=g, in0=g, scalar=1.0, in1=bank[job.bank][:, :], op0=ALU.add,
                                        op1=ALU.mult).then_inc(drained[job.bank], 1)
            keep_up(J["gate"][3].last, 3)
            ve.wait_ge(lnz_ready, l + 1)
            link(ve.scalar_tensor_tensor(out=ln1p[:, :, :], in0=zall[:, :, :], scalar=0.0, in1=ln1p[:, :, :],
                                         op0=ALU.min, op1=ALU.subtract))
            link(ve.tensor_tensor(l1m[:, :, :], ln1p[:, :, :], zall[:, :, :], ALU.subtract))
            ve.tensor_tensor(l1m[:, :, :], l1m[:, :, :], sb_keep[:, :].unsqueeze(1).broadcast_to([P, SB_H, 384]),
                             ALU.mult).then_inc(l1m_ready, 1)
            link(ve.tensor_tensor(ln1p[:, :, :], ln1p[:, :, :],
                                  sb_neg[:, :].unsqueeze(1).broadcast_to([P, SB_H, 384]), ALU.add))
            attention(J["att"], True, put_plain(lambda g: [(0, attn, HD), (4 * HD, attn, HD), (0, rows, HD),
                                                           (4 * HD, rows, HD)][g]))
            for h, job in enumerate(J["sb"]["btw"]):
                wait_full(ve, job)
                ve.tensor_tensor(zall[:, h, :], bank[job.bank][:, 0:384], ln1p[:, h, :],
                                 ALU.add).then_inc(drained[job.bank], 1)
                wait_drained(ve, job)
                ve.engine_nop().then_inc(arg_ready, 1)
            differential(l, J)
            for g, (s0, n) in enumerate(((0, 4), (4, 2))):
                job = J["sb"]["O"][g]
                c0 = MOBA_W + DIFF_W + HD * s0
                drain(job, [(by_head(attn[:, :, c0:c0 + n * HD], n, HD),
                             bank[job.bank][:, 0:n * 2 * HD].rearrange("p (h t d) -> p h t d", h=n, t=T), 1.0)])
            wait_drained(ve, *J["sb"]["O"])
            for t in range(T):
                ve.scalar_tensor_tensor(out=rows[:, t, :], in0=attn[:, t, :], scalar=0.5, in1=gates[:, t, :],
                                        op0=ALU.mult, op1=ALU.mult).then_inc(rows_ready, 1)
            turned(J["mT"], hT, 1.0)
            add_to_x(J["out"])
            keep_up(J["out"][3].last, 3)
            normalise(norm1(l, 1), x)
            keep_up(J["xv"][1].last)
            drain(J["xv"][1], [(xv[:, 1, :], bank[J["xv"][1].bank][:, :], 1.0)])
            keep_up(J["xv"][1].last, 3)
            turned(J["hT2"], hT, gained(1, l))
            if l + 1 < DEPTH:
                memory_lo(l + 2, 2, l + 1)
            for job in J["xq"]:
                keep_up(job.last)
            keep_up(J["xq"][1].last, 3)
            attention(J["xatt"], False, put_plain(lambda g: (2 * XD * g, attn, XD)))
            turned(J["xoT"], hT, 1.0)
            add_to_x(J["xo"])
            keep_up(J["xo"][3].last, 3)

        def layer2(l):
            J = L2[l]
            normalise(norm2(l, 0), x)
            for job in J["mk"]:
                keep_up(job.last)
            keep_up(J["mk"][1].last, 3)
            turned(J["hT1"], hT, gained(3, l))
            hidden(J["ffn1"], 2 * FC * l)
            post_norm(norm2(l, 1), J["ffn1"]["acc"], 0.5, 3 * l + 2)
            keep_up(J["mv"][1].last)
            drain(J["mv"][1], [(xv[:, 1, :], bank[J["mv"][1].bank][:, :], 1.0)])
            keep_up(J["mv"][1].last, 3)
            normalise(norm2(l, 2), x)
            turned(J["hT"], hT, gained(4, l))
            keep_up(J["q"][1].last)
            drain(J["q"][1], [(q_rows[:, 1, :], bank[J["q"][1].bank][:, :], 1.0)])
            keep_up(J["kv"][1].last)
            drain(J["kv"][1], [(kv[:, 1, 0:NB], bank[J["kv"][1].bank][:, :], 1.0)])
            keep_up(J["kv"][3].last)
            drain(J["kv"][3], [(kv[:, 1, NB:KVW], bank[J["kv"][3].bank][:, 0:KVW - NB], 1.0)])
            raw_drain(ve, J["crT"][1], 1)
            wait_drained(ve, *J["cmp"])
            link(ve.tensor_tensor(cmp_t[:, :, :], cmp_h[:, :, :], cmp_h[:, :, :], ALU.mult))
            link(ve.tensor_scalar(cmp_t[:, :, :], cmp_t[:, :, :], 0.044715, 1.0, ALU.mult, ALU.add))
            ve.tensor_tensor(cmp_t[:, :, :], cmp_t[:, :, :], cmp_h[:, :, :], ALU.mult).then_inc(cmpu_ready, 1)
            link(ve.memset(convT[:, :, 0:2], 0.0))
            for job in J["qmem"]:
                keep_up(job.last)
            for c in range(4):
                job = J["conv"][c]
                keep_up(job.last)
                ve.wait_ge(u_ready, 4 * l + c + 1)
                ve.tensor_tensor(convT[:, c, 2:SEQ + 2], bank[job.bank][:, SEQ:2 * SEQ], utmp[:, c % 2, :],
                                 ALU.mult).then_inc(drained[job.bank], 1)
            wait_drained(ve, *J["conv"][0:4])
            for w in range(3):
                for c in range(4):
                    src, f = convT[:, c, w:w + SEQ], conv_w[:, l, w, c:c + 1]
                    if w == 0:
                        ins = ve.tensor_scalar(yconvT[:, c, :], src, f, None, ALU.mult)
                    else:
                        ins = ve.scalar_tensor_tensor(out=yconvT[:, c, :], in0=src, scalar=f, in1=yconvT[:, c, :],
                                                      op0=ALU.mult, op1=ALU.add)
                link(ins)
            for c in range(2):
                job = J["conv"][4 + c]
                keep_up(job.last)
                wait_full(ve, job)
                y = yconvT[:, 2 * c:2 * c + 2, :].rearrange("p c n -> p (c n)")
                ve.tensor_tensor(y, bank[job.bank][:, :], y, ALU.mult).then_inc(drained[job.bank], 1)
            keep_up(J["conv"][5].last, 3)
            wait_drained(ve, *J["conv"][4:6])
            link(ve.tensor_copy(f_hi[:, :, :], yconvT[:, :, :]))
            ve.tensor_tensor(f_lo[:, :, :], yconvT[:, :, :], f_hi[:, :, :].bitcast(F32),
                             ALU.subtract).then_inc(conv_split, 1)
            ve.wait_ge(cmpth_ready, l + 1)
            if l == 0:
                link(ve.memset(cmp_g[:, :, :], 0.0))
            link(ve.scalar_tensor_tensor(
                out=cmp_g[:, :, :].rearrange("p a (g i) -> p (a g) i", g=NSA_G)[:, :, 0:NCMP],
                in0=cmp_t[:, :, :].rearrange("p a (g i) -> p (a g) i", g=NSA_G), scalar=1.0,
                in1=cmp_h[:, :, :].rearrange("p a (g i) -> p (a g) i", g=NSA_G), op0=ALU.add, op1=ALU.mult))
            for half in range(2):
                ins = ve.tensor_copy(
                    cmp_rep[:, half, :].rearrange("p (g j n) -> p g j n", g=NSA_G, j=HPG),
                    cmp_g[:, 2 + half, :].rearrange("p (g n) -> p g n", g=NSA_G).unsqueeze(2).broadcast_to(
                        [P, NSA_G, HPG, NPAD]))
            ins.then_inc(cmpg_ready, 1)
            copied(J["qkT"], qkT, lambda c: qk2_scale[c])
            ve.wait_ge(nsag_ready, l + 1)
            link(ve.tensor_scalar(nsa_g[:, :, :], nsa_g[:, :, :], 1.0, 0.5, ALU.add, ALU.mult))
            job = J["kvc"][1]
            wait_full(ve, job)
            ve.tensor_tensor(vbd[:, :, :], bank[job.bank][:, 0:HD].unsqueeze(1).broadcast_to([P, NSA_H, HD]),
                             blockdiag[:, :].unsqueeze(2).broadcast_to([P, NSA_H, HD]),
                             ALU.mult).then_inc(drained[job.bank], 1)
            for g, job in enumerate(J["cs"]):
                wait_full(ve, job)
                heads = cs[:, :, :].rearrange("p (t h) n -> p t (h n)", t=T)[:, :, g * HPG * NPAD:(g + 1) * HPG * NPAD]
                neg = cmp_neg[:, :, :].rearrange("p (t h) n -> p t (h n)", t=T)[:, :, g * HPG * NPAD:(g + 1) * HPG * NPAD]
                ve.tensor_tensor(heads, bank[job.bank][:, 0:T * HPG * NPAD].rearrange("p (t n) -> p t n", t=T), neg,
                                 ALU.add).then_inc(drained[job.bank], 1)
            wait_drained(ve, *J["cs"])
            link(ve.tensor_reduce(cstat[:, 0, :], cs[:, :, :], AX.X, ALU.max))
            ve.tensor_tensor(cs[:, :, :], cs[:, :, :], cstat[:, 0, :].unsqueeze(2).broadcast_to([P, 16, NPAD]),
                             ALU.subtract).then_inc(cexp_in, 1)
            ve.wait_ge(cexp_out, l + 1)
            link(ve.tensor_tensor(cs[:, :, :], cs[:, :, :], cmp_keep[:, :, :], ALU.mult))
            link(ve.tensor_reduce(cstat[:, 1, :], cs[:, :, :], AX.X, ALU.add))
            link(ve.tensor_scalar(cstat[:, 1, :], cstat[:, 1, :], 1e-30, None, ALU.max))
            link(ve.reciprocal(cstat[:, 2, :], cstat[:, 1, :]))
            ve.tensor_tensor(cs[:, :, :], cs[:, :, :], cstat[:, 2, :].unsqueeze(2).broadcast_to([P, 16, NPAD]),
                             ALU.mult).then_inc(cmpp_ready, 1)

            def gate_of(b):
                return nsa_g[:, :, :].rearrange("p t (h b) -> p t h b", b=3)[:, :, :, b]

            for t, job in enumerate(J["co"]):
                wait_full(ve, job)
                ve.tensor_tensor(attn[:, t, 0:NSA_W].rearrange("p (h d) -> p h d", h=NSA_H),
                                 bank[job.bank][:, :].rearrange("p (h d) -> p h d", h=NSA_H),
                                 gate_of(0)[:, t].unsqueeze(2).broadcast_to([P, NSA_H, HD]),
                                 ALU.mult).then_inc(drained[job.bank], 1)
            wait_drained(ve, *J["co"])

            def put_nsa(g, s0, s1, job):
                b, h0 = 1 + g // 2, 4 * (g % 2)
                link(ve.tensor_tensor(gsc[:, s0:s1, :], rinv[:, s0:s1, :],
                                      gate_of(b)[:, :, h0:h0 + 4].rearrange("p t h -> p h t"), ALU.mult))
                ve.tensor_tensor(by_head(rows[:, :, g * 4 * HD:(g + 1) * 4 * HD], 4, HD),
                                 bank[job.bank][:, :].rearrange("p (h t d) -> p h t d", h=4, t=T),
                                 over_dims(gsc[:, s0:s1, :], 4, HD), ALU.mult).then_inc(drained[job.bank], 1)
                wait_drained(ve, job)
                ve.engine_nop().then_inc(ysum_part, 1)

            attention(J["att"], True, put_nsa)
            attention(J["matt"], False, put_plain(lambda g: (NSA_W + 2 * XD * g, attn, XD)))
            turned(J["yT"], memS, 1.0)
            for c in range(2):
                for b in range(3):
                    n = 3 * c + b
                    keep_up(J["merge"][2 * n].last)
                    for t in range(T):
                        job = J["br"][2 * n + t]
                        keep_up(job.last)
                        wait_drained(ve, J["merge"][2 * n + t])
                        wait_full(ve, job)
                        cols = slice(c * NB, (c + 1) * NB)
                        dst = rows[:, t, cols] if b == 0 else attn[:, t, 0:NB]
                        ve.scalar_tensor_tensor(out=dst, in0=merge[:, n % 2, t, :], scalar=1.0,
                                                in1=bank[job.bank][:, :], op0=ALU.add,
                                                op1=ALU.mult).then_inc(drained[job.bank], 1)
                        if b:
                            wait_drained(ve, job)
                            ins = ve.tensor_tensor(rows[:, t, cols], rows[:, t, cols], dst, ALU.add)
                            if n == 5:
                                ins.then_inc(rows_ready, 1)
                            else:
                                link(ins)
            keep_up(J["br"][-1].last, 3)
            turned(J["mT"], hT, 0.5)
            keep_up(J["out"][0].last)
            keep_up(J["out"][2].last, 3)
            post_norm(norm2(l, 3), J["out"], 1.0, 3 * l + 3)
            normalise(norm2(l, 4), x)
            turned(J["hT2"], hT, gained(6, l))
            more = l + 1 < DEPTH
            hidden(J["ffn2"], 2 * FC * l + FC,
                   (lambda: memory_lo(DEPTH + l + 2, 5, l + 1)) if more else None)
            post_norm(norm2(l, 5), J["ffn2"]["acc"], 0.5, 3 * l + 4)

        normalise(0, attn)
        copied(mem1, memnT, lambda c: 1.0)
        tables()
        memory_lo(1, 2, 0)
        keep_up(-1, 3)
        for l in range(DEPTH):
            layer1(l)
        mean(final)
        ve.wait_ge(row_loaded, 16)
        for t in range(T):
            ve.scalar_tensor_tensor(out=x[:, t, :], in0=x[:, t, :], scalar=rstd[:, t:t + 1], in1=gain_row,
                                    op0=ALU.mult, op1=ALU.mult).then_inc(x_ready, 1)
        normalise(mem2_norm, attn)
        copied(mem2, memnT, lambda c: 1.0)
        memory_lo(DEPTH + 1, 5, 0)
        for l in range(DEPTH):
            layer2(l)


def weight_columns(W):
    def cols(*spans):
        return np.concatenate([np.arange(a, b) for a, b in spans])

    m = MOBA_W
    at = np.cumsum([0, m, m, m, m, DIFF_W, DIFF_W, DIFF_W, DIFF_W, SB_W, SB_W, SB_W, SB_W])
    piece = lambda i: (at[i], at[i + 1])
    mix = np.cumsum((0,) + MIX)
    heads = np.concatenate([np.arange(HD) + HD * h for j in range(HPG) for h in (j, j + HPG)])
    pairs = np.concatenate([np.arange(P) + P * (j + side) for j in range(FC) for side in (0, FC)])
    table = {
        "w_xkv_k": (W["w_xkv"], cols((0, XW))), "w_xkv_v": (W["w_xkv"], cols((XW, 2 * XW))),
        "w_s": (W["w_in"], cols(piece(8), piece(9))),
        "w_qk": (W["w_in"], cols(piece(0), piece(1), piece(4), piece(5))),
        "w_v": (W["w_in"], cols(piece(2), piece(6), piece(10))),
        "w_gate": (W["w_in"], cols(piece(3), piece(7), piece(11))),
        "w_out": (W["w_out"], cols((0, D))), "w_xq": (W["w_xq"], cols((0, XW))),
        "w_xo": (W["w_xo"], cols((0, D))),
        "ffn1_in": (W["ffn1_w_in_2"], pairs), "ffn1_out": (W["ffn1_w_out_2"], cols((0, D))),
        "ffn2_in": (W["ffn2_w_in_2"], pairs), "ffn2_out": (W["ffn2_w_out_2"], cols((0, D))),
        "w_mkv_k": (W["w_mem_kv_2"], cols((0, XW))), "w_mkv_v": (W["w_mem_kv_2"], cols((XW, 2 * XW))),
        "w_q": (W["w_mix_in_2"], mix[3] + heads),
        "w_kv": (W["w_mix_in_2"], cols((mix[4], mix[6]))),
        "w_qmem": (W["w_mix_in_2"], cols((mix[6], mix[7]))),
        "w_conv": (W["w_mix_in_2"], np.concatenate(
            [cols((P * c, P * c + P), (mix[2] + P * c, mix[2] + P * c + P)) for c in range(4)]
            + [cols((mix[1], mix[2]))])),
        "w_merge": (W["w_mix_in_2"], cols((mix[7], mix[8]))),
        "cmp_k_w1": (W["cmp_k_w1_2"], cols((0, CMP_HID))), "cmp_v_w1": (W["cmp_v_w1_2"], cols((0, CMP_HID))),
        "w_br0": (W["w_branch_conv_2"], cols((0, D))), "w_br1": (W["w_branch_nsa_2"], cols((0, D))),
        "w_br2": (W["w_branch_mem_2"], cols((0, D))), "w_mix_out": (W["w_mix_out_2"], cols((0, D))),
    }
    return table


def weight_stream(W):
    table = weight_columns(W)
    plan = all_units()
    stream = np.zeros((len(plan), P, UNIT), np.float32)
    ordered = {}
    for n, (l, (name, k0, nk, c0, width)) in enumerate(plan):
        w, order = table[name]
        if (name, l) not in ordered:
            ordered[name, l] = np.asarray(w[l])[:, order]
        block = ordered[name, l][k0 * P:(k0 + nk) * P, c0:c0 + width]
        stream[n, :, :nk * width] = block.reshape(nk, P, width).transpose(1, 0, 2).reshape(P, nk * width)
    return stream


def kernel(**inputs):
    import concourse.bacc as bacc
    from concourse.bass_utils import run_bass_kernel_spmd

    W = {k: np.asarray(v) for k, v in inputs.items()}

    def spread(a):
        return np.ascontiguousarray(np.broadcast_to(a, (P,) + a.shape))

    def on_partitions(a):
        return np.ascontiguousarray(np.moveaxis(a.reshape(a.shape[:-1] + (-1, P)), -1, 0))

    lam_init = [0.8 - 0.6 * math.exp(-0.3 * l) for l in range(DEPTH)]
    rot64 = np.arange(0, 16, 2, dtype=np.float32) / np.float32(16)
    rot32 = np.arange(0, 8, 2, dtype=np.float32) / np.float32(8)
    theta = np.float32(THETA)
    inv = np.concatenate([np.float32(1) / theta ** rot64, np.float32(1) / theta ** rot32,
                          theta ** -rot64]).astype(np.float32)
    posts = [W["final_norm_g"]]
    for l in range(DEPTH):
        posts += [W["ffn1_norm_post_2"][l], W["mix_norm_post_2"][l], W["ffn2_norm_post_2"][l]]
    arrays = {
        "x": W["x"][0], "mem": W["mem"][0], "mem2": W["mem_2"][0], "stream": weight_stream(W),
        "gain_cols": on_partitions(np.stack([W[n] for n in (
            "attn_norm_g", "xattn_norm_g", "mem_norm_g", "ffn1_norm_pre_2", "mix_norm_pre_2", "mem_norm_2",
            "ffn2_norm_pre_2")])),
        "post_g": np.stack([spread(p) for p in posts]),
        "head_g": spread(W["diff_head_norm_g"]),
        "lam": spread(np.stack([W["diff_lambda_" + n] for n in ("q1", "k1", "q2", "k2")], axis=1)),
        "lam_const": spread(np.array([[v, 1.0 - v] for v in lam_init], np.float32)),
        "conv_w": on_partitions(W["conv_w_2"]),
        "cmp_b1": on_partitions(np.stack([W["cmp_k_b1_2"], W["cmp_v_b1_2"]], axis=1)),
        "cmp_pos": np.ascontiguousarray(np.stack([W["cmp_pos_k_2"], W["cmp_pos_v_2"]], axis=1).reshape(
            DEPTH, 2, 16, P).transpose(3, 0, 1, 2)),
        "cmp_w2": np.ascontiguousarray(np.stack([W["cmp_k_w2_2"], W["cmp_v_w2_2"]], axis=1).reshape(
            DEPTH, 2, 2, P, HD).transpose(3, 0, 1, 2, 4)),
        "inv_freq": spread(inv),
        "positions": np.ascontiguousarray(np.stack([W["positions"][0], W["positions_2"][0]]).reshape(
            2, T, P).transpose(2, 0, 1)),
    }
    arrays = {k: np.ascontiguousarray(v) for k, v in arrays.items()}
    nc = bacc.Bacc("TRN2", target_bir_lowering=False, num_devices=1)
    arrays = {"in_" + k: v for k, v in arrays.items()}
    args = {k[3:]: nc.dram_tensor(k, v.shape, mybir.dt.from_np(v.dtype), kind="ExternalInput").ap()
            for k, v in arrays.items()}
    args["out"] = nc.dram_tensor("out", (SEQ, D), F32, kind="ExternalOutput").ap()
    build(nc, args)
    r = run_bass_kernel_spmd(nc, [arrays], core_ids=[0])
    return r.results[0]["out"].reshape(1, SEQ, D)
```

```python
import math
from contextlib import ExitStack

import numpy as np

import concourse.bass as bass
from concourse import mybir

F32 = mybir.dt.float32
BF16 = mybir.dt.bfloat16
F32R = mybir.dt.float32r
I32 = mybir.dt.int32
ALU = mybir.AluOpType
ACT = mybir.ActivationFunctionType
AX = mybir.AxisListType

P = 128
SEQ = 256
T = SEQ // P
D = 1024
KC = D // P
DEPTH = 2
EPS = 1e-6
THETA = 500000.0
NEG = -1e30

MOBA_W, DIFF_W, SB_W = 384, 256, 384
MOBA_H, DIFF_H, SB_H = 6, 4, 6
HD = 64
DIFF_QK = 32
X_H, XD = 4, 128
XW = X_H * XD

D_FF = 2816
FC = D_FF // P
CONV = 512
NSA_H, NSA_G, HPG = 8, 2, 4
NSA_W = NSA_H * HD
CMP_L, CMP_STRIDE, CMP_HID = 32, 16, 256
NCMP = SEQ // CMP_STRIDE - 1
NPAD = NCMP + 1
KVW = 6 * NSA_G * HD + 3 * NSA_H
MIX = (CONV, CONV, CONV, NSA_W, 6 * NSA_G * HD, 3 * NSA_H, XW, 3 * D)

UNIT = 1024
RAW = 5
SPLIT = 3
NB = 512


def cols_units(name, chunks, first=0):
    return [(name, 0, KC, P * c, P) for c in range(first, first + chunks)]


def rows_units(name, c0, width=NB, nk=KC):
    per = UNIT // width if width != KVW - NB else 2
    return [(name, k, per, c0, width) for k in range(0, nk, per)]


def layer1_units(l):
    k, s = cols_units("w_xkv_k", 4), cols_units("w_s", 6)
    return ((k + s if l else s + k)
            + rows_units("w_qk", 0) + rows_units("w_qk", NB) + rows_units("w_qk", 2 * NB, 256)
            + rows_units("w_v", 0) + rows_units("w_v", NB)
            + rows_units("w_gate", 0) + rows_units("w_gate", NB)
            + rows_units("w_out", 0) + rows_units("w_out", NB)
            + rows_units("w_xkv_v", 0) + cols_units("w_xq", 4)
            + rows_units("w_xo", 0, nk=4) + rows_units("w_xo", NB, nk=4))


def ffn_units(name):
    units = []
    for pair in range(FC // 2 + 1):
        for j in (2 * pair, 2 * pair + 1):
            if pair < FC // 2:
                units += cols_units(name + "_in", 2, 2 * j)
        for j in (2 * pair - 2, 2 * pair - 1):
            if pair:
                units += [(name + "_out", j, 1, 0, D)]
    return units


def layer2_units(l):
    keys, v0, v1 = cols_units("w_mkv_k", 4), rows_units("w_mkv_v", 0, 256), rows_units("w_mkv_v", 256, 256)
    units = (keys if l == 0 else []) + ffn_units("ffn1") + (v0 + v1 if l == 0 else v1)
    units += rows_units("w_q", 0) + rows_units("w_kv", 0) + rows_units("w_kv", NB, KVW - NB)
    units += cols_units("w_qmem", 4)
    units += [(name, k, 4, 0, CMP_HID) for name in ("cmp_k_w1", "cmp_v_w1") for k in (0, 4, 8, 12)]
    units += cols_units("w_conv", 12)
    for c in (0, NB):
        for b in range(3):
            units += rows_units("w_merge", b * D + c) + rows_units(f"w_br{b}", c, nk=4)
    units += rows_units("w_mix_out", 0) + rows_units("w_mix_out", NB)
    ahead = l + 1 < DEPTH
    return ([(l, u) for u in units] + [(l + 1, u) for u in keys if ahead]
            + [(l, u) for u in ffn_units("ffn2")] + [(l + 1, u) for u in v0 if ahead])


def all_units():
    return ([(l, u) for l in range(DEPTH) for u in layer1_units(l)]
            + [u for l in range(DEPTH) for u in layer2_units(l)])


class Job:

    def __init__(self, bank, full, drained):
        self.bank = bank
        self.full = full
        self.drained = drained
        self.last = None
        self.hi = None


class Banks:

    def __init__(self, full, drained):
        self.full_sem, self.drained_sem = full, drained
        self.fulls, self.uses, self.at = [0] * 8, [0] * 8, 0

    def take(self, among=8, base=0, full=None):
        self.at += 1
        return self.take_bank(base + self.at % among, full)

    def take_bank(self, b, full=None):
        self.uses[b] += 1
        if full is None:
            self.fulls[b] += 1
            full = (self.full_sem[b], self.fulls[b])
        return Job(b, full, self.uses[b])


def build(nc, args):
    with ExitStack() as ctx:
        program(nc, ctx, args)


def program(nc, ctx, A):
    def sb(name, shape, dt=F32):
        return ctx.enter_context(nc.sbuf_tensor(name, shape, dt))

    def sem(name):
        return ctx.enter_context(nc.semaphore(name))

    bank = [ctx.enter_context(nc.psum_tensor(f"bank{i}", [P, NB], F32)) for i in range(8)]

    raw = sb("raw", [P, RAW, UNIT])
    w_hi = sb("w_hi", [P, SPLIT, UNIT], F32R)
    w_lo = sb("w_lo", [P, SPLIT, UNIT], F32R)
    x = sb("x", [P, T, D])
    rows = sb("rows", [P, T, D])
    attn = sb("attn", [P, T, D])
    h_hi, h_lo = sb("h_hi", [P, KC, SEQ], F32R), sb("h_lo", [P, KC, SEQ], F32R)
    m_hi, m_lo = sb("m_hi", [P, KC, SEQ], F32R), sb("m_lo", [P, KC, SEQ], F32R)
    f_hi, f_lo = sb("f_hi", [P, 4, SEQ], F32R), sb("f_lo", [P, 4, SEQ], F32R)
    hT, memS, fS = (h_hi, h_lo), (m_hi, m_lo), (f_hi, f_lo)
    memnT = sb("memnT", [P, KC, SEQ])
    qkT = sb("qkT", [P, 10, SEQ])
    xkT = sb("xkT", [P, X_H, SEQ])
    xv = sb("xv", [P, T, XW])
    probs = sb("probs", [P, 3, NB])
    probsT = sb("probsT", [P, 3, NB])
    negmax = sb("negmax", [P, 16, T])
    rowsum = sb("rowsum", [P, 16, T])
    rinv = sb("rinv", [P, 16, T])
    sumsq = sb("sumsq", [P, T])
    sumsq4 = sb("sumsq4", [P, T, T])
    ms = sb("ms", [P, T])
    rstd = sb("rstd", [P, T])
    half_pow = sb("half_pow", [P, 32])
    gain_cols = sb("gain_cols", [P, 7, DEPTH, KC])
    WORK = 11520
    work = sb("work", [P, WORK])

    at = [0]

    def part(n):
        at[0] += n
        return work[:, at[0] - n:at[0]]

    qk_rows = part(T * 1280).rearrange("p (t n) -> p t n", t=T)
    gates = work[:, 0:T * D].rearrange("p (t n) -> p t n", t=T)
    mem2_rows = gates
    v_rows = part(T * D).rearrange("p (t n) -> p t n", t=T)
    xqT1 = work[:, at[0] - 4 * SEQ:at[0]].rearrange("p (c n) -> p c n", c=X_H)
    l1m = part(SB_H * 384).rearrange("p (h n) -> p h n", h=SB_H)
    sT = work[:, at[0] - SB_H * 384:at[0] - SB_H * 384 + 6 * SEQ].rearrange("p (c n) -> p c n", c=6)
    zall = part(SB_H * 384).rearrange("p (h n) -> p h n", h=SB_H)
    ln1p = part(SB_H * 384).rearrange("p (h n) -> p h n", h=SB_H)
    assert at[0] <= WORK, at
    at[0] = 0
    q_rows = part(T * NSA_W).rearrange("p (t n) -> p t n", t=T)
    qrot = part(T * NSA_W).rearrange("p (t n) -> p t n", t=T)
    merge = work[:, 0:2 * T * NB].rearrange("p (s t n) -> p s t n", s=2, t=T)
    kv = part(T * KVW).rearrange("p (t n) -> p t n", t=T)
    convT = part(4 * (SEQ + 2)).rearrange("p (c n) -> p c n", c=4)
    yconvT = part(4 * SEQ).rearrange("p (c n) -> p c n", c=4)
    bT = work[:, at[0]:at[0] + 4 * SEQ]
    cmp_raw = part(4 * P).rearrange("p (a n) -> p a n", a=4)
    cmp_rows = cmp_raw.rearrange("p a n -> p (a n)")
    cmp_x = part(2 * 16 * 2 * NCMP).rearrange("p (v m g i) -> p v m g i", v=2, m=16, g=2)
    utmp = part(2 * SEQ).rearrange("p (c n) -> p c n", c=2)
    cmp_rep = part(2 * P).rearrange("p (a n) -> p a n", a=2)
    vbd = part(NSA_H * HD).rearrange("p (h d) -> p h d", h=NSA_H)
    cs = part(T * NSA_H * NPAD).rearrange("p (h n) -> p h n", n=NPAD)
    cmp_pT = part(T * P).rearrange("p (t n) -> p t n", t=T)
    xqT2 = part(X_H * SEQ).rearrange("p (c n) -> p c n", c=X_H)
    gain_row = part(D)
    assert at[0] <= WORK, at
    ffn_th = probs
    hid = probsT
    cmp_h = sb("cmp_h", [P, 4, 30])
    cmp_t = sb("cmp_t", [P, 4, 30])
    cmp_g = sb("cmp_g", [P, 4, 32])
    kcT = sb("kcT", [P, NPAD])
    cstat = sb("cstat", [P, 3, 16])
    nsa_g = sb("nsa_g", [P, T, 3 * NSA_H])
    gsc = sb("gsc", [P, 16, T])

    dsq = rows[:, :, NB:NB + DIFF_H * HD].rearrange("p t (h d) -> p t h d", h=DIFF_H)
    rt = [probsT[:, :, :].rearrange("p s n -> p (s n)")[:, 192 * i:192 * (i + 1)] for i in range(4)]

    ident = sb("ident", [P, P])
    ident_bf = sb("ident_bf", [P, P], BF16)
    causal_bf = sb("causal_bf", [P, T, SEQ], BF16)
    later = sb("later", [P, P])
    ones = sb("ones", [P, P])
    sb_keep = sb("sb_keep", [P, 384])
    sb_neg = sb("sb_neg", [P, 384])
    cmp_keep = sb("cmp_keep", [P, T * NSA_H, NPAD])
    cmp_neg = sb("cmp_neg", [P, T * NSA_H, NPAD])
    blockdiag = sb("blockdiag", [P, NSA_H])
    pos_i = sb("pos_i", [P, 2, T], I32)
    pos_f = sb("pos_f", [P, 2, T])
    inv_freq = sb("inv_freq", [P, 20])
    ang = sb("ang", [P, T, 20])
    turns = sb("turns", [P, T, 20])
    turns_i = sb("turns_i", [P, T, 20], I32)
    wrap = sb("wrap", [P, T, 20])
    ang2 = sb("ang2", [P, T, 20])
    sint = sb("sint", [P, T, 20])
    cost = sb("cost", [P, T, 20])
    lam_in = sb("lam_in", [P, DEPTH, 4, DIFF_QK])
    lam_prod = sb("lam_prod", [P, DEPTH, 2, DIFF_QK])
    lam_dot = sb("lam_dot", [P, DEPTH, 2])
    lam_exp = sb("lam_exp", [P, DEPTH, 2])
    neg_lam = sb("neg_lam", [P, DEPTH])
    head_g = sb("head_g", [P, DEPTH, HD])
    lam_const = sb("lam_const", [P, DEPTH, 2])
    conv_w = sb("conv_w", [P, DEPTH, 3, 4])
    cmp_b1 = sb("cmp_b1", [P, DEPTH, 2, 2])
    cmp_pos = sb("cmp_pos", [P, DEPTH, 2, 16])
    cmp_w2 = sb("cmp_w2", [P, DEPTH, 2, 2, HD])
    dstat = sb("dstat", [P, T, DIFF_H])
    dstat2 = sb("dstat2", [P, T, DIFF_H])

    full = [sem(f"bank{i}_full") for i in range(8)]
    drained = [sem(f"bank{i}_drained") for i in range(8)]
    loaded = [sem(f"unit_loaded{i}") for i in range(RAW)]
    weights_hi = sem("weights_hi_ready")
    weights_split = sem("weights_split")
    weights_used = sem("weights_used")
    turn_hi = sem("turned_hi_ready")
    mem_hi = sem("memory_hi_ready")
    x_loaded = [sem(f"x_loaded{t}") for t in range(T)]
    gains_loaded, mem_loaded, params_loaded, row_loaded, stored = map(
        sem, ("gains_loaded", "mem_loaded", "params_loaded", "gain_row_loaded", "stored"))
    mem2_loaded = sem("mem2_loaded")
    consts_ready = sem("consts_ready")
    x_ready = sem("x_ready")
    sumsq_ready = sem("sumsq_ready")
    ms_ready = sem("ms_ready")
    rstd_ready = sem("rstd_ready")
    rows_ready = sem("rows_ready")
    memT_ready = sem("memT_ready")
    rope_ready = sem("rope_ready")
    tables_ready = sem("tables_ready")
    tables_in = sem("angles_ready")
    lam_ready = sem("lam_ready")
    max_ready = sem("max_ready")
    pv_done = sem("pv_done")
    ffn_th_ready = sem("ffn_th_ready")
    ffn_out_used = sem("ffn_out_used")
    lnz_ready = sem("log_1_exp_ready")
    lb_ready = sem("log_beta_ready")
    lbm_ready = sem("log_beta_masked")
    l1m_ready = sem("log_1_beta_ready")
    arg_ready = sem("exponent_ready")
    w_ready = sem("stick_weights_ready")
    th_ready = sem("gate_tanh_ready")
    vec_step, act_step, pool_step = sem("vector_step"), sem("scalar_step"), sem("pool_step")
    cmpx_ready, cmph_ready, cmpg_ready, cexp_in, cexp_out, cmpp_ready = map(sem, (
        "cmp_x_ready", "cmp_hidden_ready", "cmp_gelu_ready", "cmp_shifted", "cmp_exp_done", "cmp_probs_ready"))
    cmpu_ready, cmpth_ready = sem("cmp_cubic_ready"), sem("cmp_tanh_ready")
    ysum_part, ysum_done = sem("nsa_part_ready"), sem("nsa_part_added")
    u_ready = sem("conv_u_ready")
    conv_split = sem("conv_branch_split")
    nsag_ready = sem("nsa_gate_tanh_ready")
    dsum_ready, dpow_ready = sem("diff_ms_ready"), sem("diff_rstd_ready")

    mem1_norm = 1

    def norm1(l, i):
        return 0 if (l, i) == (0, 0) else 1 + 2 * l + i

    mem2_norm = 1 + 2 * DEPTH
    final = mem2_norm + 1

    def norm2(l, i):
        return final + 1 + 6 * l + i

    sq = []
    for n in range(norm2(DEPTH, 0)):
        post = n > final and (n - final - 1) % 2 == 1
        sq.append((sq[-1] if sq else 0) + (2 * T if post else T))

    B = Banks(full, drained)
    plan_of = all_units()
    is_raw = [u[0].startswith("cmp_") for _, u in plan_of]
    width_of = [u[2] * u[4] for _, u in plan_of]
    nth_split = np.cumsum([0 if x else 1 for x in is_raw]).tolist()
    units = []
    pvs, outs, used, turns_hi = [0], [0], [0], [0]

    def take(n):
        return [B.take() for _ in range(n)]

    def release(n, event=None):
        for k in range(n):
            if event is not None and k == n - 1:
                units.append(event)
            else:
                used[0] += 1
                units.append((weights_used, used[0]))

    def plan_turn(n):
        jobs = take(n)
        for j in jobs:
            turns_hi[0] += 1
            j.hi = turns_hi[0]
        return jobs

    def plan_norm():
        return plan_turn(4)

    def plan_cols(n):
        jobs = take(n)
        for j in jobs:
            release(2, j.full)
            j.last = len(units) - 1
        return jobs

    def plan_block(n_units):
        jobs = take(T)
        release(n_units, jobs[-1].full)
        for j in jobs:
            j.last = len(units) - 1
        return jobs

    def plan_attention(groups):
        n = sum(groups)
        S, PT, O, first = [], [], [], {}
        starts = [sum(groups[:g]) for g in range(len(groups))]
        for i in range(n + 3):
            if i < n:
                S.append(B.take(6))
            if 2 <= i < n + 2:
                PT.append(B.take(6))
            if i >= 3 and i - 3 in starts:
                g = starts.index(i - 3)
                O.append(B.take_bank(6 + g % 2, (pv_done, pvs[0] + starts[g] + groups[g])))
        B.at = 7
        base = pvs[0]
        pvs[0] += n
        return dict(n=n, groups=groups, starts=starts, S=S, PT=PT, O=O, pv=base)

    def plan_sb_out(btw):
        jobs = dict(btw=btw, O=[], pv=pvs[0])
        for g, n in ((0, 4), (1, 2)):
            jobs["O"].append(B.take(full=(pv_done, pvs[0] + 4 * g + n)))
        pvs[0] += SB_H
        return jobs

    def plan_ffn():
        last = (ffn_out_used, outs[0] + FC)
        acc = [B.take_bank(b, last if b == 3 else None) for b in range(4)]
        inner, out_unit = [], []
        base = outs[0]
        for pair in range(FC // 2 + 1):
            if pair < FC // 2:
                for j in (2 * pair, 2 * pair + 1):
                    inner.append(B.take_bank(4 + j % 4))
                    release(2, inner[-1].full)
                    inner[-1].last = len(units) - 1
            if pair:
                for j in (2 * pair - 2, 2 * pair - 1):
                    release(1, (ffn_out_used, base + j + 1))
                    out_unit.append(len(units) - 1)
        outs[0] += FC
        B.at = 3
        return dict(acc=acc, inner=inner, base=base, out_unit=out_unit)

    def plan_layer1(l):
        J = {}
        if l == 0:
            J["hT"] = plan_norm()
            J["s"] = plan_cols(2)
            J["mem1"] = take(4)
            J["s"] += plan_cols(1)
            J["xk"] = plan_cols(2)
        else:
            J["xk"] = plan_cols(1)
            J["hT"] = plan_norm()
            J["xk"] += plan_cols(1)
            J["s"] = plan_cols(3)
        J["qk"] = plan_block(4) + plan_block(4) + plan_block(2)
        J["z"] = take(SB_H)
        J["v"] = plan_block(4) + plan_block(4)
        J["qkT"] = take(5)
        J["gate"] = plan_block(4)
        btw = take(SB_H)
        J["gate"] += plan_block(4)
        J["sb"] = plan_sb_out(btw)
        J["att"] = plan_attention([4, 4, 4, 2])
        J["mT"] = plan_turn(4)
        J["out"] = plan_block(4) + plan_block(4)
        J["xv"] = plan_block(4)
        J["hT2"] = plan_norm()
        J["xq"] = plan_cols(1)
        if l == DEPTH - 1:
            J["mem2"] = take(4)
        J["xq"] += plan_cols(1)
        J["xatt"] = plan_attention([2, 2])
        J["xoT"] = plan_turn(2)
        J["xo"] = plan_block(2) + plan_block(2)
        return J

    def plan_layer2(l):
        J = L2[l]
        if l == 0:
            J["mk"] = plan_cols(2)
        J["hT1"] = plan_norm()
        J["ffn1"] = plan_ffn()
        if l == 0:
            J["mv"] = plan_block(2)
        J["mv"] += plan_block(2)
        J["hT"] = plan_norm()
        J["q"] = plan_block(4)
        J["kv"] = plan_block(4) + plan_block(4)
        J["crT"] = take(2)
        J["qmem"] = plan_cols(2)
        J["cmp"] = take(1)
        release(8, J["cmp"][0].full)
        J["conv"] = plan_cols(1)
        J["cmpT"] = take(1)
        J["conv"] += plan_cols(1)
        J["kvc"] = take(2)
        J["conv"] += plan_cols(1)
        J["qkT"] = take(5)
        J["cs"] = take(NSA_G)
        J["conv"] += plan_cols(2)
        J["cpT"] = take(1)
        J["conv"] += plan_cols(1)
        J["co"] = take(2)
        J["att"] = plan_attention([4, 4, 4, 4])
        J["matt"] = plan_attention([2, 2])
        J["merge"], J["br"] = [], []
        for n in range(6):
            J["merge"] += plan_block(4)
            J["br"] += plan_block(2)
            if n == 0:
                J["yT"] = plan_turn(4)
        J["mT"] = plan_turn(4)
        J["out"] = plan_block(4) + plan_block(4)
        if l + 1 < DEPTH:
            L2[l + 1]["mk"] = plan_cols(2)
        J["hT2"] = plan_norm()
        J["ffn2"] = plan_ffn()
        if l + 1 < DEPTH:
            L2[l + 1]["mv"] = plan_block(2)

    L1 = [plan_layer1(l) for l in range(DEPTH)]
    mem1 = L1[0]["mem1"]
    mem2 = L1[DEPTH - 1]["mem2"]
    L2 = [{} for _ in range(DEPTH)]
    for l in range(DEPTH):
        plan_layer2(l)
    n_units = len(units)
    assert n_units == len(plan_of) == A["stream"].shape[0], (n_units, len(plan_of))

    def wait_empty(pe, job):
        if job.drained > 1:
            pe.wait_ge(drained[job.bank], job.drained - 1)

    def wait_full(eng, job):
        eng.wait_ge(*job.full)

    def wait_drained(eng, *jobs):
        for job in jobs:
            eng.wait_ge(drained[job.bank], job.drained)

    order = [("n", 0, 0), "mem1", ("merged", 0), ("n", 0, 1)]
    for l in range(1, DEPTH):
        order += [("n", l, 0), ("merged", l), ("n", l, 1)]
    order += ["mem2"]
    for l in range(DEPTH):
        order += [("m", l, 0), ("m", l, 2), ("mixed", l), ("m", l, 4)]
    rows_at = {key: T * i for i, key in enumerate(order)}

    def x_at(l, i):
        return T * (1 + 3 * l + i)

    def wait_x1(eng, l, i, t):
        if i == 1:
            wait_drained(eng, L1[l]["out"][t], L1[l]["out"][2 + t])
        elif l == 0:
            eng.wait_ge(x_loaded[t], 16)
        else:
            wait_drained(eng, L1[l - 1]["xo"][t], L1[l - 1]["xo"][2 + t])

    small = [
        (head_g[:, :, :], A["head_g"]),
        (lam_in[:, :, :, :], A["lam"]), (lam_const[:, :, :], A["lam_const"]),
        (conv_w[:, :, :, :], A["conv_w"]), (cmp_b1[:, :, :, :], A["cmp_b1"]),
        (cmp_pos[:, :, :, :], A["cmp_pos"]), (cmp_w2[:, :, :, :, :], A["cmp_w2"]),
        (inv_freq[:, :], A["inv_freq"]), (pos_i[:, :, :], A["positions"]),
    ]
    N_SMALL = 16 * len(small)
    SCALE = HD ** -0.5
    qk_scale = [SCALE] * 3 + [1.0] * 3 + [DIFF_QK ** -0.5] * 2 + [1.0] * 2
    qk2_scale = [SCALE] * 8 + [1.0] * 2

    def raw_free(u):
        return units[u] if is_raw[u] else (weights_split, nth_split[u])

    def split_free(u):
        n = nth_split[u] - SPLIT
        return units[nth_split.index(n)] if n > 0 else None

    def moba_heads():
        return [dict(q=qkT[64 * (h % 2):64 * (h % 2) + 64, h // 2, :],
                     k=qkT[64 * (h % 2):64 * (h % 2) + 64, 3 + h // 2, :],
                     v=v_rows[:, :, HD * h:HD * h + HD]) for h in range(MOBA_H)]

    def diff_heads():
        out = []
        for s in range(2 * DIFF_H):
            b, c = 32 * (s % 4), s // 4
            v0 = MOBA_W + HD * (s // 2)
            out.append(dict(q=qkT[b:b + 32, 6 + c, :], k=qkT[b:b + 32, 8 + c, :], v=v_rows[:, :, v0:v0 + HD]))
        return out

    def nsa_heads():
        out = []
        for chunk, slot in ((8, 3), (9, 5)):
            for h in range(NSA_H):
                g, j = h // HPG, h % HPG
                v0 = (2 * slot + g) * HD
                out.append(dict(q=qkT[64 * g:64 * g + 64, 4 + j, :], k=qkT[64 * g:64 * g + 64, chunk, :],
                                v=kv[:, :, v0:v0 + HD]))
        return out

    def memory_heads(xqT):
        return [dict(q=xqT[:, h, :], k=xkT[:, h, :], v=xv[:, :, XD * h:XD * h + XD]) for h in range(X_H)]

    BY_TILE = [(0, 0), (1, 0), (0, 1), (1, 1)]
    BY_COLUMNS = [(0, 0), (0, 1), (1, 0), (1, 1)]
    CONSTS, FIRST_CONSTS = 21, 3
    TWO_PI = (6.28125, float(np.float32(2 * math.pi - 6.28125)),
              2 * math.pi - 6.28125 - float(np.float32(2 * math.pi - 6.28125)))
    PI_F = float(np.nextafter(np.float32(math.pi), np.float32(0)))

    def raw_drain(eng, job, v):
        wait_full(eng, job)
        tokens = bank[job.bank][0:HD, :].rearrange("p (g n two) -> p g n two", g=NSA_G, two=2)
        for odd in range(2):
            dst = cmp_raw[HD * odd:HD * odd + HD, 2 * v:2 * v + 2, :]
            if v == 0:
                ins = eng.activation(dst, tokens[:, :, :, odd], ACT.Copy)
            else:
                ins = eng.tensor_copy(dst, tokens[:, :, :, odd])
        ins.then_inc(drained[job.bank], 1)

    block = ctx.enter_context(nc.Block())


    @block.sync
    def _(sp):
        for t in range(T):
            sp.dma_start(x[:, t, :], A["x"][t * P:(t + 1) * P, :]).then_inc(x_loaded[t], 16)
        sp.dma_start(gain_cols[:, :, :, :], A["gain_cols"]).then_inc(gains_loaded, 16)
        for u in range(n_units):
            if u == 3:
                for dst, src in small:
                    sp.dma_start(dst, src).then_inc(params_loaded, 16)
                sp.dma_start(attn[:, :, :], A["mem"].rearrange("(t p) n -> p t n", p=P)).then_inc(mem_loaded, 16)
            if u >= RAW:
                sp.wait_ge(*raw_free(u - RAW))
            sp.dma_start(raw[:, u % RAW, :], A["stream"][u]).then_inc(loaded[u % RAW], 16)
        for t in range(T):
            sp.wait_ge(x_ready, x_at(DEPTH - 1, 2) + t + 1)
            sp.dma_start(A["out"][t * P:(t + 1) * P, :], x[:, t, :]).then_inc(stored, 16)
        sp.wait_ge(stored, 16 * T)

    @block.tensor
    def _(pe):
        unit = [0]

        def next_unit():
            u = unit[0]
            unit[0] += 1
            if is_raw[u]:
                pe.wait_ge(loaded[u % RAW], 16 * (u // RAW + 1))
                return u, raw[:, u % RAW, :]
            pe.wait_ge(weights_split, nth_split[u])
            slot = (nth_split[u] - 1) % SPLIT
            return u, (w_hi[:, slot, :], w_lo[:, slot, :])

        def mark(mm, u):
            if units[u][0] is weights_used:
                mm.then_inc(weights_used, 1)

        def product(out, stat, mov, first, last):
            pe.matmul(out, stat[0], mov[0], start=first, stop=False)
            pe.matmul(out, stat[0], mov[1], start=False, stop=False)
            return pe.matmul(out, stat[1], mov[0], start=False, stop=last)

        def memory_chunk(n, k):
            pe.wait_ge(memT_ready, (n - 1) * KC // 2 + k // 2 + 1)

        def project_cols(jobs, src, turned_by=None, memory=None):
            for job in jobs:
                for c in range(2):
                    u, w = next_unit()
                    if c == 0:
                        wait_empty(pe, job)
                    for k in range(KC):
                        if turned_by and k % 2 == 0:
                            wait_drained(pe, turned_by[k // 2])
                        if memory and k % 2 == 0:
                            memory_chunk(memory, k)
                        mm = product(bank[job.bank][:, c * SEQ:(c + 1) * SEQ],
                                     [part[:, k * P:(k + 1) * P] for part in w],
                                     [part[:, k, :] for part in src], k == 0, k == KC - 1)
                    mark(mm, u)
                mm.then_inc(job.full[0], 1)

        def project_rows(jobs, src, nk, per_unit, width, turned_by=None):
            for step in range(nk // per_unit):
                u, w = next_unit()
                for t, job in enumerate(jobs):
                    if step == 0:
                        wait_empty(pe, job)
                    for kk in range(per_unit):
                        k = step * per_unit + kk
                        if turned_by and t == 0 and k % 2 == 0:
                            wait_drained(pe, turned_by[k // 2])
                        mm = product(bank[job.bank][:, 0:width], [part[:, k, t * P:(t + 1) * P] for part in src],
                                     [part[:, kk * width:(kk + 1) * width] for part in w], k == 0, k == nk - 1)
                    if k == nk - 1:
                        mm.then_inc(job.full[0], 1)
                mark(mm, u)

        def turn(jobs, src):
            for i, job in enumerate(jobs):
                wait_empty(pe, job)
                for c in range(2):
                    for t in range(T):
                        mm = pe.transpose(bank[job.bank][:, c * SEQ + t * P:c * SEQ + (t + 1) * P],
                                          src(2 * i + c, t), ident[:, :])
                mm.then_inc(job.full[0], 1)

        def turn_rows(jobs, key):
            for t in range(T):
                pe.wait_ge(rows_ready, rows_at[key] + t + 1)
                for i, job in enumerate(jobs):
                    if t == 0:
                        wait_empty(pe, job)
                    for c in range(2):
                        mm = pe.transpose(bank[job.bank][:, c * SEQ + t * P:c * SEQ + (t + 1) * P],
                                          rows[:, t, (2 * i + c) * P:(2 * i + c + 1) * P], ident[:, :])
                    if t == T - 1:
                        mm.then_inc(job.full[0], 1)

        def weighted_sum(out, pT, v, first, causal_heads):
            dv = v.shape[2]
            mm = pe.matmul(out[:, 0:dv], pT[:, 0:P], v[:, 0, :], start=first,
                           stop=causal_heads, skip_group_check=True)
            if not causal_heads:
                mm = pe.matmul(out[:, 0:dv], pT[:, SEQ:SEQ + P], v[:, 1, :], start=False, stop=True,
                               skip_group_check=True)
            pe.matmul(out[:, dv:2 * dv], pT[:, P:SEQ], v[:, 0, :], start=False, stop=False,
                      skip_group_check=True)
            late = pT[:, SEQ:SEQ + P] if causal_heads else pT[:, SEQ + P:2 * SEQ]
            return pe.matmul(out[:, dv:2 * dv], late, v[:, 1, :], start=False, stop=True,
                             skip_group_check=True)

        def attention(J, heads, causal_heads):
            n = J["n"]
            for i in range(n + 3):
                if i < n:
                    h, job = heads[i], J["S"][i]
                    out = bank[job.bank]
                    wait_empty(pe, job)
                    if causal_heads:
                        pe.matmul(out[:, :], ident_bf[:, :], causal_bf[:, :, :].rearrange("p t n -> p (t n)"),
                                  start=True, stop=False, skip_group_check=True)
                        pe.matmul(out[:, 0:P], h["q"][:, 0:P], h["k"][:, 0:P], start=False, stop=True,
                                  skip_group_check=True)
                        mm = pe.matmul(out[:, SEQ:2 * SEQ], h["q"][:, P:SEQ], h["k"], start=False,
                                       stop=True, skip_group_check=True)
                    else:
                        for t in range(T):
                            mm = pe.matmul(out[:, t * SEQ:(t + 1) * SEQ], h["q"][:, t * P:(t + 1) * P],
                                           h["k"], start=True, stop=True)
                    mm.then_inc(job.full[0], 1)
                if 2 <= i < n + 2:
                    i2 = i - 2
                    job, p = J["PT"][i2], probs[:, i2 % 3, :]
                    wait_drained(pe, J["S"][i2])
                    wait_empty(pe, job)
                    out = bank[job.bank]
                    pe.transpose(out[:, 0:P], p[:, 0:P], ident[:, :])
                    pe.transpose(out[:, P:SEQ], p[:, SEQ:SEQ + P], ident[:, :])
                    if causal_heads:
                        mm = pe.transpose(out[:, SEQ:SEQ + P], p[:, SEQ + P:2 * SEQ], ident[:, :])
                    else:
                        pe.transpose(out[:, SEQ:SEQ + P], p[:, P:SEQ], ident[:, :])
                        mm = pe.transpose(out[:, SEQ + P:2 * SEQ], p[:, SEQ + P:2 * SEQ], ident[:, :])
                    mm.then_inc(job.full[0], 1)
                if i >= 3:
                    i3 = i - 3
                    g = max(k for k, s in enumerate(J["starts"]) if s <= i3)
                    first = i3 == J["starts"][g]
                    job, v = J["O"][g], heads[i3]["v"]
                    wait_drained(pe, J["PT"][i3])
                    if first:
                        wait_empty(pe, job)
                    c0 = (i3 - J["starts"][g]) * 2 * v.shape[2]
                    weighted_sum(bank[job.bank][:, c0:c0 + 2 * v.shape[2]], probsT[:, i3 % 3, :], v,
                                 first, causal_heads).then_inc(pv_done, 1)

        def swiglu(J, turned_by):
            for pair in range(FC // 2 + 1):
                if pair < FC // 2:
                    project_cols(J["inner"][2 * pair:2 * pair + 2], hT, None if pair else turned_by)
                if not pair:
                    continue
                for j in (2 * pair - 2, 2 * pair - 1):
                    u, w = next_unit()
                    wait_drained(pe, J["inner"][j])
                    tiles = [(c, t) for t in range(T) for c in range(2)] if j == FC - 1 else [
                        (c, t) for c in range(2) for t in range(T)]
                    for c, t in tiles:
                        job = J["acc"][2 * c + t]
                        if j == 0:
                            wait_empty(pe, job)
                        mm = product(bank[job.bank][:, :], [part[:, j % 4, t * P:(t + 1) * P] for part in fS],
                                     [part[:, c * NB:(c + 1) * NB] for part in w], j == 0, j == FC - 1)
                        if j == FC - 1 and (c, t) != (1, 1):
                            mm.then_inc(job.full[0], 1)
                    mm.then_inc(ffn_out_used, 1)

        def layer1(l):
            J = L1[l]
            if l == 0:
                pe.wait_ge(consts_ready, FIRST_CONSTS)
                turn_rows(J["hT"], ("n", l, 0))
                project_cols(J["s"][0:2], hT, J["hT"])
                pe.wait_ge(consts_ready, CONSTS)
                turn_rows(mem1, "mem1")
                project_cols(J["s"][2:3], hT)
                project_cols(J["xk"], memS, memory=l + 1)
            else:
                project_cols(J["xk"][0:1], memS, memory=l + 1)
                turn_rows(J["hT"], ("n", l, 0))
                project_cols(J["xk"][1:2], memS)
                project_cols(J["s"], hT, J["hT"])
            project_rows(J["qk"][0:2], hT, KC, 2, NB)
            project_rows(J["qk"][2:4], hT, KC, 2, NB)
            project_rows(J["qk"][4:6], hT, KC, 4, 256)
            wait_drained(pe, *J["s"])
            for h in range(SB_H):
                job, b, c = J["z"][h], 64 * (h % 2), h // 2
                q, k = sT[b:b + 64, c, :], sT[b:b + 64, 3 + c, :]
                wait_empty(pe, job)
                pe.matmul(bank[job.bank][:, 0:SEQ], k[:, 0:P], q, start=True, stop=True)
                pe.matmul(bank[job.bank][:, SEQ:384], k[:, P:SEQ], q[:, P:SEQ], start=True,
                          stop=True).then_inc(job.full[0], 1)
            project_rows(J["v"][0:2], hT, KC, 2, NB)
            project_rows(J["v"][2:4], hT, KC, 2, NB)
            pe.wait_ge(rope_ready, T * l + 1)
            turn(J["qkT"], lambda c, t: qk_rows[:, t, c * P:(c + 1) * P])
            project_rows(J["gate"][0:2], hT, KC, 2, NB)
            pe.wait_ge(l1m_ready, l + 1)
            for h in range(SB_H):
                job = J["sb"]["btw"][h]
                out = bank[job.bank]
                wait_empty(pe, job)
                pe.matmul(out[:, 0:SEQ], later[:, :], l1m[:, h, 0:SEQ], start=True, stop=False,
                          skip_group_check=True)
                pe.matmul(out[:, P:SEQ], ones[:, :], l1m[:, h, SEQ:384], start=False, stop=True,
                          skip_group_check=True)
                pe.matmul(out[:, SEQ:384], later[:, :], l1m[:, h, SEQ:384], start=False, stop=True,
                          skip_group_check=True).then_inc(job.full[0], 1)
            project_rows(J["gate"][2:4], hT, KC, 2, NB)
            wait_drained(pe, *J["v"])
            for h in range(SB_H):
                job = J["sb"]["O"][h // 4]
                if h % 4 == 0:
                    wait_empty(pe, job)
                pe.wait_ge(w_ready, SB_H * l + h + 1)
                v0 = MOBA_W + DIFF_W + HD * h
                c0 = (h % 4) * 2 * HD
                weighted_sum(bank[job.bank][:, c0:c0 + 2 * HD], zall[:, h, :], v_rows[:, :, v0:v0 + HD],
                             h % 4 == 0, True).then_inc(pv_done, 1)
            wait_drained(pe, *J["qkT"])
            attention(J["att"], diff_heads() + moba_heads(), True)
            turn_rows(J["mT"], ("merged", l))
            project_rows(J["out"][0:2], hT, KC, 2, NB, J["mT"])
            project_rows(J["out"][2:4], hT, KC, 2, NB)
            project_rows(J["xv"], memS, KC, 2, NB)
            turn_rows(J["hT2"], ("n", l, 1))
            project_cols(J["xq"][0:1], hT, J["hT2"])
            if l == DEPTH - 1:
                turn_rows(mem2, "mem2")
            project_cols(J["xq"][1:2], hT)
            wait_drained(pe, *J["xk"])
            wait_drained(pe, *J["xv"])
            wait_drained(pe, *J["xq"])
            attention(J["xatt"], memory_heads(xqT1), False)
            wait_drained(pe, *J["xatt"]["O"])
            turn(J["xoT"], lambda c, t: attn[:, t, c * P:(c + 1) * P])
            project_rows(J["xo"][0:2], hT, 4, 2, NB, J["xoT"])
            project_rows(J["xo"][2:4], hT, 4, 2, NB)

        def layer2(l):
            J = L2[l]
            if l == 0:
                project_cols(J["mk"], memS, memory=DEPTH + l + 1)
            turn_rows(J["hT1"], ("m", l, 0))
            swiglu(J["ffn1"], J["hT1"])
            if l == 0:
                project_rows(J["mv"][0:2], memS, KC, 4, 256)
            project_rows(J["mv"][2:4], memS, KC, 4, 256)
            turn_rows(J["hT"], ("m", l, 2))
            project_rows(J["q"], hT, KC, 2, NB, J["hT"])
            project_rows(J["kv"][0:2], hT, KC, 2, NB)
            project_rows(J["kv"][2:4], hT, KC, 2, KVW - NB)
            wait_drained(pe, *J["kv"])
            for v, job in enumerate(J["crT"]):
                wait_empty(pe, job)
                for g in range(NSA_G):
                    for t in range(T):
                        mm = pe.transpose(bank[job.bank][0:HD, g * SEQ + t * P:g * SEQ + (t + 1) * P],
                                          kv[:, t, v * P + g * HD:v * P + (g + 1) * HD], ident[:, :])
                mm.then_inc(job.full[0], 1)
            project_cols(J["qmem"], hT)
            job = J["cmp"][0]
            wait_empty(pe, job)
            pe.wait_ge(cmpx_ready, l + 1)
            for v in range(2):
                for step in range(4):
                    u, w = next_unit()
                    for mm_ in range(4):
                        m = 4 * step + mm_
                        mm = pe.matmul(bank[job.bank][0:2 * NCMP, v * CMP_HID:(v + 1) * CMP_HID],
                                       cmp_x[:, v, m, :, :].rearrange("p g i -> p (g i)"),
                                       w[:, mm_ * CMP_HID:(mm_ + 1) * CMP_HID], start=(m == 0), stop=(m == 15))
                    mark(mm, u)
            mm.then_inc(job.full[0], 1)
            project_cols(J["conv"][0:1], hT)
            wait_drained(pe, job)
            job = J["cmpT"][0]
            wait_empty(pe, job)
            for a in range(4):
                mm = pe.transpose(bank[job.bank][:, 2 * NCMP * a:2 * NCMP * (a + 1)],
                                  cmp_rows[0:2 * NCMP, a * P:(a + 1) * P], ident[0:2 * NCMP, 0:2 * NCMP])
            mm.then_inc(job.full[0], 1)
            project_cols(J["conv"][1:2], hT)
            pe.wait_ge(cmpg_ready, l + 1)
            wait_empty(pe, J["kvc"][0])
            for half in range(2):
                mm = pe.matmul(bank[J["kvc"][0].bank][0:HD, 0:32], cmp_w2[:, l, 0, half, :],
                               cmp_g[:, half, :], start=(half == 0), stop=(half == 1))
            mm.then_inc(J["kvc"][0].full[0], 1)
            wait_empty(pe, J["kvc"][1])
            for half in range(2):
                mm = pe.matmul(bank[J["kvc"][1].bank][:, 0:HD], cmp_rep[:, half, :],
                               cmp_w2[:, l, 1, half, :], start=(half == 0), stop=(half == 1))
            mm.then_inc(J["kvc"][1].full[0], 1)
            project_cols(J["conv"][2:3], hT)
            pe.wait_ge(rope_ready, T * DEPTH + l + 1)

            def qk_chunk(c, t):
                if c < 8:
                    return (q_rows if c < 4 else qrot)[:, t, (c % 4) * P:(c % 4 + 1) * P]
                slot = 2 if c == 8 else 4
                return kv[:, t, slot * P:(slot + 1) * P]
            turn(J["qkT"], qk_chunk)
            wait_drained(pe, *J["kvc"])
            wait_drained(pe, *J["qkT"][0:2])
            for g, job in enumerate(J["cs"]):
                wait_empty(pe, job)
                for t in range(T):
                    for j in range(HPG):
                        c0 = (t * HPG + j) * NPAD
                        mm = pe.matmul(bank[job.bank][:, c0:c0 + NPAD],
                                       qkT[64 * g:64 * g + 64, j, t * P:(t + 1) * P],
                                       kcT[64 * g:64 * g + 64, :], start=True, stop=True)
                mm.then_inc(job.full[0], 1)
            project_cols(J["conv"][3:5], hT)
            pe.wait_ge(cmpp_ready, l + 1)
            job = J["cpT"][0]
            wait_empty(pe, job)
            for t in range(T):
                mm = pe.transpose(bank[job.bank][:, t * P:(t + 1) * P],
                                  cs[:, t * NSA_H:(t + 1) * NSA_H, :].rearrange("p h n -> p (h n)"), ident[:, :])
            mm.then_inc(job.full[0], 1)
            project_cols(J["conv"][5:6], hT)
            wait_drained(pe, job)
            for t, job in enumerate(J["co"]):
                wait_empty(pe, job)
                pe.matmul(bank[job.bank][:, :], cmp_pT[:, t, :], vbd[:, :, :].rearrange("p h d -> p (h d)"),
                          start=True, stop=True).then_inc(job.full[0], 1)
            wait_drained(pe, *J["qkT"])
            attention(J["att"], nsa_heads(), True)
            wait_drained(pe, *J["mk"])
            wait_drained(pe, *J["mv"])
            wait_drained(pe, *J["qmem"])
            attention(J["matt"], memory_heads(xqT2), False)
            wait_drained(pe, *J["conv"])
            pe.wait_ge(conv_split, l + 1)
            for c in range(2):
                for b in range(3):
                    n = 2 * (3 * c + b)
                    project_rows(J["merge"][n:n + 2], hT, KC, 2, NB)
                    src = fS if b == 0 else [part[:, 4 * b - 4:4 * b, :] for part in memS]
                    project_rows(J["br"][n:n + 2], src, 4, 2, NB,
                                 J["yT"][2 * b - 2:2 * b] if b and not c else None)
                    if n == 0:
                        pe.wait_ge(ysum_done, 4 * (l + 1))
                        wait_drained(pe, *J["matt"]["O"])
                        turn(J["yT"], lambda c, t: attn[:, t, c * P:(c + 1) * P])
            turn_rows(J["mT"], ("mixed", l))
            project_rows(J["out"][0:2], hT, KC, 2, NB, J["mT"])
            project_rows(J["out"][2:4], hT, KC, 2, NB)
            if l + 1 < DEPTH:
                project_cols(L2[l + 1]["mk"], memS, memory=DEPTH + l + 2)
            turn_rows(J["hT2"], ("m", l, 4))
            swiglu(J["ffn2"], J["hT2"])
            if l + 1 < DEPTH:
                project_rows(L2[l + 1]["mv"][0:2], memS, KC, 4, 256)

        for l in range(DEPTH):
            layer1(l)
        for l in range(DEPTH):
            layer2(l)
        assert unit[0] == n_units

    @block.gpsimd
    def _(pool):
        n_const = [0]

        def const(ins):
            n_const[0] += 1
            ins.then_inc(consts_ready, 1)
            pool.wait_ge(consts_ready, n_const[0])

        def select(t, pattern, base, mult, fill, op=ALU.is_ge):
            const(pool.affine_select(out=t, in_=t, pattern=pattern, compare_op=op, fill=fill, base=base,
                                     channel_multiplier=mult))

        def power(n):
            for t in range(T):
                pool.wait_ge(ms_ready, T * n + t + 1)
                pool.tensor_tensor(rstd[:, t:t + 1], ms[:, t:t + 1], half_pow[:, 0:1],
                                   ALU.pow).then_inc(rstd_ready, 1)

        const(pool.memset(half_pow[:, :], -0.5))
        const(pool.memset(ident[:, :], 0.0))
        select(ident[:, :], [[-1, P]], 0, 1, 1.0, ALU.not_equal)
        assert n_const[0] == FIRST_CONSTS
        power(norm1(0, 0))
        const(pool.tensor_copy(ident_bf[:, :], ident[:, :]))
        const(pool.memset(causal_bf[:, :, :], 0.0))
        select(causal_bf[:, :, :], [[P, T], [-1, SEQ]], 0, 1, NEG)
        const(pool.memset(ones[:, :], 1.0))
        const(pool.memset(later[:, :], 1.0))
        select(later[:, :], [[-1, P]], -1, 1, 0.0)
        const(pool.memset(sb_keep[:, :], 1.0))
        select(sb_keep[:, 0:SEQ], [[1, SEQ]], -1, -1, 0.0)
        select(sb_keep[:, SEQ:384], [[1, P]], -1, -1, 0.0)
        const(pool.memset(sb_neg[:, :], 0.0))
        select(sb_neg[:, 0:SEQ], [[1, SEQ]], -1, -1, NEG)
        select(sb_neg[:, SEQ:384], [[1, P]], -1, -1, NEG)
        ends = [[P, T], [0, NSA_H], [-CMP_STRIDE, NPAD]]
        const(pool.memset(cmp_keep[:, :, :], 1.0))
        select(cmp_keep[:, :, :], ends, 1 - CMP_L, 1, 0.0)
        const(pool.tensor_scalar(cmp_neg[:, :, :], cmp_keep[:, :, :], -1.0, -NEG, ALU.add, ALU.mult))
        const(pool.memset(blockdiag[:, :], 0.5))
        select(blockdiag[:, :], [[-NPAD, NSA_H]], 0, 1, 0.0)
        select(blockdiag[:, :], [[NPAD, NSA_H]], NPAD - 1, -1, 0.0)
        assert n_const[0] == CONSTS, n_const[0]

        def rotate(dst, src, heads, width, half, c0):
            def dims(v, a):
                return v.rearrange("p t (h d) -> p t h d", d=width)[:, :, :, a:a + half]
            cos = cost[:, :, c0:c0 + half].unsqueeze(2).broadcast_to([P, T, heads, half])
            sin = sint[:, :, c0:c0 + half].unsqueeze(2).broadcast_to([P, T, heads, half])
            prods = []
            for r, (a, tab) in enumerate(((0, cos), (half, sin), (half, cos), (0, sin))):
                o = rt[r][:, 0:T * heads * half].rearrange("p (t h d) -> p t h d", t=T, h=heads)
                for t in range(T):
                    ins = pool.tensor_tensor(o[:, t], dims(src, a)[:, t], tab[:, t], ALU.mult)
                prods.append(o)
            link(ins)
            for t in range(T):
                pool.tensor_tensor(dims(dst, 0)[:, t], prods[0][:, t], prods[1][:, t], ALU.subtract)
                ins = pool.tensor_tensor(dims(dst, half)[:, t], prods[2][:, t], prods[3][:, t], ALU.add)
            return ins

        steps = [0]

        def link(ins):
            steps[0] += 1
            ins.then_inc(pool_step, 1)
            pool.wait_ge(pool_step, steps[0])

        for l in range(DEPTH):
            J = L1[l]
            power(norm1(l, 0) if l else mem1_norm)
            wait_drained(pool, *J["qk"])
            if l == 0:
                pool.wait_ge(tables_ready, 2)
            link(rotate(qk_rows[:, :, 0:768], qk_rows[:, :, 0:768], 12, HD, 8, 0))
            rotate(qk_rows[:, :, 768:1280], qk_rows[:, :, 768:1280], 16, DIFF_QK, 4, 8).then_inc(rope_ready, T)
            pool.wait_ge(lb_ready, l + 1)
            pool.tensor_tensor(ln1p[:, :, :], ln1p[:, :, :], sb_neg[:, :].unsqueeze(1).broadcast_to([P, SB_H, 384]),
                               ALU.add).then_inc(lbm_ready, 1)
            pool.wait_ge(dsum_ready, l + 1)
            pool.tensor_tensor(dstat2[:, :, :], dstat[:, :, :],
                               half_pow[:, 0:T * DIFF_H].rearrange("p (t h) -> p t h", t=T),
                               ALU.pow).then_inc(dpow_ready, 1)
            if l == DEPTH - 1:
                pool.wait_ge(rows_ready, rows_at["merged", l] + T)
                pool.dma_start(mem2_rows, A["mem2"].rearrange("(t p) n -> p t n", p=P)).then_inc(mem2_loaded, 16)
            power(norm1(l, 1))
        wait_drained(pool, *L1[DEPTH - 1]["mT"])
        pool.dma_start(gain_row, A["post_g"][0]).then_inc(row_loaded, 16)
        power(mem2_norm)
        power(final)

        def post_gain(l, i):
            if (l, i) == (0, 0):
                pool.wait_ge(x_ready, T)
            else:
                pool.wait_ge(x_ready, x_at(l, i))
            pool.dma_start(gain_row, A["post_g"][1 + 3 * l + i]).then_inc(row_loaded, 16)

        for l in range(DEPTH):
            J = L2[l]
            power(norm2(l, 0))
            post_gain(l, 0)
            power(norm2(l, 1))
            power(norm2(l, 2))
            post_gain(l, 1)
            pool.wait_ge(params_loaded, N_SMALL)
            wait_drained(pool, *J["crT"])
            for v in range(2):
                for g in range(NSA_G):
                    for half in range(2):
                        raw = cmp_raw[:, 2 * v + g, :].rearrange("p (i m) -> p m i", m=8)
                        src = raw[:, :, half:half + NCMP]
                        where = cmp_pos[:, l, v, 8 * half:8 * half + 8].unsqueeze(2).broadcast_to([P, 8, NCMP])
                        ins = pool.tensor_tensor(cmp_x[:, v, 8 * half:8 * half + 8, g, :], src, where, ALU.add)
            ins.then_inc(cmpx_ready, 1)
            wait_drained(pool, *J["q"])
            link(pool.tensor_copy(qrot, q_rows))
            link(rotate(qrot, q_rows, NSA_H, HD, 8, 12))
            for slot in (2, 4):
                ins = rotate(kv[:, :, slot * P:(slot + 1) * P], kv[:, :, slot * P:(slot + 1) * P], NSA_G, HD, 8, 12)
                if slot == 2:
                    link(ins)
            ins.then_inc(rope_ready, 1)
            for g in range(4):
                pool.wait_ge(ysum_part, 4 * l + g + 1)
                c0 = (g % 2) * 4 * HD
                y = attn[:, :, c0:c0 + 4 * HD]
                pool.tensor_tensor(y, y, rows[:, :, g * 4 * HD:(g + 1) * 4 * HD], ALU.add).then_inc(ysum_done, 1)
                if g == 1:
                    pool.wait_ge(ysum_done, 4 * l + g + 1)
            power(norm2(l, 3))
            power(norm2(l, 4))
            post_gain(l, 2)
            power(norm2(l, 5))

    @block.scalar
    def _(act):
        steps = [0]

        def link(ins):
            steps[0] += 1
            ins.then_inc(act_step, 1)
            act.wait_ge(act_step, steps[0])

        def drain(job, pieces):
            wait_full(act, job)
            for dst, src, factor in pieces:
                ins = act.activation(dst, src, ACT.Copy, scale=factor)
            ins.then_inc(drained[job.bank], 1)

        next_split = [0]

        def keep_up(last, ahead=2):
            while next_split[0] <= min(last + ahead, n_units - 1):
                u = next_split[0]
                next_split[0] += 1
                if is_raw[u]:
                    continue
                act.wait_ge(loaded[u % RAW], 16 * (u // RAW + 1))
                if split_free(u):
                    act.wait_ge(*split_free(u))
                slot, n = (nth_split[u] - 1) % SPLIT, width_of[u]
                act.activation(w_hi[:, slot, 0:n], raw[:, u % RAW, 0:n], ACT.Copy).then_inc(weights_hi, 1)

        def square_sums(src, wait_rows=None):
            for t in range(T):
                if wait_rows:
                    wait_rows(t)
                act.activation(rows[:, t, :], src[:, t, :], ACT.Square,
                               accum_out=sumsq[:, t:t + 1]).then_inc(sumsq_ready, 1)

        def copied(jobs, dst, factors):
            for i, job in enumerate(jobs):
                if i % 2 == 0:
                    b = bank[job.bank]
                    drain(job, [(dst[:, 2 * i + c, :], b[:, c * SEQ:(c + 1) * SEQ], factors(2 * i + c))
                                for c in range(2)])

        def turned(jobs, dst, factor):
            for i, job in enumerate(jobs):
                wait_full(act, job)
                if isinstance(factor, float):
                    ins = act.activation(dst[0][:, 2 * i:2 * i + 2, :], bank[job.bank][:, :], ACT.Copy, scale=factor)
                else:
                    for c in range(2):
                        ins = act.activation(dst[0][:, 2 * i + c, :], bank[job.bank][:, c * SEQ:(c + 1) * SEQ],
                                             ACT.Copy, scale=factor(2 * i + c))
                ins.then_inc(turn_hi, 1)

        def memory_hi(mem_jobs, which, l, last_read):
            if last_read is not None:
                wait_full(act, last_read)
            for c in range(KC):
                wait_drained(act, mem_jobs[c // 2])
                ins = act.activation(m_hi[:, c, :], memnT[:, c, :], ACT.Copy, scale=gain_cols[:, which, l, c:c + 1])
                if c % 2 == 1:
                    ins.then_inc(mem_hi, 1)

        def gained(which, l):
            return lambda c: gain_cols[:, which, l, c:c + 1]

        def softmax_numerators(J, causal_heads, base):
            for i, job in enumerate(J["S"]):
                act.wait_ge(max_ready, base + i + 1)
                if i >= 3:
                    wait_full(act, J["PT"][i - 3])
                b = bank[job.bank]
                for t in range(T):
                    n = P if causal_heads and t == 0 else SEQ
                    ins = act.activation(probs[:, i % 3, t * SEQ:t * SEQ + n], b[:, t * SEQ:t * SEQ + n],
                                         ACT.Exp, bias=negmax[:, i, t:t + 1],
                                         accum_out=rowsum[:, i, t:t + 1])
                ins.then_inc(drained[job.bank], 1)

        def post_squares(jobs, which):
            for c, t in which:
                job = jobs[2 * c + t]
                wait_full(act, job)
                act.activation(attn[:, t, c * NB:(c + 1) * NB], bank[job.bank][:, :], ACT.Square,
                               accum_out=sumsq4[:, t, c:c + 1]).then_inc(sumsq_ready, 1)

        def tanh_gates(J, base):
            for j in range(FC):
                job = J["inner"][j]
                if j >= 2 and j % 2 == 0:
                    keep_up(J["out_unit"][j - 3] if j > 2 else job.last - 2)
                keep_up(job.last)
                wait_full(act, job)
                if j >= 2:
                    wait_drained(act, J["inner"][j - 2])
                act.activation(ffn_th[:, j % 2, 0:SEQ], bank[job.bank][:, 0:SEQ], ACT.Tanh,
                               scale=0.5).then_inc(ffn_th_ready, 1)
            keep_up(J["out_unit"][-1])

        def layer1(l):
            J = L1[l]
            square_sums(x, lambda t: wait_x1(act, l, 0, t))
            if l == 0:
                keep_up(-1)
                act.wait_ge(gains_loaded, 16)
            else:
                keep_up(J["xk"][0].last)
                drain(J["xk"][0], [(xkT[:, 0:2, :], bank[J["xk"][0].bank][:, :], 1.0)])
            turned(J["hT"], hT, gained(0, l))
            if l == 0:
                keep_up(-1, 3)
                act.wait_ge(mem_loaded, 16)
                wait_full(act, J["hT"][-1])
                square_sums(attn)
            else:
                keep_up(J["xk"][1].last)
                drain(J["xk"][1], [(xkT[:, 2:4, :], bank[J["xk"][1].bank][:, :], 1.0)])
            for u, job in enumerate(J["s"]):
                b = bank[job.bank]
                keep_up(job.last)
                drain(job, [(sT[:, 2 * u + c, :], b[:, c * SEQ:(c + 1) * SEQ],
                             SCALE if 2 * u + c < 3 else 1.0) for c in range(2)])
                if l == 0 and u == 1:
                    keep_up(job.last, 3)
                    copied(mem1, memnT, lambda c: 1.0)
                    memory_hi(mem1, 2, 0, None)
            if l == 0:
                for c, job in enumerate(J["xk"]):
                    keep_up(job.last)
                    drain(job, [(xkT[:, 2 * c:2 * c + 2, :], bank[job.bank][:, :], 1.0)])
            for j in (0, 2, 4):
                n = 256 if j == 4 else NB
                job = J["qk"][j]
                keep_up(job.last)
                drain(job, [(qk_rows[:, 0, (j // 2) * NB:(j // 2) * NB + n], bank[job.bank][:, 0:n], 1.0)])
                if l == 0 and j == 2:
                    act.wait_ge(params_loaded, N_SMALL)
                    act.wait_ge(tables_in, 1)
                    act.activation(sint[:, :, :], ang[:, :, :], ACT.Sin).then_inc(tables_ready, 1)
                    act.activation(cost[:, :, :], ang2[:, :, :], ACT.Sin).then_inc(tables_ready, 1)
            keep_up(J["qk"][5].last, 3)
            for h, job in enumerate(J["z"]):
                drain(job, [(zall[:, h, :], bank[job.bank][:, 0:384], 1.0)])
            wait_drained(act, *J["z"])
            link(act.activation(ln1p[:, :, :], zall[:, :, :], ACT.Abs))
            keep_up(J["qk"][5].last, 4)
            link(act.activation(ln1p[:, :, :], ln1p[:, :, :], ACT.Exp, scale=-1.0))
            if l == 0:
                act.wait_ge(lam_ready, 1)
                act.activation(lam_exp[:, :, :], lam_dot[:, :, :], ACT.Exp).then_inc(lam_ready, 1)
            for j in (0, 2):
                job = J["v"][j]
                keep_up(job.last)
                drain(job, [(v_rows[:, 0, (j // 2) * NB:(j // 2 + 1) * NB], bank[job.bank][:, :], 1.0)])
                if j == 0:
                    act.activation(ln1p[:, :, :], ln1p[:, :, :], ACT.Ln, bias=1.0).then_inc(lnz_ready, 1)
            keep_up(J["v"][3].last, 3)
            copied(J["qkT"], qkT, lambda c: qk_scale[c])
            wait_full(act, J["qkT"][-1])
            for j, job in enumerate(J["gate"]):
                keep_up(job.last)
                wait_full(act, job)
                act.activation(gates[:, j % 2, (j // 2) * NB:(j // 2 + 1) * NB], bank[job.bank][:, :], ACT.Tanh,
                               scale=0.5).then_inc(th_ready, 1)
                if j == 1:
                    keep_up(job.last, 3)
                    for h in range(SB_H):
                        act.wait_ge(arg_ready, SB_H * l + h + 1)
                        act.activation(zall[:, h, :], zall[:, h, :], ACT.Exp).then_inc(w_ready, 1)
            keep_up(J["gate"][3].last)
            softmax_numerators(J["att"], True, 18 * l)
            turned(J["mT"], hT, 1.0)
            keep_up(J["out"][0].last)
            wait_full(act, J["out"][1])
            keep_up(J["out"][2].last)
            wait_full(act, J["out"][3])
            keep_up(J["out"][3].last, 3)
            square_sums(x, lambda t: wait_x1(act, l, 1, t))
            keep_up(J["xv"][0].last)
            drain(J["xv"][0], [(xv[:, 0, :], bank[J["xv"][0].bank][:, :], 1.0)])
            keep_up(J["xv"][0].last, 1)
            turned(J["hT2"], hT, gained(1, l))
            if l + 1 < DEPTH:
                memory_hi(mem1, 2, l + 1, J["xv"][-1])
            if l == DEPTH - 1:
                act.wait_ge(mem2_loaded, 16)
                wait_full(act, J["hT2"][-1])
                square_sums(mem2_rows)
            for u, job in enumerate(J["xq"]):
                keep_up(job.last)
                drain(job, [(xqT1[:, 2 * u:2 * u + 2, :], bank[job.bank][:, :], XD ** -0.5)])
                if l == DEPTH - 1 and u == 0:
                    keep_up(job.last, 3)
                    copied(mem2, memnT, lambda c: 1.0)
            keep_up(J["xq"][1].last)
            softmax_numerators(J["xatt"], False, 18 * l + 14)
            turned(J["xoT"], hT, 1.0)
            keep_up(J["xo"][0].last)
            if l == DEPTH - 1:
                memory_hi(mem2, 5, 0, L1[l]["xv"][-1])
            wait_full(act, J["xo"][1])
            keep_up(J["xo"][2].last)
            wait_full(act, J["xo"][3])
            keep_up(J["xo"][3].last, 3)

        def after_x(l, i):
            return lambda t: act.wait_ge(x_ready, x_at(l, i) - T + t + 1)

        def memory_keys(jobs):
            for c, job in enumerate(jobs):
                keep_up(job.last)
                drain(job, [(xkT[:, 2 * c:2 * c + 2, :], bank[job.bank][:, :], 1.0)])
            keep_up(jobs[1].last, 1)

        def memory_values(jobs, half):
            keep_up(jobs[0].last)
            drain(jobs[0], [(xv[:, 0, half * SEQ:(half + 1) * SEQ], bank[jobs[0].bank][:, 0:SEQ], 1.0)])
            keep_up(jobs[0].last, 1)

        def layer2(l):
            J = L2[l]
            if l == 0:
                wait_full(act, mem2[-1])
            square_sums(x, after_x(l, 0))
            if l == 0:
                memory_keys(J["mk"])
            else:
                memory_values(J["mv"][0:2], 0)
            turned(J["hT1"], hT, gained(3, l))
            tanh_gates(J["ffn1"], 2 * FC * l)
            post_squares(J["ffn1"]["acc"], BY_TILE)
            keep_up(J["ffn1"]["out_unit"][-1], 4)
            square_sums(x, after_x(l, 1))
            if l == 0:
                memory_values(J["mv"][0:2], 0)
            memory_values(J["mv"][2:4], 1)
            turned(J["hT"], hT, gained(4, l))
            keep_up(J["q"][0].last)
            drain(J["q"][0], [(q_rows[:, 0, :], bank[J["q"][0].bank][:, :], 1.0)])
            keep_up(J["kv"][0].last)
            drain(J["kv"][0], [(kv[:, 0, 0:NB], bank[J["kv"][0].bank][:, :], 1.0)])
            keep_up(J["kv"][2].last)
            drain(J["kv"][2], [(kv[:, 0, NB:KVW], bank[J["kv"][2].bank][:, 0:KVW - NB], 1.0)])
            raw_drain(act, J["crT"][0], 0)
            for u, job in enumerate(J["qmem"]):
                keep_up(job.last)
                drain(job, [(xqT2[:, 2 * u:2 * u + 2, :], bank[job.bank][:, :], XD ** -0.5)])
            wait_drained(act, *J["kv"])
            act.activation(nsa_g[:, :, :], kv[:, :, 6 * P:KVW], ACT.Tanh, scale=0.5).then_inc(nsag_ready, 1)
            keep_up(J["conv"][0].last, 1)

            def conv_u(c):
                job = J["conv"][c]
                keep_up(job.last)
                wait_full(act, job)
                if c >= 2:
                    wait_drained(act, J["conv"][c - 2])
                act.activation(utmp[:, c % 2, :], bank[job.bank][:, 0:SEQ], ACT.Copy).then_inc(u_ready, 1)

            job = J["cmp"][0]
            wait_full(act, job)
            act.activation(cmp_rows[0:2 * NCMP, :], bank[job.bank][0:2 * NCMP, :], ACT.Copy).then_inc(
                drained[job.bank], 1)
            conv_u(0)
            job = J["cmpT"][0]
            wait_full(act, job)
            for a in range(4):
                ins = act.activation(cmp_h[:, a, :], bank[job.bank][:, 2 * NCMP * a:2 * NCMP * (a + 1)],
                                     ACT.Identity, bias=cmp_b1[:, l, a // 2, a % 2:a % 2 + 1])
            ins.then_inc(drained[job.bank], 1)
            act.wait_ge(cmpu_ready, l + 1)
            act.activation(cmp_t[:, :, :], cmp_t[:, :, :], ACT.Tanh,
                           scale=math.sqrt(2.0 / math.pi)).then_inc(cmpth_ready, 1)
            conv_u(1)
            job = J["kvc"][0]
            drain(job, [(kcT[64 * g:64 * g + 64, :], bank[job.bank][0:64, NPAD * g:NPAD * g + NPAD], 0.5)
                        for g in range(NSA_G)])
            conv_u(2)
            copied(J["qkT"], qkT, lambda c: qk2_scale[c])
            keep_up(J["conv"][2].last, 4)
            act.wait_ge(cexp_in, l + 1)
            act.activation(cs[:, :, :], cs[:, :, :], ACT.Exp).then_inc(cexp_out, 1)
            conv_u(3)
            keep_up(J["conv"][4].last)
            drain(J["conv"][4], [(bT[:, 0:2 * SEQ], bank[J["conv"][4].bank][:, :], 1.0)])
            drain(J["cpT"][0], [(cmp_pT[:, :, :], bank[J["cpT"][0].bank][:, 0:SEQ], 1.0)])
            keep_up(J["conv"][5].last, 3)
            drain(J["conv"][5], [(bT[:, 2 * SEQ:4 * SEQ], bank[J["conv"][5].bank][:, :], 1.0)])
            softmax_numerators(J["att"], True, 18 * DEPTH + 20 * l)
            softmax_numerators(J["matt"], False, 18 * DEPTH + 20 * l + 16)
            for n in range(6):
                if n == 1:
                    turned(J["yT"], memS, 1.0)
                for t in range(T):
                    job = J["merge"][2 * n + t]
                    keep_up(job.last)
                    wait_full(act, job)
                    if n >= 2:
                        wait_drained(act, J["br"][2 * n - 4 + t])
                    act.activation(merge[:, n % 2, t, :], bank[job.bank][:, :], ACT.Tanh,
                                   scale=0.5).then_inc(drained[job.bank], 1)
                keep_up(J["br"][2 * n].last)
            wait_full(act, J["br"][-1])
            keep_up(J["br"][-1].last, 3)
            turned(J["mT"], hT, 0.5)
            keep_up(J["out"][0].last)
            if l + 1 < DEPTH:
                memory_hi(mem2, 5, l + 1, J["br"][-1])
            keep_up(J["out"][0].last, 3)
            post_squares(J["out"], BY_COLUMNS[0:2])
            keep_up(J["out"][2].last)
            post_squares(J["out"], BY_COLUMNS[2:4])
            keep_up(J["out"][2].last, 4 if l + 1 < DEPTH else 3)
            square_sums(x, after_x(l, 2))
            if l + 1 < DEPTH:
                memory_keys(L2[l + 1]["mk"])
            turned(J["hT2"], hT, gained(6, l))
            tanh_gates(J["ffn2"], 2 * FC * l + FC)
            post_squares(J["ffn2"]["acc"], BY_TILE)
            keep_up(J["ffn2"]["out_unit"][-1], 3)

        for l in range(DEPTH):
            layer1(l)
        square_sums(x, lambda t: wait_x1(act, DEPTH, 0, t))
        keep_up(L1[DEPTH - 1]["xo"][3].last, 4)
        for l in range(DEPTH):
            layer2(l)

    @block.vector
    def _(ve):
        steps = [0]

        def link(ins):
            steps[0] += 1
            ins.then_inc(vec_step, 1)
            ve.wait_ge(vec_step, steps[0])

        def scaled(dst, src, factor):
            if isinstance(factor, float) and factor == 1.0:
                return ve.tensor_copy(dst, src)
            return ve.tensor_scalar(dst, src, factor, None, ALU.mult)

        def drain(job, pieces):
            wait_full(ve, job)
            for dst, src, factor in pieces:
                ins = scaled(dst, src, factor)
            ins.then_inc(drained[job.bank], 1)

        next_split = [0]

        def keep_up(last, ahead=2):
            while next_split[0] <= min(last + ahead, n_units - 1):
                u = next_split[0]
                next_split[0] += 1
                if is_raw[u]:
                    continue
                slot, n = (nth_split[u] - 1) % SPLIT, width_of[u]
                ve.wait_ge(weights_hi, nth_split[u])
                ve.tensor_tensor(w_lo[:, slot, 0:n], raw[:, u % RAW, 0:n], w_hi[:, slot, 0:n].bitcast(F32),
                                 ALU.subtract).then_inc(weights_split, 1)

        def copied(jobs, dst, factors):
            for i, job in enumerate(jobs):
                if i % 2 == 1:
                    b = bank[job.bank]
                    drain(job, [(dst[:, 2 * i + c, :], b[:, c * SEQ:(c + 1) * SEQ], factors(2 * i + c))
                                for c in range(2)])

        def turned(jobs, dst, factor):
            for i, job in enumerate(jobs):
                ve.wait_ge(turn_hi, job.hi)
                if isinstance(factor, float):
                    hi, lo = (part[:, 2 * i:2 * i + 2, :].rearrange("p c n -> p (c n)") for part in dst)
                    ins = ve.scalar_tensor_tensor(out=lo, in0=bank[job.bank][:, :], scalar=factor,
                                                  in1=hi.bitcast(F32), op0=ALU.mult, op1=ALU.subtract)
                else:
                    for c in range(2):
                        ins = ve.scalar_tensor_tensor(
                            out=dst[1][:, 2 * i + c, :], in0=bank[job.bank][:, c * SEQ:(c + 1) * SEQ],
                            scalar=factor(2 * i + c), in1=dst[0][:, 2 * i + c, :].bitcast(F32), op0=ALU.mult,
                            op1=ALU.subtract)
                ins.then_inc(drained[job.bank], 1)

        def memory_lo(n, which, l):
            for c in range(KC):
                ve.wait_ge(mem_hi, (n - 1) * KC // 2 + c // 2 + 1)
                ins = ve.scalar_tensor_tensor(out=m_lo[:, c, :], in0=memnT[:, c, :],
                                              scalar=gain_cols[:, which, l, c:c + 1],
                                              in1=m_hi[:, c, :].bitcast(F32), op0=ALU.mult, op1=ALU.subtract)
                if c % 2 == 1:
                    ins.then_inc(memT_ready, 1)

        def gained(which, l):
            return lambda c: gain_cols[:, which, l, c:c + 1]

        def mean(n, t):
            ve.wait_ge(sumsq_ready, sq[n] - T + t + 1)
            ve.tensor_scalar(ms[:, t:t + 1], sumsq[:, t:t + 1], 1.0 / D, EPS, ALU.mult, ALU.add).then_inc(ms_ready, 1)
            ve.wait_ge(rstd_ready, T * n + t + 1)

        def normalise(n, src):
            for t in range(T):
                mean(n, t)
                ve.tensor_scalar(rows[:, t, :], src[:, t, :], rstd[:, t:t + 1], None,
                                 ALU.mult).then_inc(rows_ready, 1)

        def times_gain(n, jobs, order, a, b):
            for k in range(a, b):
                c, t = order[k]
                job = jobs[2 * c + t]
                ve.wait_ge(sumsq_ready, sq[n] - 2 * T + k + 1)
                ve.tensor_tensor(rows[:, t, c * NB:(c + 1) * NB], bank[job.bank][:, :],
                                 gain_row[:, c * NB:(c + 1) * NB], ALU.mult).then_inc(drained[job.bank], 1)

        def post_norm(n, jobs, factor, order):
            done = 0
            for t, last in enumerate((order.index((1, 0)), order.index((1, 1)))):
                done = max(done, 2 if order is BY_COLUMNS else 0)
                times_gain(n, jobs, order, done, last)
                ve.wait_ge(sumsq_ready, sq[n] - 2 * T + last + 1)
                link(ve.tensor_tensor(ms[:, t:t + 1], sumsq4[:, t, 0:1], sumsq4[:, t, 1:2], ALU.add))
                ve.tensor_scalar(ms[:, t:t + 1], ms[:, t:t + 1], 1.0 / (D * factor * factor),
                                 EPS / (factor * factor), ALU.mult, ALU.add).then_inc(ms_ready, 1)
                times_gain(n, jobs, order, last, last + 1)
                done = last + 1
                ve.wait_ge(rstd_ready, T * n + t + 1)
                wait_drained(ve, jobs[t], jobs[2 + t])
                ve.scalar_tensor_tensor(out=x[:, t, :], in0=rows[:, t, :], scalar=rstd[:, t:t + 1], in1=x[:, t, :],
                                        op0=ALU.mult, op1=ALU.add).then_inc(x_ready, 1)

        def add_to_x(jobs, c=0):
            for j, job in enumerate(jobs):
                xs = x[:, j % 2, (j // 2 + c) * NB:(j // 2 + c + 1) * NB]
                keep_up(job.last)
                wait_full(ve, job)
                ve.tensor_tensor(xs, bank[job.bank][:, :], xs, ALU.add).then_inc(drained[job.bank], 1)

        def attention(J, causal_heads, put, aside=None):
            n = J["n"]
            for i in range(n + 3):
                if i < n:
                    wait_full(ve, J["S"][i])
                    ve.tensor_reduce(negmax[:, i, :], bank[J["S"][i].bank][:, :].rearrange("p (t n) -> p t n", t=T),
                                     AX.X, ALU.max, negate=True).then_inc(max_ready, 1)
                if 2 <= i < n + 2:
                    i2 = i - 2
                    if i2 >= 3:
                        ve.wait_ge(pv_done, J["pv"] + i2 - 2)
                    w = 384 if causal_heads else NB
                    drain(J["PT"][i2], [(probsT[:, i2 % 3, 0:w], bank[J["PT"][i2].bank][:, 0:w], 1.0)])
                if aside is not None:
                    aside(i)
                for g, s0 in enumerate(J["starts"]):
                    s1 = s0 + J["groups"][g]
                    if i - 3 == s1 - 1:
                        wait_full(ve, J["O"][g])
                        link(ve.reciprocal(rinv[:, s0:s1, :], rowsum[:, s0:s1, :]))
                        put(g, s0, s1, J["O"][g])

        def by_head(v, heads, width):
            return v.rearrange("p t (h d) -> p h t d", h=heads)

        def over_dims(v, heads, width):
            return v.unsqueeze(3).broadcast_to([P, heads, T, width])

        def put_plain(c_of):
            def put(g, s0, s1, job):
                n = s1 - s0
                c0, dst, width = c_of(g)
                ve.tensor_tensor(by_head(dst[:, :, c0:c0 + n * width], n, width),
                                 bank[job.bank][:, 0:n * 2 * width].rearrange("p (h t d) -> p h t d", h=n, t=T),
                                 over_dims(rinv[:, s0:s1, :], n, width), ALU.mult).then_inc(drained[job.bank], 1)
            return put

        def difference(l, J, squares):
            if squares:
                link(ve.tensor_reduce(dstat[:, :, :], dsq[:, :, :, :], AX.X, ALU.add))
                ve.tensor_scalar(dstat[:, :, :], dstat[:, :, :], 1.0 / HD, EPS, ALU.mult,
                                 ALU.add).then_inc(dsum_ready, 1)
                return
            wait_drained(ve, *J["att"]["O"][0:2])
            if l == 0:
                lambdas()
            y = attn[:, :, MOBA_W:MOBA_W + DIFF_W]
            for t in range(T):
                pair = rows[:, t, 0:NB].rearrange("p (h c d) -> p h c d", h=DIFF_H, c=2)
                ins = ve.scalar_tensor_tensor(out=y[:, t, :].rearrange("p (h d) -> p h d", h=DIFF_H),
                                              in0=pair[:, :, 1, :], scalar=neg_lam[:, l:l + 1],
                                              in1=pair[:, :, 0, :], op0=ALU.mult, op1=ALU.add)
            link(ins)
            yh = y.rearrange("p t (h d) -> p t h d", h=DIFF_H)
            link(ve.tensor_tensor(dsq[:, :, :, :], yh, yh, ALU.mult))

        def difference_norm(l):
            yh = attn[:, :, MOBA_W:MOBA_W + DIFF_W].rearrange("p t (h d) -> p t h d", h=DIFF_H)
            ve.wait_ge(dpow_ready, l + 1)
            link(ve.tensor_tensor(dsq[:, :, :, :], yh, dstat2[:, :, :].unsqueeze(3).broadcast_to([P, T, DIFF_H, HD]),
                                  ALU.mult))
            for t in range(T):
                ins = ve.tensor_tensor(yh[:, t], dsq[:, t], head_g[:, l, :].unsqueeze(1).broadcast_to([P, DIFF_H, HD]),
                                       ALU.mult)
            link(ins)

        def lambdas():
            ve.wait_ge(lam_ready, 2)
            link(ve.tensor_tensor(neg_lam[:, :], lam_exp[:, :, 1], lam_exp[:, :, 0], ALU.subtract))
            link(ve.tensor_tensor(neg_lam[:, :], neg_lam[:, :], lam_const[:, :, 0], ALU.subtract))
            for k in range(DEPTH):
                ins = ve.tensor_scalar(head_g[:, k, :], head_g[:, k, :], lam_const[:, k, 1:2], None, ALU.mult)
            link(ins)

        def tables():
            ve.wait_ge(params_loaded, N_SMALL)
            link(ve.tensor_copy(pos_f[:, :, :], pos_i[:, :, :]))
            for w, (a, b) in ((0, (0, 12)), (1, (12, 20))):
                for t in range(T):
                    ins = ve.tensor_scalar(ang[:, t, a:b], inv_freq[:, a:b], pos_f[:, w, t:t + 1], None, ALU.mult)
            link(ins)
            link(ve.tensor_scalar(turns[:, :, :], ang[:, :, :], 1.0 / (2 * math.pi), None, ALU.mult))
            link(ve.tensor_copy(turns_i[:, :, :], turns[:, :, :]))
            link(ve.tensor_copy(turns[:, :, :], turns_i[:, :, :]))
            for part_of_2pi in TWO_PI:
                link(ve.scalar_tensor_tensor(out=ang[:, :, :], in0=turns[:, :, :], scalar=-part_of_2pi,
                                             in1=ang[:, :, :], op0=ALU.mult, op1=ALU.add))
            link(ve.tensor_scalar(ang2[:, :, :], ang[:, :, :], math.pi / 2, None, ALU.add))
            link(ve.tensor_scalar(wrap[:, :, :], ang2[:, :, :], math.pi, -2 * math.pi, ALU.is_gt, ALU.mult))
            link(ve.tensor_tensor(ang2[:, :, :], ang2[:, :, :], wrap[:, :, :], ALU.add))
            link(ve.tensor_scalar(ang[:, :, :], ang[:, :, :], PI_F, -PI_F, ALU.min, ALU.max))
            ve.tensor_scalar(ang2[:, :, :], ang2[:, :, :], PI_F, -PI_F, ALU.min, ALU.max).then_inc(tables_in, 1)
            link(ve.tensor_tensor(lam_prod[:, :, :, :], lam_in[:, :, 0:4:2, :], lam_in[:, :, 1:4:2, :], ALU.mult))
            ve.tensor_reduce(lam_dot[:, :, :], lam_prod[:, :, :, :], AX.X, ALU.add).then_inc(lam_ready, 1)

        def hidden(J, base):
            for j in range(FC):
                job = J["inner"][j]
                if j >= 2 and j % 2 == 0:
                    keep_up(J["out_unit"][j - 3] if j > 2 else job.last - 2)
                keep_up(job.last)
                ve.wait_ge(ffn_th_ready, base + j + 1)
                if j >= 4:
                    ve.wait_ge(ffn_out_used, J["base"] + j - 3)
                b = bank[job.bank]
                th, h = ffn_th[:, j % 2, 0:SEQ], hid[:, j % 2, 0:SEQ]
                link(ve.scalar_tensor_tensor(out=h, in0=th, scalar=1.0, in1=b[:, 0:SEQ], op0=ALU.add,
                                             op1=ALU.mult))
                link(ve.scalar_tensor_tensor(out=h, in0=h, scalar=0.5, in1=b[:, SEQ:2 * SEQ],
                                             op0=ALU.mult, op1=ALU.mult))
                link(ve.tensor_copy(f_hi[:, j % 4, :], h))
                ve.tensor_tensor(f_lo[:, j % 4, :], h, f_hi[:, j % 4, :].bitcast(F32),
                                 ALU.subtract).then_inc(drained[job.bank], 1)
            keep_up(J["out_unit"][-1])

        def layer1(l):
            J = L1[l]
            normalise(norm1(l, 0), x)
            if l == 0:
                keep_up(-1)
                ve.wait_ge(gains_loaded, 16)
            else:
                keep_up(J["xk"][0].last)
            turned(J["hT"], hT, gained(0, l))
            if l == 0:
                keep_up(-1, 3)
                normalise(mem1_norm, attn)
            else:
                keep_up(J["xk"][1].last)
            for u, job in enumerate(J["s"]):
                keep_up(job.last)
                if l == 0 and u == 1:
                    keep_up(job.last, 3)
                    copied(mem1, memnT, lambda c: 1.0)
                    memory_lo(1, 2, 0)
            if l == 0:
                for job in J["xk"]:
                    keep_up(job.last)
            for j in (1, 3, 5):
                n = 256 if j == 5 else NB
                job = J["qk"][j]
                keep_up(job.last)
                drain(job, [(qk_rows[:, 1, (j // 2) * NB:(j // 2) * NB + n], bank[job.bank][:, 0:n], 1.0)])
                if l == 0 and j == 1:
                    tables()
            keep_up(J["qk"][5].last, 3)
            keep_up(J["qk"][5].last, 4)
            keep_up(J["v"][1].last)
            drain(J["v"][1], [(v_rows[:, 1, 0:NB], bank[J["v"][1].bank][:, :], 1.0)])
            keep_up(J["v"][1].last, 3)
            ve.wait_ge(lnz_ready, l + 1)
            link(ve.scalar_tensor_tensor(out=ln1p[:, :, :], in0=zall[:, :, :], scalar=0.0, in1=ln1p[:, :, :],
                                         op0=ALU.min, op1=ALU.subtract))
            keep_up(J["v"][3].last)
            ve.tensor_tensor(l1m[:, :, :], ln1p[:, :, :], zall[:, :, :], ALU.subtract).then_inc(lb_ready, 1)
            drain(J["v"][3], [(v_rows[:, 1, NB:2 * NB], bank[J["v"][3].bank][:, :], 1.0)])
            keep_up(J["v"][3].last, 3)
            copied(J["qkT"], qkT, lambda c: qk_scale[c])
            ve.wait_ge(lb_ready, l + 1)
            ve.tensor_tensor(l1m[:, :, :], l1m[:, :, :], sb_keep[:, :].unsqueeze(1).broadcast_to([P, SB_H, 384]),
                             ALU.mult).then_inc(l1m_ready, 1)
            for j, job in enumerate(J["gate"]):
                g = gates[:, j % 2, (j // 2) * NB:(j // 2 + 1) * NB]
                keep_up(job.last)
                ve.wait_ge(th_ready, 4 * l + j + 1)
                ve.scalar_tensor_tensor(out=g, in0=g, scalar=1.0, in1=bank[job.bank][:, :], op0=ALU.add,
                                        op1=ALU.mult).then_inc(drained[job.bank], 1)
                if j == 1:
                    keep_up(job.last, 3)
                    ve.wait_ge(lbm_ready, l + 1)
                    for h, btw in enumerate(J["sb"]["btw"]):
                        wait_full(ve, btw)
                        ve.tensor_tensor(zall[:, h, :], bank[btw.bank][:, 0:384], ln1p[:, h, :],
                                         ALU.add).then_inc(drained[btw.bank], 1)
                        wait_drained(ve, btw)
                        ve.engine_nop().then_inc(arg_ready, 1)
            keep_up(J["gate"][3].last)
            for g, (s0, n) in enumerate(((0, 4), (4, 2))):
                job = J["sb"]["O"][g]
                c0 = MOBA_W + DIFF_W + HD * s0
                drain(job, [(by_head(attn[:, :, c0:c0 + n * HD], n, HD),
                             bank[job.bank][:, 0:n * 2 * HD].rearrange("p (h t d) -> p h t d", h=n, t=T), 1.0)])
            plain = put_plain(lambda g: [(0, rows, HD), (4 * HD, rows, HD), (0, attn, HD), (4 * HD, attn, HD)][g])

            def difference_step(i):
                if i in (11, 12):
                    difference(l, J, i == 12)
                elif i == 13:
                    difference_norm(l)
                elif i >= 15:
                    t = i - 15
                    if t == 0:
                        wait_drained(ve, *J["gate"], *J["sb"]["O"])
                    ve.scalar_tensor_tensor(out=rows[:, t, MOBA_W:D], in0=attn[:, t, MOBA_W:D], scalar=0.5,
                                            in1=gates[:, t, MOBA_W:D], op0=ALU.mult, op1=ALU.mult)

            attention(J["att"], True, plain, difference_step)
            wait_drained(ve, *J["att"]["O"][2:4])
            for t in range(T):
                ve.scalar_tensor_tensor(out=rows[:, t, 0:MOBA_W], in0=attn[:, t, 0:MOBA_W], scalar=0.5,
                                        in1=gates[:, t, 0:MOBA_W], op0=ALU.mult, op1=ALU.mult).then_inc(rows_ready, 1)
            turned(J["mT"], hT, 1.0)
            add_to_x(J["out"])
            keep_up(J["out"][3].last, 3)
            normalise(norm1(l, 1), x)
            keep_up(J["xv"][1].last)
            drain(J["xv"][1], [(xv[:, 1, :], bank[J["xv"][1].bank][:, :], 1.0)])
            keep_up(J["xv"][1].last, 1)
            turned(J["hT2"], hT, gained(1, l))
            if l + 1 < DEPTH:
                memory_lo(l + 2, 2, l + 1)
            if l == DEPTH - 1:
                normalise(mem2_norm, mem2_rows)
            keep_up(J["xq"][0].last, 3)
            if l == DEPTH - 1:
                copied(mem2, memnT, lambda c: 1.0)
            keep_up(J["xq"][1].last)
            attention(J["xatt"], False, put_plain(lambda g: (2 * XD * g, attn, XD)))
            turned(J["xoT"], hT, 1.0)
            add_to_x(J["xo"][0:2])
            if l == DEPTH - 1:
                memory_lo(DEPTH + 1, 5, 0)
            add_to_x(J["xo"][2:4], 1)
            keep_up(J["xo"][3].last, 3)

        def memory_values(jobs, half):
            keep_up(jobs[1].last)
            drain(jobs[1], [(xv[:, 1, half * SEQ:(half + 1) * SEQ], bank[jobs[1].bank][:, 0:SEQ], 1.0)])
            keep_up(jobs[1].last, 1)

        def layer2(l):
            J = L2[l]
            normalise(norm2(l, 0), x)
            if l == 0:
                keep_up(J["mk"][0].last)
                keep_up(J["mk"][1].last, 1)
            else:
                memory_values(J["mv"][0:2], 0)
            turned(J["hT1"], hT, gained(3, l))
            hidden(J["ffn1"], 2 * FC * l)
            ve.wait_ge(row_loaded, 16 * (3 * l + 2))
            post_norm(norm2(l, 1), J["ffn1"]["acc"], 0.5, BY_TILE)
            keep_up(J["ffn1"]["out_unit"][-1], 4)
            normalise(norm2(l, 2), x)
            if l == 0:
                memory_values(J["mv"][0:2], 0)
            memory_values(J["mv"][2:4], 1)
            turned(J["hT"], hT, gained(4, l))
            keep_up(J["q"][1].last)
            drain(J["q"][1], [(q_rows[:, 1, :], bank[J["q"][1].bank][:, :], 1.0)])
            keep_up(J["kv"][1].last)
            drain(J["kv"][1], [(kv[:, 1, 0:NB], bank[J["kv"][1].bank][:, :], 1.0)])
            keep_up(J["kv"][3].last)
            drain(J["kv"][3], [(kv[:, 1, NB:KVW], bank[J["kv"][3].bank][:, 0:KVW - NB], 1.0)])
            raw_drain(ve, J["crT"][1], 1)
            for job in J["qmem"]:
                keep_up(job.last)
            link(ve.memset(convT[:, :, 0:2], 0.0))
            keep_up(J["conv"][0].last, 1)

            def conv_product(c):
                job = J["conv"][c]
                keep_up(job.last)
                ve.wait_ge(u_ready, 4 * l + c + 1)
                ve.tensor_tensor(convT[:, c, 2:SEQ + 2], bank[job.bank][:, SEQ:2 * SEQ], utmp[:, c % 2, :],
                                 ALU.mult).then_inc(drained[job.bank], 1)

            conv_product(0)
            wait_drained(ve, *J["cmpT"])
            link(ve.tensor_tensor(cmp_t[:, :, :], cmp_h[:, :, :], cmp_h[:, :, :], ALU.mult))
            link(ve.tensor_scalar(cmp_t[:, :, :], cmp_t[:, :, :], 0.044715, 1.0, ALU.mult, ALU.add))
            ve.tensor_tensor(cmp_t[:, :, :], cmp_t[:, :, :], cmp_h[:, :, :], ALU.mult).then_inc(cmpu_ready, 1)
            ve.wait_ge(cmpth_ready, l + 1)
            if l == 0:
                link(ve.memset(cmp_g[:, :, :], 0.0))
            link(ve.scalar_tensor_tensor(
                out=cmp_g[:, :, :].rearrange("p a (g i) -> p (a g) i", g=NSA_G)[:, :, 0:NCMP],
                in0=cmp_t[:, :, :].rearrange("p a (g i) -> p (a g) i", g=NSA_G), scalar=1.0,
                in1=cmp_h[:, :, :].rearrange("p a (g i) -> p (a g) i", g=NSA_G), op0=ALU.add, op1=ALU.mult))
            for half in range(2):
                ins = ve.tensor_copy(
                    cmp_rep[:, half, :].rearrange("p (g j n) -> p g j n", g=NSA_G, j=HPG),
                    cmp_g[:, 2 + half, :].rearrange("p (g n) -> p g n", g=NSA_G).unsqueeze(2).broadcast_to(
                        [P, NSA_G, HPG, NPAD]))
            ins.then_inc(cmpg_ready, 1)
            conv_product(1)
            job = J["kvc"][1]
            wait_full(ve, job)
            ve.tensor_tensor(vbd[:, :, :], bank[job.bank][:, 0:HD].unsqueeze(1).broadcast_to([P, NSA_H, HD]),
                             blockdiag[:, :].unsqueeze(2).broadcast_to([P, NSA_H, HD]),
                             ALU.mult).then_inc(drained[job.bank], 1)
            ve.wait_ge(nsag_ready, l + 1)
            link(ve.tensor_scalar(nsa_g[:, :, :], nsa_g[:, :, :], 1.0, 0.5, ALU.add, ALU.mult))
            conv_product(2)
            copied(J["qkT"], qkT, lambda c: qk2_scale[c])
            keep_up(J["conv"][2].last, 4)
            for g, job in enumerate(J["cs"]):
                wait_full(ve, job)
                heads = cs[:, :, :].rearrange("p (t h) n -> p t (h n)", t=T)[:, :, g * HPG * NPAD:(g + 1) * HPG * NPAD]
                neg = cmp_neg[:, :, :].rearrange("p (t h) n -> p t (h n)", t=T)[:, :, g * HPG * NPAD:(g + 1) * HPG * NPAD]
                ve.tensor_tensor(heads, bank[job.bank][:, 0:T * HPG * NPAD].rearrange("p (t n) -> p t n", t=T), neg,
                                 ALU.add).then_inc(drained[job.bank], 1)
            wait_drained(ve, *J["cs"])
            link(ve.tensor_reduce(cstat[:, 0, :], cs[:, :, :], AX.X, ALU.max))
            ve.tensor_tensor(cs[:, :, :], cs[:, :, :], cstat[:, 0, :].unsqueeze(2).broadcast_to([P, 16, NPAD]),
                             ALU.subtract).then_inc(cexp_in, 1)
            ve.wait_ge(cexp_out, l + 1)
            link(ve.tensor_tensor(cs[:, :, :], cs[:, :, :], cmp_keep[:, :, :], ALU.mult))
            link(ve.tensor_reduce(cstat[:, 1, :], cs[:, :, :], AX.X, ALU.add))
            link(ve.tensor_scalar(cstat[:, 1, :], cstat[:, 1, :], 1e-30, None, ALU.max))
            link(ve.reciprocal(cstat[:, 2, :], cstat[:, 1, :]))
            ve.tensor_tensor(cs[:, :, :], cs[:, :, :], cstat[:, 2, :].unsqueeze(2).broadcast_to([P, 16, NPAD]),
                             ALU.mult).then_inc(cmpp_ready, 1)
            conv_product(3)
            keep_up(J["conv"][4].last)
            keep_up(J["conv"][5].last, 3)

            def conv_step(i):
                if i == 0:
                    wait_drained(ve, *J["conv"])
                if i < 12:
                    w, c = divmod(i, 4)
                    src, f = convT[:, c, w:w + SEQ], conv_w[:, l, w, c:c + 1]
                    if w == 0:
                        link(ve.tensor_scalar(yconvT[:, c, :], src, f, None, ALU.mult))
                    else:
                        link(ve.scalar_tensor_tensor(out=yconvT[:, c, :], in0=src, scalar=f, in1=yconvT[:, c, :],
                                                     op0=ALU.mult, op1=ALU.add))
                elif i < 14:
                    y = yconvT[:, 2 * (i - 12):2 * (i - 12) + 2, :].rearrange("p c n -> p (c n)")
                    link(ve.tensor_tensor(y, bT[:, 2 * SEQ * (i - 12):2 * SEQ * (i - 11)], y, ALU.mult))
                elif i == 15:
                    link(ve.tensor_copy(f_hi[:, :, :], yconvT[:, :, :]))
                elif i == 17:
                    ve.tensor_tensor(f_lo[:, :, :], yconvT[:, :, :], f_hi[:, :, :].bitcast(F32),
                                     ALU.subtract).then_inc(conv_split, 1)

            def gate_of(b):
                return nsa_g[:, :, :].rearrange("p t (h b) -> p t h b", b=3)[:, :, :, b]

            for t, job in enumerate(J["co"]):
                wait_full(ve, job)
                ve.tensor_tensor(attn[:, t, 0:NSA_W].rearrange("p (h d) -> p h d", h=NSA_H),
                                 bank[job.bank][:, :].rearrange("p (h d) -> p h d", h=NSA_H),
                                 gate_of(0)[:, t].unsqueeze(2).broadcast_to([P, NSA_H, HD]),
                                 ALU.mult).then_inc(drained[job.bank], 1)
            wait_drained(ve, *J["co"])

            def put_nsa(g, s0, s1, job):
                b, h0 = 1 + g // 2, 4 * (g % 2)
                link(ve.tensor_tensor(gsc[:, s0:s1, :], rinv[:, s0:s1, :],
                                      gate_of(b)[:, :, h0:h0 + 4].rearrange("p t h -> p h t"), ALU.mult))
                ve.tensor_tensor(by_head(rows[:, :, g * 4 * HD:(g + 1) * 4 * HD], 4, HD),
                                 bank[job.bank][:, :].rearrange("p (h t d) -> p h t d", h=4, t=T),
                                 over_dims(gsc[:, s0:s1, :], 4, HD), ALU.mult).then_inc(drained[job.bank], 1)
                wait_drained(ve, job)
                ve.engine_nop().then_inc(ysum_part, 1)

            attention(J["att"], True, put_nsa, conv_step)
            attention(J["matt"], False, put_plain(lambda g: (NSA_W + 2 * XD * g, attn, XD)))
            ve.wait_ge(ysum_done, 4 * (l + 1))
            for c in range(2):
                for b in range(3):
                    n = 3 * c + b
                    keep_up(J["merge"][2 * n].last)
                    for t in range(T):
                        job = J["br"][2 * n + t]
                        keep_up(job.last)
                        wait_drained(ve, J["merge"][2 * n + t])
                        wait_full(ve, job)
                        cols = slice(c * NB, (c + 1) * NB)
                        dst = rows[:, t, cols] if b == 0 else attn[:, t, 0:NB]
                        ve.scalar_tensor_tensor(out=dst, in0=merge[:, n % 2, t, :], scalar=1.0,
                                                in1=bank[job.bank][:, :], op0=ALU.add,
                                                op1=ALU.mult).then_inc(drained[job.bank], 1)
                        if b:
                            wait_drained(ve, job)
                            ins = ve.tensor_tensor(rows[:, t, cols], rows[:, t, cols], dst, ALU.add)
                            if n == 5:
                                ins.then_inc(rows_ready, 1)
                            else:
                                link(ins)
                    if n == 0:
                        turned(J["yT"], memS, 1.0)
            keep_up(J["br"][-1].last, 3)
            turned(J["mT"], hT, 0.5)
            keep_up(J["out"][0].last)
            if l + 1 < DEPTH:
                memory_lo(DEPTH + l + 2, 5, l + 1)
            keep_up(J["out"][0].last, 3)
            ve.wait_ge(row_loaded, 16 * (3 * l + 3))
            times_gain(norm2(l, 3), J["out"], BY_COLUMNS, 0, 2)
            keep_up(J["out"][2].last)
            post_norm(norm2(l, 3), J["out"], 1.0, BY_COLUMNS)
            if l + 1 < DEPTH:
                keep_up(J["out"][2].last, 4)
            normalise(norm2(l, 4), x)
            if l + 1 < DEPTH:
                keep_up(L2[l + 1]["mk"][1].last, 1)
            else:
                keep_up(J["out"][2].last, 3)
            turned(J["hT2"], hT, gained(6, l))
            hidden(J["ffn2"], 2 * FC * l + FC)
            ve.wait_ge(row_loaded, 16 * (3 * l + 4))
            post_norm(norm2(l, 5), J["ffn2"]["acc"], 0.5, BY_TILE)
            keep_up(J["ffn2"]["out_unit"][-1], 3)

        for l in range(DEPTH):
            layer1(l)
        ve.wait_ge(row_loaded, 16)
        for t in range(T):
            mean(final, t)
            ve.scalar_tensor_tensor(out=x[:, t, :], in0=x[:, t, :], scalar=rstd[:, t:t + 1], in1=gain_row,
                                    op0=ALU.mult, op1=ALU.mult).then_inc(x_ready, 1)
        keep_up(L1[DEPTH - 1]["xo"][3].last, 4)
        for l in range(DEPTH):
            layer2(l)


def weight_columns(W):
    def cols(*spans):
        return np.concatenate([np.arange(a, b) for a, b in spans])

    m = MOBA_W
    at = np.cumsum([0, m, m, m, m, DIFF_W, DIFF_W, DIFF_W, DIFF_W, SB_W, SB_W, SB_W, SB_W])
    piece = lambda i: (at[i], at[i + 1])
    mix = np.cumsum((0,) + MIX)
    heads = np.concatenate([np.arange(HD) + HD * h for j in range(HPG) for h in (j, j + HPG)])
    pairs = np.concatenate([np.arange(P) + P * (j + side) for j in range(FC) for side in (0, FC)])
    table = {
        "w_xkv_k": (W["w_xkv"], cols((0, XW))), "w_xkv_v": (W["w_xkv"], cols((XW, 2 * XW))),
        "w_s": (W["w_in"], cols(piece(8), piece(9))),
        "w_qk": (W["w_in"], cols(piece(0), piece(1), piece(4), piece(5))),
        "w_v": (W["w_in"], cols(piece(2), piece(6), piece(10))),
        "w_gate": (W["w_in"], cols(piece(3), piece(7), piece(11))),
        "w_out": (W["w_out"], cols((0, D))), "w_xq": (W["w_xq"], cols((0, XW))),
        "w_xo": (W["w_xo"], cols((0, D))),
        "ffn1_in": (W["ffn1_w_in_2"], pairs), "ffn1_out": (W["ffn1_w_out_2"], cols((0, D))),
        "ffn2_in": (W["ffn2_w_in_2"], pairs), "ffn2_out": (W["ffn2_w_out_2"], cols((0, D))),
        "w_mkv_k": (W["w_mem_kv_2"], cols((0, XW))), "w_mkv_v": (W["w_mem_kv_2"], cols((XW, 2 * XW))),
        "w_q": (W["w_mix_in_2"], mix[3] + heads),
        "w_kv": (W["w_mix_in_2"], cols((mix[4], mix[6]))),
        "w_qmem": (W["w_mix_in_2"], cols((mix[6], mix[7]))),
        "w_conv": (W["w_mix_in_2"], np.concatenate(
            [cols((P * c, P * c + P), (mix[2] + P * c, mix[2] + P * c + P)) for c in range(4)]
            + [cols((mix[1], mix[2]))])),
        "w_merge": (W["w_mix_in_2"], cols((mix[7], mix[8]))),
        "cmp_k_w1": (W["cmp_k_w1_2"], cols((0, CMP_HID))), "cmp_v_w1": (W["cmp_v_w1_2"], cols((0, CMP_HID))),
        "w_br0": (W["w_branch_conv_2"], cols((0, D))), "w_br1": (W["w_branch_nsa_2"], cols((0, D))),
        "w_br2": (W["w_branch_mem_2"], cols((0, D))), "w_mix_out": (W["w_mix_out_2"], cols((0, D))),
    }
    return table


def weight_stream(W):
    table = weight_columns(W)
    plan = all_units()
    stream = np.zeros((len(plan), P, UNIT), np.float32)
    ordered = {}
    for n, (l, (name, k0, nk, c0, width)) in enumerate(plan):
        w, order = table[name]
        if (name, l) not in ordered:
            ordered[name, l] = np.asarray(w[l])[:, order]
        block = ordered[name, l][k0 * P:(k0 + nk) * P, c0:c0 + width]
        stream[n, :, :nk * width] = block.reshape(nk, P, width).transpose(1, 0, 2).reshape(P, nk * width)
    return stream


def kernel(**inputs):
    import concourse.bacc as bacc
    from concourse.bass_utils import run_bass_kernel_spmd

    W = {k: np.asarray(v) for k, v in inputs.items()}

    def spread(a):
        return np.ascontiguousarray(np.broadcast_to(a, (P,) + a.shape))

    def on_partitions(a):
        return np.ascontiguousarray(np.moveaxis(a.reshape(a.shape[:-1] + (-1, P)), -1, 0))

    lam_init = [0.8 - 0.6 * math.exp(-0.3 * l) for l in range(DEPTH)]
    rot64 = np.arange(0, 16, 2, dtype=np.float32) / np.float32(16)
    rot32 = np.arange(0, 8, 2, dtype=np.float32) / np.float32(8)
    theta = np.float32(THETA)
    inv = np.concatenate([np.float32(1) / theta ** rot64, np.float32(1) / theta ** rot32,
                          theta ** -rot64]).astype(np.float32)
    posts = [W["final_norm_g"]]
    for l in range(DEPTH):
        posts += [W["ffn1_norm_post_2"][l], W["mix_norm_post_2"][l], W["ffn2_norm_post_2"][l]]
    arrays = {
        "x": W["x"][0], "mem": W["mem"][0], "mem2": W["mem_2"][0], "stream": weight_stream(W),
        "gain_cols": on_partitions(np.stack([W[n] for n in (
            "attn_norm_g", "xattn_norm_g", "mem_norm_g", "ffn1_norm_pre_2", "mix_norm_pre_2", "mem_norm_2",
            "ffn2_norm_pre_2")])),
        "post_g": np.stack([spread(p) for p in posts]),
        "head_g": spread(W["diff_head_norm_g"]),
        "lam": spread(np.stack([W["diff_lambda_" + n] for n in ("q1", "k1", "q2", "k2")], axis=1)),
        "lam_const": spread(np.array([[v, 1.0 - v] for v in lam_init], np.float32)),
        "conv_w": on_partitions(W["conv_w_2"]),
        "cmp_b1": on_partitions(np.stack([W["cmp_k_b1_2"], W["cmp_v_b1_2"]], axis=1)),
        "cmp_pos": np.ascontiguousarray(np.stack([W["cmp_pos_k_2"], W["cmp_pos_v_2"]], axis=1).reshape(
            DEPTH, 2, 16, P).transpose(3, 0, 1, 2)),
        "cmp_w2": np.ascontiguousarray(np.stack([W["cmp_k_w2_2"], W["cmp_v_w2_2"]], axis=1).reshape(
            DEPTH, 2, 2, P, HD).transpose(3, 0, 1, 2, 4)),
        "inv_freq": spread(inv),
        "positions": np.ascontiguousarray(np.stack([W["positions"][0], W["positions_2"][0]]).reshape(
            2, T, P).transpose(2, 0, 1)),
    }
    arrays = {k: np.ascontiguousarray(v) for k, v in arrays.items()}
    nc = bacc.Bacc("TRN2", target_bir_lowering=False, num_devices=1)
    arrays = {"in_" + k: v for k, v in arrays.items()}
    args = {k[3:]: nc.dram_tensor(k, v.shape, mybir.dt.from_np(v.dtype), kind="ExternalInput").ap()
            for k, v in arrays.items()}
    args["out"] = nc.dram_tensor("out", (SEQ, D), F32, kind="ExternalOutput").ap()
    build(nc, args)
    r = run_bass_kernel_spmd(nc, [arrays], core_ids=[0])
    return r.results[0]["out"].reshape(1, SEQ, D)
```
